# Optimizing a Trainium2 kernel written in Bass

```python
import jax, jax.numpy as jnp
from jax import lax
import numpy as np

D_MODEL = 1024
BATCH = 1
SEQ = 256
DEPTH = 2

N_MIXERS = 2
N_ATTN_LAYERS = (DEPTH + 1) // 2
N_CONV_LAYERS = DEPTH // 2
N_HEADS = 8
QK_NOPE_DIM = 128
QK_ROPE_DIM = 64
QK_HEAD_DIM = QK_NOPE_DIM + QK_ROPE_DIM
V_HEAD_DIM = 128
Q_LORA_RANK = 768
KV_LORA_RANK = 256
ROPE_THETA = 10000.0
Q_BLOCK = 128
CONV_WIDTH = 31
CONV_DIM = D_MODEL
N_EXPERTS = 16
N_GROUPS = 4
EXPERTS_PER_GROUP = N_EXPERTS // N_GROUPS
TOP_K = 2
EXPERT_FF = 512
NORM_EPS = 1e-6

kernel_name = 'hybrid_mla_conformer_grouped_moe'

def rms_norm(x, g):
    xf = x.astype(jnp.float32)
    y = xf * lax.rsqrt(jnp.mean(xf * xf, axis=-1, keepdims=True) + NORM_EPS)
    return y.astype(x.dtype) * g

def layer_norm(x, g, b):
    xf = x.astype(jnp.float32)
    mu = jnp.mean(xf, axis=-1, keepdims=True)
    var = jnp.mean(jnp.square(xf - mu), axis=-1, keepdims=True)
    y = (xf - mu) * lax.rsqrt(var + NORM_EPS)
    return y.astype(x.dtype) * g + b

def rope(x, positions):
    half = QK_ROPE_DIM // 2
    inv_freq = 1.0 / (ROPE_THETA ** (jnp.arange(half, dtype=jnp.float32) * (2.0 / QK_ROPE_DIM)))
    ang = positions.astype(jnp.float32)[..., None] * inv_freq
    cos = jnp.cos(ang)[:, :, None, :]
    sin = jnp.sin(ang)[:, :, None, :]
    x1 = x[..., :half].astype(jnp.float32)
    x2 = x[..., half:].astype(jnp.float32)
    out = jnp.concatenate([x1 * cos - x2 * sin, x2 * cos + x1 * sin], axis=-1)
    return out.astype(x.dtype)

def causal_block_attention(q, k, v):
    b, s, h, dqk = q.shape
    nb = s // Q_BLOCK
    scale = QK_HEAD_DIM ** -0.5
    q_blocks = q.reshape(b, nb, Q_BLOCK, h, dqk).transpose(1, 0, 2, 3, 4)
    k_pos = jnp.arange(s)

    def one_block(args):
        qb, blk = args
        q_pos = blk * Q_BLOCK + jnp.arange(Q_BLOCK)
        scores = jnp.einsum('bqhd,bkhd->bhqk', qb, k, preferred_element_type=jnp.float32) * scale
        mask = k_pos[None, :] <= q_pos[:, None]
        scores = jnp.where(mask[None, None], scores, -jnp.inf)
        p = jax.nn.softmax(scores, axis=-1)
        return jnp.einsum('bhqk,bkhd->bqhd', p.astype(v.dtype), v)

    out = lax.map(one_block, (q_blocks, jnp.arange(nb)))
    return out.transpose(1, 0, 2, 3, 4).reshape(b, s, h, v.shape[-1])

def mla_mixer(h, positions, w_dqkv, q_norm_g, w_uq, kv_norm_g, w_ukv, qk_q_g, qk_k_g, w_o):
    b, s, _ = h.shape
    lat = h @ w_dqkv
    c_q = rms_norm(lat[..., :Q_LORA_RANK], q_norm_g)
    c_kv = rms_norm(lat[..., Q_LORA_RANK:Q_LORA_RANK + KV_LORA_RANK], kv_norm_g)
    k_pe = lat[..., Q_LORA_RANK + KV_LORA_RANK:]
    q = (c_q @ w_uq).reshape(b, s, N_HEADS, QK_HEAD_DIM)
    kv = (c_kv @ w_ukv).reshape(b, s, N_HEADS, QK_NOPE_DIM + V_HEAD_DIM)
    k_nope, v = kv[..., :QK_NOPE_DIM], kv[..., QK_NOPE_DIM:]
    k = jnp.concatenate([k_nope, jnp.broadcast_to(k_pe[:, :, None, :], (b, s, N_HEADS, QK_ROPE_DIM))], axis=-1)
    q = rms_norm(q, qk_q_g)
    k = rms_norm(k, qk_k_g)
    q = jnp.concatenate([q[..., :QK_NOPE_DIM], rope(q[..., QK_NOPE_DIM:], positions)], axis=-1)
    k = jnp.concatenate([k[..., :QK_NOPE_DIM], rope(k[..., QK_NOPE_DIM:], positions)], axis=-1)
    o = causal_block_attention(q, k, v)
    return o.reshape(b, s, N_HEADS * V_HEAD_DIM) @ w_o

def conformer_conv_mixer(h, pw1_w, pw1_b, dw_w, dw_b, ln_g, ln_b, pw2_w, pw2_b):
    u = h @ pw1_w + pw1_b
    u = u[..., :CONV_DIM] * jax.nn.sigmoid(u[..., CONV_DIM:])
    u = lax.conv_general_dilated(
        u, dw_w[:, None, :], window_strides=(1,), padding=[(CONV_WIDTH - 1, 0)],
        dimension_numbers=('NWC', 'WIO', 'NWC'), feature_group_count=CONV_DIM) + dw_b
    u = jax.nn.silu(layer_norm(u, ln_g, ln_b))
    return u @ pw2_w + pw2_b

def route(h, router_w, router_bias):
    b, s, _ = h.shape
    logits = jnp.einsum('bsd,de->bse', h.astype(jnp.float32), router_w.astype(jnp.float32))
    scores = jax.nn.sigmoid(logits)
    biased = scores + router_bias.astype(jnp.float32)
    grouped = biased.reshape(b, s, N_GROUPS, EXPERTS_PER_GROUP)
    group_score = jnp.sum(lax.top_k(grouped, TOP_K)[0], axis=-1)
    g_sel = jnp.argmax(group_score, axis=-1)
    g_idx = jnp.broadcast_to(g_sel[..., None, None], (b, s, 1, EXPERTS_PER_GROUP))
    in_group = jnp.take_along_axis(grouped, g_idx, axis=2)[:, :, 0, :]
    _, local_idx = lax.top_k(in_group, TOP_K)
    expert_idx = g_sel[..., None] * EXPERTS_PER_GROUP + local_idx
    w = jnp.take_along_axis(scores, expert_idx, axis=-1)
    w = w / jnp.sum(w, axis=-1, keepdims=True)
    gates = jnp.sum(jax.nn.one_hot(expert_idx, N_EXPERTS, dtype=jnp.float32) * w[..., None], axis=-2)
    return gates

def moe_ffn(h, gates, w_gate, w_up, w_down):
    out = jnp.zeros_like(h)
    for e in range(N_EXPERTS):
        a = jax.nn.silu(h @ w_gate[e]) * (h @ w_up[e])
        out = out + gates[..., e:e + 1].astype(h.dtype) * (a @ w_down[e])
    return out

def setup_inputs(seed: int = 0) -> dict:
    key = jax.random.key(seed)
    ks = jax.random.split(key, 32)
    f32 = jnp.float32
    D = D_MODEL

    def nrm(k, shape, fan_in, mult=1.0):
        return jax.random.normal(k, shape, f32) * (mult * fan_in ** -0.5)

    def gain(k, shape):
        return 1.0 + 0.05 * jax.random.normal(k, shape, f32)

    def bias(k, shape):
        return 0.01 * jax.random.normal(k, shape, f32)

    x = jax.random.normal(ks[0], (BATCH, SEQ, D), f32)
    c = jax.random.normal(ks[1], (BATCH, D), f32)
    offsets = jax.random.randint(ks[2], (BATCH, 1), 0, 1024, dtype=jnp.int32)
    positions = (offsets + jnp.arange(SEQ, dtype=jnp.int32)[None, :]).astype(jnp.int32)
    NA, NC = N_ATTN_LAYERS, N_CONV_LAYERS
    return {
        'x': x,
        'c': c,
        'positions': positions,
        'ada_w': nrm(ks[3], (DEPTH, D, 6 * D), D, 0.5),
        'ada_b': bias(ks[4], (DEPTH, 6 * D)),
        'norm1_g': gain(ks[5], (DEPTH, D)),
        'norm2_g': gain(ks[6], (DEPTH, D)),
        'mla_w_dqkv': nrm(ks[7], (NA, D, Q_LORA_RANK + KV_LORA_RANK + QK_ROPE_DIM), D),
        'mla_q_norm_g': gain(ks[8], (NA, Q_LORA_RANK)),
        'mla_w_uq': nrm(ks[9], (NA, Q_LORA_RANK, N_HEADS * QK_HEAD_DIM), Q_LORA_RANK),
        'mla_kv_norm_g': gain(ks[10], (NA, KV_LORA_RANK)),
        'mla_w_ukv': nrm(ks[11], (NA, KV_LORA_RANK, N_HEADS * (QK_NOPE_DIM + V_HEAD_DIM)), KV_LORA_RANK),
        'mla_qk_q_g': gain(ks[12], (NA, QK_HEAD_DIM)),
        'mla_qk_k_g': gain(ks[13], (NA, QK_HEAD_DIM)),
        'mla_w_o': nrm(ks[14], (NA, N_HEADS * V_HEAD_DIM, D), N_HEADS * V_HEAD_DIM),
        'conv_pw1_w': nrm(ks[15], (NC, D, 2 * CONV_DIM), D),
        'conv_pw1_b': bias(ks[16], (NC, 2 * CONV_DIM)),
        'conv_dw_w': nrm(ks[17], (NC, CONV_WIDTH, CONV_DIM), CONV_WIDTH),
        'conv_dw_b': bias(ks[18], (NC, CONV_DIM)),
        'conv_ln_g': gain(ks[19], (NC, CONV_DIM)),
        'conv_ln_b': bias(ks[20], (NC, CONV_DIM)),
        'conv_pw2_w': nrm(ks[21], (NC, CONV_DIM, D), CONV_DIM),
        'conv_pw2_b': bias(ks[22], (NC, D)),
        'router_w': nrm(ks[23], (D, N_EXPERTS), D),
        'router_bias': bias(ks[24], (N_EXPERTS,)),
        'moe_w_gate': nrm(ks[25], (DEPTH, N_EXPERTS, D, EXPERT_FF), D),
        'moe_w_up': nrm(ks[26], (DEPTH, N_EXPERTS, D, EXPERT_FF), D),
        'moe_w_down': nrm(ks[27], (DEPTH, N_EXPERTS, EXPERT_FF, D), EXPERT_FF),
    }

def reference(x, c, positions, ada_w, ada_b, norm1_g, norm2_g,
              mla_w_dqkv, mla_q_norm_g, mla_w_uq, mla_kv_norm_g, mla_w_ukv,
              mla_qk_q_g, mla_qk_k_g, mla_w_o,
              conv_pw1_w, conv_pw1_b, conv_dw_w, conv_dw_b, conv_ln_g, conv_ln_b,
              conv_pw2_w, conv_pw2_b,
              router_w, router_bias, moe_w_gate, moe_w_up, moe_w_down):
    mod_all = jnp.einsum('bd,lde->lbe', jax.nn.silu(c), ada_w) + ada_b[:, None, :]
    for i in range(DEPTH):
        shift1, scale1, gate1, shift2, scale2, gate2 = jnp.split(mod_all[i][:, None, :], 6, axis=-1)
        h = rms_norm(x, norm1_g[i]) * (1 + scale1) + shift1
        j = i // N_MIXERS
        if i % N_MIXERS == 0:
            y = mla_mixer(h, positions, mla_w_dqkv[j], mla_q_norm_g[j], mla_w_uq[j],
                          mla_kv_norm_g[j], mla_w_ukv[j], mla_qk_q_g[j], mla_qk_k_g[j], mla_w_o[j])
        else:
            y = conformer_conv_mixer(h, conv_pw1_w[j], conv_pw1_b[j], conv_dw_w[j], conv_dw_b[j],
                                     conv_ln_g[j], conv_ln_b[j], conv_pw2_w[j], conv_pw2_b[j])
        x = x + gate1 * y
        h = rms_norm(x, norm2_g[i]) * (1 + scale2) + shift2
        gates = route(h, router_w, router_bias)
        x = x + gate2 * moe_ffn(h, gates, moe_w_gate[i], moe_w_up[i], moe_w_down[i])
    return x


_drawn_inputs = setup_inputs


def setup_inputs(seed=0):
    import zlib

    import numpy as np

    out = dict(_drawn_inputs(seed))
    spreads = {}
    factors = {'mla_q_norm_g': 3.514,
     'mla_kv_norm_g': 3.592,
     'mla_qk_q_g': 3.844,
     'mla_qk_k_g': 4.864,
     'conv_pw1_b': 8.0,
     'conv_dw_b': 4.19,
     'conv_ln_g': 3.281,
     'conv_ln_b': 34.403,
     'conv_pw2_b': 24.923}
    for name, (base, spread) in spreads.items():
        noise = np.random.default_rng([zlib.crc32(name.encode()), seed]).standard_normal(out[name].shape)
        drawn = base * np.exp(spread * noise) if base else spread * noise
        out[name] = __import__('jax').numpy.asarray(drawn.astype(out[name].dtype))
    for name, factor in factors.items():
        out[name] = (out[name] * factor).astype(out[name].dtype)
    return out
```

```python
from contextlib import ExitStack

import concourse.bass as bass
from concourse import mybir

P = 128
D = 1024
T = 256
KD = D // P
NT = T // P
HEADS = 8
PAIRS = HEADS // 2
NOPE = 128
ROPE = 64
QK = NOPE + ROPE
VD = 128
QR = 768
KVR = 256
KQ = QR // P
KKV = KVR // P
TAPS = 31
PADL = TAPS - 1
E = 16
GRP = 4
PER = E // GRP
FF = 512
KF = FF // P
SLOTS = 2 * T
SB = SLOTS // P
CHUNK = 64
MAXCH = T // CHUNK
EPS = 1e-6
SCALE = float(QK) ** -0.5

RING = 6
SLOT_F = 4 * (QR + KVR + ROPE)

VC = {}
_at = 0
for _name, _n in (("norm1", 2 * KD), ("norm2", 2 * KD), ("ada_b", 2 * 48), ("q_norm", KQ), ("kv_norm", KKV),
                  ("gq_nope", 1), ("gk_nope", 1), ("gq_rope", 1), ("gk_rope", 1), ("inv_freq", 1),
                  ("pw1_b", 2 * KD), ("dw_b", KD), ("ln_g", KD), ("ln_b", KD), ("pw2_b", KD), ("c", KD),
                  ("dw_w", KD * TAPS), ("router_w", KD * E)):
    VC[_name] = _at
    _at += _n
NVEC = _at

CC = {}
_at = 0
for _name, _n in (("ident", P), ("ones", P), ("before", P), ("causal", 3 * P), ("rot", P), ("sel_a", P),
                  ("sel_b", P), ("iota", SLOTS), ("tri16", 2 * E), ("first4", 2 * GRP), ("tri4", PER * PER)):
    CC[_name] = _at
    _at += _n
NCON = _at

ALU = mybir.AluOpType
ACT = mybir.ActivationFunctionType
AX = mybir.AxisListType.X
F32 = mybir.dt.float32
I32 = mybir.dt.int32

TWO_PI = 6.283185307179586
PI_A = 6.28125
PI_B = 0.0019350051879882812
PI_C = TWO_PI - PI_A - PI_B
MAGIC = 12582912.0

NA_PRE = 18


def unit_plan():
    first = [("ada", j) for j in range(4)] + [("dqkv", 0), ("dqkv", 1), ("ukv", 0)]
    first += [("uq", i) for i in range(3)] + [("ada", j) for j in range(4, NA_PRE)] + [("wo", 0), ("wo", 1)]
    second = [("pw1", i) for i in range(4)] + [("ada", j) for j in range(NA_PRE, 24)] + [("pw2", 0), ("pw2", 1)]
    return first, second


def build(nc, xT, vec, con, rbias, pos, ada_w, w_dqkv, w_uq, w_ukv, w_o, pw1, pw2, w_gate, w_up, w_down, out):
    ctx = ExitStack()
    with ctx:
        def sb(name, shape, dt=F32):
            return ctx.enter_context(nc.sbuf_tensor(name, shape, dt))

        def sem(name):
            return ctx.enter_context(nc.semaphore(name))

        PS = ctx.enter_context(nc.psum_tensor("ps", [P, 8, 512], F32))
        ring = [sb(f"ring{s}", [P, SLOT_F]) for s in range(RING)]
        XT = sb("XT", [P, KD, T])
        hT = sb("hT", [P, KD, T])
        V = sb("vecs", [P, NVEC])
        C = sb("consts", [P, NCON])
        rb = sb("router_bias", [P, E])
        mods = sb("mods", [P, 2, 48])
        gsc = sb("norm_gain", [P, 4, KD])
        sc = sb("silu_c", [P, KD])
        rstd = sb("rstd", [P, 512])
        root = sb("root", [P, 512])
        tab = sb("chunk_table", [P, 2, 3 * E], I32)
        WORK = sb("work", [P, 14800])

        def view(at, *shape):
            n = 1
            for s in shape:
                n *= s
            v = WORK[:, at:at + n]
            if len(shape) == 2:
                v = v.rearrange("p (a b) -> p a b", b=shape[1])
            if len(shape) == 3:
                v = v.rearrange("p (a b c) -> p a b c", b=shape[1], c=shape[2])
            return v

        sq = view(0, KD, T)
        latT = view(2048, 9, T)
        kn = view(4352, HEADS, T)
        kr = view(6400, PAIRS, T)
        vt = view(7424, NT, HEADS * VD)
        qn = view(9472, HEADS, T)
        qr = view(11520, PAIRS, T)
        sin_t = view(12544, T)
        cos_t = view(12800, T)
        ropetmp = view(13056, 2, T)
        krope = view(13568, T)
        kpe_sq = view(13824, T)
        posi = WORK[:, 14080:14336].bitcast(I32)
        attn_s = view(0, 2, 3 * P)
        attn_p = view(768, 2, 3 * P)
        attn_pt = view(2048, 2, 3 * P)
        attn_sm = view(2816, 2, 8)
        oT = hT
        hgT = view(0, KD, SLOTS + CHUNK)
        yT = view(4608, KD, SLOTS + CHUNK)
        htok = view(4608, NT, D)
        perm = view(4608 + 2048, NT, SLOTS)
        ysl = view(9216, SB, D)
        wperm = view(9216, NT, SLOTS)
        wpT = view(13312, SB, T)
        small = view(10240, 2048)
        upad = view(2048, KD, PADL + T)
        cacc = view(4352, KD, T)
        sig = view(6400, 2, T)
        csq = view(0, KD, T)

        small_gb = view(7000, KD)
        eps = sb("eps", [P, 2])
        eps_ready = sem("eps_ready")
        qk_scaled_all = sem("root_read")

        hc = sb("chunk_in", [P, KD, CHUNK])
        sg = sb("chunk_silu", [P, KF, CHUNK])
        aT = sb("chunk_act", [P, KF, CHUNK])

        def vcol(name, i=0, n=1):
            return V[:, VC[name] + i:VC[name] + i + n]

        def con_(name, n=P, at=0, rows=P):
            return C[0:rows, CC[name] + at:CC[name] + at + n]

        ident, ones = con_("ident"), con_("ones")
        LT = range(2)

        x_in, vec_in, con_in, rb_in, pos_in = (sem(n) for n in ("x_in", "vec_in", "con_in", "rb_in", "pos_in"))
        slot_landed = [sem(f"slot_landed{s}") for s in range(RING)]
        unit_used = sem("unit_used")
        silu_c = sem("silu_c_ready")
        ada_done, ada_stored, mods_ready = sem("ada_done"), sem("ada_stored"), sem("mods_ready")
        dve_seq, act_seq = sem("dve_seq"), sem("act_seq")
        resid = sem("residual_updated")
        N4 = range(4)
        norm_sq = [sem(f"norm_sq{n}") for n in N4]
        norm_sum = [sem(f"norm_sum{n}") for n in N4]
        norm_root = [sem(f"norm_root{n}") for n in N4]
        norm_scaled = [sem(f"norm_scaled{n}") for n in N4]
        h_ready = [sem(f"h_ready{n}") for n in N4]
        angles, tables = sem("rope_angles"), sem("rope_tables")
        lat_done, lat_stored, lat_sq, lat_sum, lat_root, lat_ready = (
            sem(n) for n in ("lat_done", "lat_stored", "lat_sq", "lat_sum", "lat_root", "lat_ready"))
        kpe_scaled, kpe_rot, krope_ready = sem("kpe_scaled"), sem("kpe_rot"), sem("krope_ready")
        qk_done, qk_stored, qk_sum, qk_root, qk_scaled, q_rot, qk_ready = (
            sem(n) for n in ("qk_done", "qk_stored", "qk_sum", "qk_root", "qk_scaled", "q_rot", "qk_ready"))
        v_done, v_stored = sem("v_done"), sem("v_stored")
        s_done, s_masked, s_max, p_exp, p_ready, pt_done, pt_stored, o_done, o_stored = (
            sem(n) for n in ("s_done", "s_masked", "s_max", "p_exp", "p_ready", "pt_done", "pt_stored",
                             "o_done", "o_stored"))
        wo_done = sem("wo_done")
        glu_done, glu_sig, glu_ready = sem("glu_done"), sem("glu_sig"), sem("glu_ready")
        conv_ready, ln_sum, ln_mean, ln_centred, ln_sq, ln_var, ln_root, ln_scaled, ln_silu = (
            sem(n) for n in ("conv_ready", "ln_sum", "ln_mean", "ln_centred", "ln_sq", "ln_var", "ln_root",
                             "ln_scaled", "ln_silu"))
        pw2_done = sem("pw2_done")
        logits_done, scores_ready, picks_ready, counts_done, count_rows, offs_done, table_ready = (
            [sem(f"{n}{l}") for l in LT] for n in ("logits_done", "scores_ready", "picks_ready", "counts_done",
                                                   "count_rows", "offs_done", "table_ready"))
        htok_done, htok_stored, perm_ready, wperm_ready, gather_done, gather_stored, wpt_done, wpt_stored = (
            [sem(f"{n}{l}") for l in LT] for n in ("htok_done", "htok_stored", "perm_ready", "wperm_ready",
                                                   "gather_done", "gather_stored", "wpt_done", "wpt_stored"))
        hc_ready, gate_done, silu_done, up_done, act_ready, down_done, y_stored = (
            [sem(f"{n}{l}") for l in LT] for n in ("hc_ready", "gate_done", "silu_done", "up_done", "act_ready",
                                                   "down_done", "y_stored"))
        ysl_done, ysl_stored, moe_done = ([sem(f"{n}{l}") for l in LT] for n in ("ysl_done", "ysl_stored",
                                                                                 "moe_done"))
        padded = sem("hgt_padded")
        stored = sem("out_stored")

        first, second = unit_plan()
        U1 = len(first)
        U2 = U1 + 3 * E
        U3 = U2 + len(second)
        MOE_AT = (U1, U3)
        unit_no = {}
        for i, u in enumerate(first):
            unit_no[u] = i
        for i, u in enumerate(second):
            unit_no[u] = U2 + i
        static_no = {u: i for i, u in enumerate(first + second)}

        def slot(u):
            return u % RING

        def wait_unit(eng, u):
            eng.wait_ge(slot_landed[slot(u)], 16 * (u // RING + 1))

        def unit_ap(kind, i):
            r = ring[slot(unit_no[(kind, i)])]
            shape = {"ada": (KD, 512), "dqkv": (4, QR + KVR + ROPE), "ukv": (2, 2048), "uq": (2, HEADS * QK),
                     "wo": (4, D), "pw1": (2, 2 * D), "pw2": (4, D)}[kind]
            return r[:, 0:shape[0] * shape[1]].rearrange("p (k n) -> p k n", n=shape[1])

        def tiles(w, n=None):
            return w.rearrange("(k p) n -> p k n", p=P)

        def unit_source(kind, i):
            if kind == "ada":
                l, j = divmod(i, 12)
                return tiles(ada_w[l])[:, :, j * 512:(j + 1) * 512]
            w, step = {"dqkv": (w_dqkv, 4), "ukv": (w_ukv, 2), "uq": (w_uq, 2), "wo": (w_o, 4),
                       "pw1": (pw1, 2), "pw2": (pw2, 4)}[kind]
            return tiles(w)[:, i * step:(i + 1) * step, :]

        expert_w = (w_gate, w_up, w_down)

        def expert_ap(u, i):
            n = FF if i < 2 else D
            return ring[slot(u)][:, 0:4096].rearrange("p (k n) -> p k n", n=n)

        block = ctx.enter_context(nc.Block())

        @block.sync
        def _(sp):
            def load_static(u, kind, i):
                sp.dma_start(unit_ap(kind, i), unit_source(kind, i)).then_inc(slot_landed[slot(u)], 16)

            def load_expert(l, u, e, i):
                n = FF if i < 2 else D
                k = KD if i < 2 else KF
                src = expert_w[i][l].rearrange("e (k p) n -> e p k n", p=P)
                if not isinstance(e, int):
                    src = src[bass.ds(e, 1)].rearrange("e p k n -> (e p) k n")
                else:
                    src = src[e]
                sp.dma_start(expert_ap(u, i), src).then_inc(slot_landed[slot(u)], 16)

            def table(l, col):
                return sp.value_load(tab[0:1, l, col] if not isinstance(col, int) else tab[0:1, l, col:col + 1],
                                     min_val=1, max_val=E * MAXCH + 1)

            def mixer_units(units, base, after_moe):
                for n, (kind, i) in enumerate(units):
                    u = base + n
                    if u >= RING:
                        if n >= RING:
                            sp.wait_ge(unit_used, static_no[units[n - RING]] + 1)
                        elif after_moe is not None:
                            e, part = E - 2 + n // 3, n % 3
                            if part == 0:
                                end = table(after_moe, 2 * E + e)
                            sp.wait_ge(down_done[after_moe] if part == 2 else up_done[after_moe], end)
                    load_static(u, kind, i)

            def moe_units(l):
                base = MOE_AT[l]
                before = (first, second)[l]
                first_used = len(first) * (l > 0) + len(before) - RING
                for n in range(RING):
                    sp.wait_ge(unit_used, first_used + n + 1)
                    load_expert(l, base + n, n // 3, n % 3)
                sp.wait_ge(table_ready[l], 1)
                with sp.Fori(1, E // 2) as p:
                    for q in range(2):
                        end = table(l, bass.ds(p * 2 + (2 * E - 2 + q), 1))
                        for i in range(3):
                            sp.wait_ge(down_done[l] if i == 2 else up_done[l], end)
                            load_expert(l, base + 3 * q + i, p * 2 + q, i)

            mixer_units(first, 0, None)
            moe_units(0)
            mixer_units(second, U2, 0)
            moe_units(1)
            for k in range(0, KD, 2):
                sp.wait_ge(resid, 3 * KD + k + 2)
                sp.dma_start(out[:, k:k + 2, :], XT[:, k:k + 2, :]).then_inc(stored, 16)
            sp.wait_ge(stored, 16 * (KD // 2))

        @block.tensor
        def _(pe):
            mm = nc.tensor.matmul
            tr = nc.tensor.transpose

            def used(ins):
                ins.then_inc(unit_used, 1)

            def ada(a):
                wait_unit(pe, unit_no[("ada", a)])
                if a == 0:
                    pe.wait_ge(silu_c, 1)
                if a >= 2:
                    pe.wait_ge(ada_stored, a - 1)
                w = unit_ap("ada", a)
                for m in range(4):
                    for k in range(KD):
                        ins = mm(PS[:, 6 + a % 2, m:m + 1], w[:, k, m * P:(m + 1) * P], sc[:, k:k + 1],
                                 start=(k == 0), stop=(k == KD - 1))
                ins.then_inc(ada_done, 1)
                pe.wait_ge(ada_done, a + 1)
                pe.sem_inc(unit_used, 1)

            def norm_sums(n):
                for i in range(4):
                    pe.wait_ge(norm_sq[n], i + 1)
                    for k in (2 * i, 2 * i + 1):
                        ins = mm(PS[:, 4, 0:T], ones, sq[:, k, :], start=(k == 0), stop=(k == KD - 1))
                ins.then_inc(norm_sum[n], 1)

            def lat():
                wait_unit(pe, unit_no[("dqkv", 0)])
                wait_unit(pe, unit_no[("dqkv", 1)])
                pe.wait_ge(norm_root[0], 1)
                w = [unit_ap("dqkv", 0), unit_ap("dqkv", 1)]
                for m in range(9):
                    b, at = m // 2, (m % 2) * T
                    for k in range(KD):
                        if m == 0:
                            pe.wait_ge(h_ready[0], k + 1)
                        wk = w[k // 4][:, k % 4, :]
                        if m < 8:
                            ins = mm(PS[:, b, at:at + T], wk[:, m * P:(m + 1) * P], hT[:, k, :],
                                     start=(k == 0), stop=(k == KD - 1))
                        else:
                            for half in range(2):
                                ins = mm(PS[64 * half:64 * half + 64, b, 0:T], wk[:, 1024:1088], hT[:, k, :],
                                         start=(k == 0), stop=(k == KD - 1))
                    if m % 2 == 1 or m == 8:
                        ins.then_inc(lat_done, 1)
                pe.wait_ge(lat_done, 5)
                pe.sem_inc(unit_used, 2)
                pe.wait_ge(lat_sq, 4)
                for m in range(KQ):
                    mm(PS[:, 5, 0:T], ones, sq[:, m, :], start=(m == 0), stop=(m == KQ - 1))
                for m in range(KKV):
                    ins = mm(PS[:, 5, T:2 * T], ones, sq[:, KQ + m, :], start=(m == 0), stop=(m == KKV - 1))
                ins.then_inc(lat_sum, 1)
                pe.wait_ge(kpe_scaled, 1)
                pe.wait_ge(lat_stored, 5)
                mm(PS[:, 4, 0:T], con_("rot"), ropetmp[:, 1, :], start=True, stop=True).then_inc(kpe_rot, 1)

            def k_proj(g):
                if g == 0:
                    wait_unit(pe, unit_no[("ukv", 0)])
                    pe.wait_ge(lat_ready, 8)
                if g >= 2:
                    pe.wait_ge(qk_stored, g - 1)
                w = unit_ap("ukv", 0)
                for a in range(2):
                    h = 2 * g + a
                    for k in range(KKV):
                        ins = mm(PS[:, g % 2, a * T:(a + 1) * T], w[:, k, h * 256:h * 256 + NOPE],
                                 latT[:, KQ + k, :], start=(k == 0), stop=(k == KKV - 1))
                ins.then_inc(qk_done, 1)

            def k_sum(g):
                pe.wait_ge(qk_stored, g + 1)
                if g == 0:
                    pe.wait_ge(krope_ready, 1)
                if g >= 2:
                    pe.wait_ge(qk_root, g - 1)
                b = 4 + g % 2
                mm(PS[:, b, :], ones, sq[:, 2 * (g % 2):2 * (g % 2) + 2, :].rearrange("p a t -> p (a t)"),
                   start=True, stop=False)
                for a in range(2):
                    ins = mm(PS[:, b, a * T:(a + 1) * T], con_("sel_a"), kpe_sq, start=False, stop=(a == 1))
                ins.then_inc(qk_sum, 1)

            def values():
                w = unit_ap("ukv", 0)
                n = 0
                for t in range(NT):
                    for half in range(2):
                        if n >= 2:
                            pe.wait_ge(v_stored, n - 1)
                        else:
                            pe.wait_ge(lat_stored, 4)
                        for k in range(KKV):
                            rhs = w[:, k, :].rearrange("p (h c) -> p h c", c=NOPE + VD)[:, 4 * half:4 * half + 4, NOPE:]
                            ins = mm(PS[:, 2 + n % 2, :].rearrange("p (h c) -> p h c", c=VD),
                                     latT[:, KQ + k, t * P:(t + 1) * P], rhs, start=(k == 0), stop=(k == KKV - 1))
                        ins.then_inc(v_done, 1)
                        n += 1
                pe.wait_ge(v_done, 4)
                pe.sem_inc(unit_used, 1)

            def q_proj(g):
                n = PAIRS + g
                if g == 0:
                    for i in range(3):
                        wait_unit(pe, unit_no[("uq", i)])
                    pe.wait_ge(v_stored, 4)
                pe.wait_ge(qk_stored, n - 1)
                if g >= 2:
                    pe.wait_ge(qk_ready, n - 1)
                for a in range(2):
                    h = 2 * g + a
                    for k in range(KQ):
                        w = unit_ap("uq", k // 2)
                        mm(PS[:, g % 2, a * T:(a + 1) * T], w[:, k % 2, h * NOPE:(h + 1) * NOPE],
                           latT[:, k, :], start=(k == 0), stop=(k == KQ - 1))
                for k in range(KQ):
                    w = unit_ap("uq", k // 2)[:, k % 2, HEADS * NOPE:]
                    ins = mm(PS[:, 2 + g % 2, 0:T], w[:, g * P:(g + 1) * P], latT[:, k, :],
                             start=(k == 0), stop=(k == KQ - 1))
                ins.then_inc(qk_done, 1)
                if g == PAIRS - 1:
                    pe.wait_ge(qk_done, 2 * PAIRS)
                    pe.sem_inc(unit_used, 3)

            def q_sum(g):
                n = PAIRS + g
                pe.wait_ge(qk_stored, n + 1)
                pe.wait_ge(qk_root, n - 1)
                b = 4 + g % 2
                mm(PS[:, b, :], ones, sq[:, 2 * (g % 2):2 * (g % 2) + 2, :].rearrange("p a t -> p (a t)"),
                   start=True, stop=False)
                mm(PS[:, b, 0:T], con_("sel_a"), sq[:, 4 + g % 2, :], start=False, stop=False)
                mm(PS[:, b, T:2 * T], con_("sel_b"), sq[:, 4 + g % 2, :], start=False,
                   stop=True).then_inc(qk_sum, 1)

            def q_turn(g):
                pe.wait_ge(qk_scaled, g + 1)
                mm(PS[:, 2 + g % 2, 0:T], con_("rot"), qr[:, g, :], start=True, stop=True).then_inc(q_rot, 1)

            def attn_scores(h):
                g, a = divmod(h, 2)
                if h == 0:
                    pe.wait_ge(qk_ready, 2 * PAIRS)
                if h >= 2:
                    pe.wait_ge(s_masked, h - 1)
                r = slice(64 * a, 64 * a + 64)
                b = PS[:, h % 2, :]
                for qb, at, n in ((0, 0, P), (1, P, 2 * P)):
                    q = slice(qb * P, (qb + 1) * P)
                    mm(b[:, at:at + n], qn[:, h, q], kn[:, h, 0:n], start=True, stop=False)
                    ins = mm(b[:, at:at + n], qr[r, g, q], kr[r, g, 0:n], start=False, stop=True)
                ins.then_inc(s_done, 1)

            def attn_values(h):
                pe.wait_ge(p_ready, h + 1)
                if h >= 2:
                    pe.wait_ge(pt_stored, h - 1)
                for i in range(3):
                    ins = tr(PS[:, 2 + h % 2, i * P:(i + 1) * P], attn_p[:, h % 2, i * P:(i + 1) * P], ident)
                ins.then_inc(pt_done, 1)
                pe.wait_ge(pt_stored, h + 1)
                if h >= 2:
                    pe.wait_ge(o_stored, h - 1)
                pt = attn_pt[:, h % 2, :]
                b = PS[:, 4 + h % 2, :]
                mm(b[:, 0:T], vt[:, 0, h * VD:(h + 1) * VD], pt[:, 0:T], start=True, stop=False)
                mm(b[:, P:T], vt[:, 1, h * VD:(h + 1) * VD], pt[:, T:T + P], start=False,
                   stop=True).then_inc(o_done, 1)

            def project(units, src, done, free):
                for m in range(KD):
                    for k in range(KD):
                        if m == 0:
                            free(k)
                        w = unit_ap(units, k // 4)
                        ins = mm(PS[:, m // 2, (m % 2) * T:(m % 2 + 1) * T], w[:, k % 4, m * P:(m + 1) * P],
                                 src[:, k, :], start=(k == 0), stop=(k == KD - 1))
                    if m % 2:
                        ins.then_inc(done, 1)
                pe.wait_ge(done, KD // 2)
                pe.sem_inc(unit_used, 2)

            def mixer0():
                for a in range(4):
                    ada(a)
                pe.wait_ge(con_in, 16)
                pe.wait_ge(vec_in, 16)
                norm_sums(0)
                lat()
                k_proj(0)
                k_proj(1)
                k_sum(0)
                k_proj(2)
                k_sum(1)
                k_proj(3)
                k_sum(2)
                values()
                k_sum(3)
                q_proj(0)
                q_proj(1)
                q_sum(0)
                q_turn(0)
                q_proj(2)
                q_sum(1)
                q_turn(1)
                q_proj(3)
                q_sum(2)
                q_turn(2)
                q_sum(3)
                q_turn(3)
                for h in range(HEADS):
                    attn_scores(h)
                    if h:
                        attn_values(h - 1)
                    if h < 7:
                        ada(4 + 2 * h)
                        ada(5 + 2 * h)
                attn_values(HEADS - 1)

                def free(k):
                    if k == 0:
                        wait_unit(pe, unit_no[("wo", 0)])
                        wait_unit(pe, unit_no[("wo", 1)])
                    pe.wait_ge(o_stored, k + 1)
                project("wo", oT, wo_done, free)

            def mixer1():
                norm_sums(2)
                for i in range(4):
                    wait_unit(pe, unit_no[("pw1", i)])
                for c in range(KD):
                    if c >= 2:
                        pe.wait_ge(glu_ready, c - 1)
                    for half in range(2):
                        m = c + half * KD
                        for k in range(KD):
                            if c == 0 and half == 0:
                                pe.wait_ge(h_ready[2], k + 1)
                            ins = mm(PS[:, c % 2, half * T:(half + 1) * T],
                                     unit_ap("pw1", k // 2)[:, k % 2, m * P:(m + 1) * P], hT[:, k, :],
                                     start=(k == 0), stop=(k == KD - 1))
                    ins.then_inc(glu_done, 1)
                pe.wait_ge(glu_done, KD)
                pe.sem_inc(unit_used, 4)
                for a in range(NA_PRE, 24):
                    ada(a)
                for k in range(KD):
                    pe.wait_ge(conv_ready, k + 1)
                    ins = mm(PS[:, 4, 0:T], ones, cacc[:, k, :], start=(k == 0), stop=(k == KD - 1))
                ins.then_inc(ln_sum, 1)
                for k in range(KD):
                    pe.wait_ge(ln_sq, k // 2 + 1)
                    ins = mm(PS[:, 5, 0:T], ones, csq[:, k, :], start=(k == 0), stop=(k == KD - 1))
                ins.then_inc(ln_var, 1)

                def free(k):
                    if k == 0:
                        wait_unit(pe, unit_no[("pw2", 0)])
                        wait_unit(pe, unit_no[("pw2", 1)])
                    pe.wait_ge(ln_silu, k + 1)
                project("pw2", cacc, pw2_done, free)

            def moe(l):
                base = MOE_AT[l]
                n = 2 * l + 1
                norm_sums(n)
                for t in range(NT):
                    for k in range(KD):
                        if t == 0:
                            pe.wait_ge(h_ready[n], k + 1)
                        ins = mm(PS[:, 0, t * E:(t + 1) * E], hT[:, k, t * P:(t + 1) * P],
                                 vcol("router_w", k * E, E), start=(k == 0), stop=(k == KD - 1))
                ins.then_inc(logits_done[l], 1)
                for i in range(4):
                    t, half = divmod(i, 2)
                    if i >= 2:
                        pe.wait_ge(htok_stored[l], i - 1)
                    for j in range(4):
                        ins = tr(PS[:, 3 + i % 2, j * P:(j + 1) * P],
                                 hT[:, half * 4 + j, t * P:(t + 1) * P], ident)
                    ins.then_inc(htok_done[l], 1)
                pe.wait_ge(picks_ready[l], 1)
                picks = [small[:, 256 + t * E:256 + (t + 1) * E] for t in range(NT)]
                b = PS[:, 1, :]
                mm(b[:, 0:E], con_("before"), picks[0], start=True, stop=True)
                mm(b[:, E:2 * E], con_("before"), picks[1], start=True, stop=False)
                mm(b[:, E:2 * E], ones, picks[0], start=False, stop=True)
                for t in range(NT):
                    ins = mm(b[0:E, 64:64 + P], picks[t], ones, start=(t == 0), stop=(t == NT - 1))
                ins.then_inc(counts_done[l], 1)
                pe.wait_ge(count_rows[l], 1)
                c16, n16 = small[0:E, 512:512 + P], small[0:E, 640:640 + P]
                b = PS[:, 2, :]
                mm(b[:, 0:E], c16, con_("tri16", E, 0, E), start=True, stop=True)
                mm(b[:, E:2 * E], n16, con_("tri16", E, 0, E), start=True, stop=True)
                mm(b[:, 2 * E:3 * E], n16, con_("tri16", E, E, E), start=True, stop=True).then_inc(offs_done[l], 1)
                pe.wait_ge(htok_stored[l], 4)
                for k in range(KD):
                    if k == 0:
                        pe.wait_ge(perm_ready[l], NT)
                    if k >= 3:
                        pe.wait_ge(gather_stored[l], k - 2)
                    for t in range(NT):
                        ins = mm(PS[:, 3 + k % 3, :], htok[:, t, k * P:(k + 1) * P], perm[:, t, :],
                                 start=(t == 0), stop=(t == NT - 1))
                    ins.then_inc(gather_done[l], 1)
                pe.wait_ge(wperm_ready[l], NT)
                for s in range(SB):
                    for t in range(NT):
                        ins = tr(PS[:, s // 2, (s % 2) * T + t * P:(s % 2) * T + (t + 1) * P],
                                 wperm[:, t, s * P:(s + 1) * P], ident)
                    if s % 2:
                        ins.then_inc(wpt_done[l], 1)
                pe.wait_ge(wpt_stored[l], 2)
                pe.wait_ge(table_ready[l], 1)
                for primed in (up_done, down_done):
                    pe.sem_inc(primed[l], 1)
                with pe.Fori(0, E // 2) as p:
                    for q in range(2):
                        us = [base + 3 * q + i for i in range(3)]
                        begin = pe.value_load(tab[0:1, l, bass.ds(p * 2 + (E + q), 1)], min_val=1,
                                              max_val=E * MAXCH + 1)
                        end = pe.value_load(tab[0:1, l, bass.ds(p * 2 + (2 * E + q), 1)], min_val=1,
                                            max_val=E * MAXCH + 1)

                        def landed(i):
                            pe.wait_ge(slot_landed[slot(us[i])], p * 16 + 16 * (us[i] // RING + 1))

                        with pe.Fori(begin, end) as g:
                            gate, up, down = (expert_ap(us[i], i) for i in range(3))
                            landed(0)
                            pe.wait_ge(hc_ready[l], g)
                            pe.wait_ge(silu_done[l], g)
                            for m in range(KF):
                                for k in range(KD):
                                    ins = mm(PS[:, 0, m * CHUNK:(m + 1) * CHUNK], gate[:, k, m * P:(m + 1) * P],
                                             hc[:, k, :], start=(k == 0), stop=(k == KD - 1))
                            ins.then_inc(gate_done[l], 1)
                            landed(1)
                            for m in range(KF):
                                for k in range(KD):
                                    ins = mm(PS[:, 1, m * CHUNK:(m + 1) * CHUNK], up[:, k, m * P:(m + 1) * P],
                                             hc[:, k, :], start=(k == 0), stop=(k == KD - 1))
                            ins.then_inc(up_done[l], 1)
                            landed(2)
                            pe.wait_ge(act_ready[l], g + 1)
                            pe.wait_ge(y_stored[l], g)
                            for m in range(KD):
                                for k in range(KF):
                                    ins = mm(PS[:, 2, m * CHUNK:(m + 1) * CHUNK], down[:, k, m * P:(m + 1) * P],
                                             aT[:, k, :], start=(k == 0), stop=(k == KF - 1))
                            ins.then_inc(down_done[l], 1)
                total = pe.value_load(tab[0:1, l, 3 * E - 1:3 * E], min_val=1, max_val=E * MAXCH + 1)
                pe.wait_ge(y_stored[l], total)
                for i in range(8):
                    s, half = divmod(i, 2)
                    if i >= 2:
                        pe.wait_ge(ysl_stored[l], i - 1)
                    for j in range(4):
                        k = half * 4 + j
                        ins = tr(PS[:, 3 + i % 2, j * P:(j + 1) * P], yT[:, k, s * P:(s + 1) * P], ident)
                    ins.then_inc(ysl_done[l], 1)
                pe.wait_ge(ysl_stored[l], 8)
                banks = (5, 0, 1, 2)
                for k in range(KD):
                    for s in range(SB):
                        ins = mm(PS[:, banks[k // 2], (k % 2) * T:(k % 2 + 1) * T], ysl[:, s, k * P:(k + 1) * P],
                                 wpT[:, s, :], start=(s == 0), stop=(s == SB - 1))
                    if k % 2:
                        ins.then_inc(moe_done[l], 1)

            mixer0()
            moe(0)
            mixer1()
            moe(1)

        @block.scalar
        def _(act):
            A = nc.scalar.activation
            act.dma_start(V[:], vec).then_inc(vec_in, 16)
            act.dma_start(XT[:], xT).then_inc(x_in, 16)
            act.dma_start(C[:], con).then_inc(con_in, 16)
            act.dma_start(posi, pos).then_inc(pos_in, 16)
            act.dma_start(rb[:], rbias).then_inc(rb_in, 16)
            act.wait_ge(eps_ready, 2)
            act.wait_ge(vec_in, 16)
            A(sc[:], vcol("c", 0, KD), ACT.Silu).then_inc(silu_c, 1)

            def norm(n):
                for i in range(4):
                    if n == 0:
                        act.wait_ge(x_in, 16)
                    else:
                        act.wait_ge(resid, KD * (n - 1) + 2 * i + 2)
                    A(sq[:, 2 * i:2 * i + 2, :], XT[:, 2 * i:2 * i + 2, :], ACT.Square).then_inc(norm_sq[n], 1)
                act.wait_ge(norm_sum[n], 1)
                A(root[:, 0:T], PS[:, 4, 0:T], ACT.Sqrt, bias=eps[:, 0:1], scale=1.0 / D).then_inc(norm_root[n], 1)
                l, w = divmod(n, 2)
                act.wait_ge(mods_ready, n + 1)
                for k in range(KD):
                    act.wait_ge(norm_scaled[n], k // 2 + 1)
                    A(hT[:, k, :], hT[:, k, :], ACT.Identity, bias=mods[:, l, 24 * w + k:24 * w + k + 1],
                      scale=gsc[:, n, k:k + 1]).then_inc(h_ready[n], 1)

            def root_of(dst, src, n):
                return A(dst, src, ACT.Sqrt, bias=eps[:, 0:1], scale=1.0 / n)

            def mixer0():
                norm(0)
                for b in range(5):
                    act.wait_ge(lat_done, b + 1)
                    if b < 4:
                        A(latT[:, 2 * b:2 * b + 2, :], PS[:, b, :].rearrange("p (a t) -> p a t", t=T),
                          ACT.Copy).then_inc(lat_stored, 1)
                    else:
                        A(latT[:, 8, :], PS[:, 4, 0:T], ACT.Copy).then_inc(lat_stored, 1)
                act.wait_ge(lat_stored, 5)
                for b in range(4):
                    A(sq[:, 2 * b:2 * b + 2, :], latT[:, 2 * b:2 * b + 2, :], ACT.Square).then_inc(lat_sq, 1)
                A(kpe_sq, latT[:, 8, :], ACT.Square).then_inc(act_seq, 1)
                act.wait_ge(lat_sum, 1)
                root_of(root[:, 0:T], PS[:, 5, 0:T], QR).then_inc(lat_root, 1)
                root_of(root[:, T:2 * T], PS[:, 5, T:2 * T], KVR).then_inc(lat_root, 1)
                act.wait_ge(angles, 2)
                A(sin_t, sin_t, ACT.Sin).then_inc(tables, 1)
                A(cos_t, cos_t, ACT.Sin, bias=eps[:, 1:2], scale=-1.0).then_inc(tables, 1)

                def store(n):
                    act.wait_ge(qk_done, n + 1)
                    if n == 0:
                        act.wait_ge(lat_sum, 1)
                    if n >= 2:
                        act.wait_ge(qk_sum, n - 1)
                    g = n % PAIRS
                    dst = (kn if n < PAIRS else qn)[:, 2 * g:2 * g + 2, :]
                    bank = PS[:, n % 2, :].rearrange("p (a t) -> p a t", t=T)
                    A(dst, bank, ACT.Copy)
                    last = A(sq[:, 2 * (n % 2):2 * (n % 2) + 2, :], bank, ACT.Square)
                    if n >= PAIRS:
                        A(qr[:, g, :], PS[:, 2 + n % 2, 0:T], ACT.Copy)
                        last = A(sq[:, 4 + n % 2, :], PS[:, 2 + n % 2, 0:T], ACT.Square)
                    last.then_inc(qk_stored, 1)

                def root_qk(n):
                    act.wait_ge(qk_sum, n + 1)
                    act.wait_ge(qk_scaled_all, n)
                    root_of(root[:], PS[:, 4 + n % 2, :], QK).then_inc(qk_root, 1)

                def store_v(n):
                    act.wait_ge(v_done, n + 1)
                    t, half = divmod(n, 2)
                    A(vt[:, t, half * 512:(half + 1) * 512], PS[:, 2 + n % 2, :], ACT.Copy).then_inc(v_stored, 1)

                store(0)
                store(1)
                root_qk(0)
                store(2)
                root_qk(1)
                store(3)
                root_qk(2)
                for n in range(4):
                    store_v(n)
                root_qk(3)
                store(4)
                store(5)
                root_qk(4)
                store(6)
                root_qk(5)
                store(7)
                root_qk(6)
                root_qk(7)
                for h in range(HEADS):
                    act.wait_ge(s_max, h + 1)
                    if h >= 2:
                        act.wait_ge(pt_done, h - 1)
                    sm = attn_sm[:, h % 2, :]
                    for i, (at, n) in enumerate(((0, P), (P, 2 * P))):
                        A(attn_p[:, h % 2, at:at + n], attn_s[:, h % 2, at:at + n], ACT.Exp,
                          bias=sm[:, 2 + i:3 + i], accum_out=sm[:, 4 + i:5 + i]).then_inc(p_exp, 1)
                    act.wait_ge(pt_done, h + 1)
                    if h >= 2:
                        act.wait_ge(o_done, h - 1)
                    A(attn_pt[:, h % 2, :], PS[:, 2 + h % 2, 0:3 * P], ACT.Copy).then_inc(pt_stored, 1)
                    act.wait_ge(o_done, h + 1)
                    A(oT[:, h, :], PS[:, 4 + h % 2, 0:T], ACT.Copy).then_inc(o_stored, 1)

            def mixer1():
                norm(2)
                for c in range(KD):
                    act.wait_ge(glu_done, c + 1)
                    if c >= 2:
                        act.wait_ge(glu_ready, c - 1)
                    A(sig[:, c % 2, :], PS[:, c % 2, T:2 * T], ACT.Sigmoid,
                      bias=vcol("pw1_b", KD + c)).then_inc(glu_sig, 1)
                act.wait_ge(ln_sum, 1)
                A(rstd[:, T:2 * T], PS[:, 4, 0:T], ACT.Copy, scale=1.0 / D).then_inc(ln_mean, 1)
                for i in range(4):
                    act.wait_ge(ln_centred, i + 1)
                    A(csq[:, 2 * i:2 * i + 2, :], cacc[:, 2 * i:2 * i + 2, :], ACT.Square).then_inc(ln_sq, 1)
                act.wait_ge(ln_var, 1)
                A(root[:, 0:T], PS[:, 5, 0:T], ACT.Sqrt, bias=eps[:, 0:1], scale=1.0 / D).then_inc(ln_root, 1)
                for k in range(KD):
                    act.wait_ge(ln_scaled, k // 2 + 1)
                    A(cacc[:, k, :], cacc[:, k, :], ACT.Silu, bias=vcol("ln_b", k),
                      scale=vcol("ln_g", k)).then_inc(ln_silu, 1)

            def moe(l):
                norm(2 * l + 1)
                act.wait_ge(logits_done[l], 1)
                A(small[:, 0:2 * E], PS[:, 0, 0:2 * E], ACT.Sigmoid).then_inc(scores_ready[l], 1)
                for i in range(4):
                    t, half = divmod(i, 2)
                    act.wait_ge(htok_done[l], i + 1)
                    A(htok[:, t, half * 512:(half + 1) * 512], PS[:, 3 + i % 2, :],
                      ACT.Copy).then_inc(htok_stored[l], 1)
                for k in range(KD):
                    act.wait_ge(gather_done[l], k + 1)
                    A(hgT[:, k, 0:SLOTS], PS[:, 3 + k % 3, :], ACT.Copy).then_inc(gather_stored[l], 1)
                act.wait_ge(table_ready[l], 1)
                for primed in (silu_done, y_stored):
                    act.sem_inc(primed[l], 1)
                with act.Fori(0, E) as e:
                    first_slot = act.value_load(tab[0:1, l, bass.ds(e, 1)], min_val=0, max_val=SLOTS)
                    begin = act.value_load(tab[0:1, l, bass.ds(e + E, 1)], min_val=1, max_val=E * MAXCH + 1)
                    end = act.value_load(tab[0:1, l, bass.ds(e + 2 * E, 1)], min_val=1, max_val=E * MAXCH + 1)
                    with act.Fori(begin, end) as g:
                        act.wait_ge(gate_done[l], g)
                        act.wait_ge(act_ready[l], g)
                        A(sg[:], PS[:, 0, 0:KF * CHUNK].rearrange("p (m c) -> p m c", c=CHUNK),
                          ACT.Silu).then_inc(silu_done[l], 1)
                        act.wait_ge(down_done[l], g + 1)
                        s0 = nc.s_assert_within(
                            act.snap(first_slot + (g - begin) * CHUNK), 0, SLOTS,
                            skip_runtime_bounds_check_because="a chunk starts inside its expert's slots")
                        A(yT[:, :, bass.ds(s0, CHUNK)], PS[:, 2, :].rearrange("p (m c) -> p m c", c=CHUNK),
                          ACT.Copy).then_inc(y_stored[l], 1)
                for i in range(8):
                    s, half = divmod(i, 2)
                    act.wait_ge(ysl_done[l], i + 1)
                    A(ysl[:, s, half * 512:(half + 1) * 512], PS[:, 3 + i % 2, :],
                      ACT.Copy).then_inc(ysl_stored[l], 1)

            mixer0()
            moe(0)
            mixer1()
            moe(1)

        @block.gpsimd
        def _(pool):
            nc.gpsimd.memset(eps[:, 0:1], EPS).then_inc(eps_ready, 1)
            nc.gpsimd.memset(eps[:, 1:2], TWO_PI / 4).then_inc(eps_ready, 1)

        @block.vector
        def _(dve):
            v = nc.vector
            seq = [0]

            def step(ins):
                seq[0] += 1
                ins.then_inc(dve_seq, 1)
                dve.wait_ge(dve_seq, seq[0])

            def bc(ap, shape):
                return ap.to_broadcast(shape)

            def ada_store(a):
                l, j = divmod(a, 12)
                dve.wait_ge(ada_done, a + 1)
                v.tensor_tensor(mods[:, l, 4 * j:4 * j + 4], PS[:, 6 + a % 2, 0:4],
                                vcol("ada_b", 48 * l + 4 * j, 4), ALU.add).then_inc(ada_stored, 1)

            def mods_for(n):
                l, w = divmod(n, 2)
                dve.wait_ge(ada_stored, 12 * l + 6 * w + 4)
                v.scalar_tensor_tensor(out=gsc[:, n, :], in0=mods[:, l, 24 * w + 8:24 * w + 16], scalar=1.0,
                                       in1=vcol(("norm1", "norm2")[w], KD * l, KD), op0=ALU.add,
                                       op1=ALU.mult).then_inc(mods_ready, 1)

            def norm(n):
                dve.wait_ge(norm_root[n], 1)
                step(v.reciprocal(rstd[:, 0:T], root[:, 0:T]))
                for i in range(4):
                    ks = slice(2 * i, 2 * i + 2)
                    v.tensor_tensor(hT[:, ks, :], XT[:, ks, :], bc(rstd[:, 0:T].unsqueeze(1), [P, 2, T]),
                                    ALU.mult).then_inc(norm_scaled[n], 1)

            def residual(bank, k, gate):
                at = (k % 2) * T
                return v.scalar_tensor_tensor(out=XT[:, k, :], in0=PS[:, bank, at:at + T], scalar=gate,
                                              in1=XT[:, k, :], op0=ALU.mult, op1=ALU.add)

            def rope_tables():
                dve.wait_ge(pos_in, 16)
                dve.wait_ge(vec_in, 16)
                ang, n = ropetmp[:, 0, :], ropetmp[:, 1, :]
                step(v.tensor_copy(sin_t, posi))
                step(v.tensor_scalar(ang, sin_t, vcol("inv_freq"), None, ALU.mult))
                step(v.tensor_scalar(n, ang, 1.0 / TWO_PI, MAGIC, ALU.mult, ALU.add))
                step(v.tensor_scalar(n, n, MAGIC, None, ALU.subtract))
                for part in (PI_A, PI_B, PI_C):
                    step(v.scalar_tensor_tensor(out=ang, in0=n, scalar=-part, in1=ang, op0=ALU.mult, op1=ALU.add))
                step(v.tensor_scalar(ang, ang, 3.1415925, -3.1415925, ALU.min, ALU.max))
                v.tensor_copy(sin_t, ang).then_inc(angles, 1)
                step(v.tensor_scalar(n, ang, -1.0, None, ALU.mult))
                v.tensor_tensor(cos_t, ang, n, ALU.max).then_inc(angles, 1)

            def latents():
                dve.wait_ge(lat_stored, 5)
                dve.wait_ge(angles, 2)
                v.tensor_scalar(ropetmp[:, 1, :], latT[:, 8, :], vcol("gk_rope"), None,
                                ALU.mult).then_inc(kpe_scaled, 1)
                dve.wait_ge(lat_root, 2)
                step(v.reciprocal(rstd[:], root[:]))
                for m in list(range(KQ, KQ + KKV)) + list(range(KQ)):
                    g = vcol("q_norm", m) if m < KQ else vcol("kv_norm", m - KQ)
                    r = rstd[:, 0:T] if m < KQ else rstd[:, T:2 * T]
                    v.scalar_tensor_tensor(out=latT[:, m, :], in0=latT[:, m, :], scalar=g, in1=r, op0=ALU.mult,
                                           op1=ALU.mult).then_inc(lat_ready, 1)
                dve.wait_ge(tables, 2)
                dve.wait_ge(kpe_rot, 1)
                v.tensor_tensor(krope, PS[:, 4, 0:T], sin_t, ALU.mult)
                step(v.tensor_tensor(ropetmp[:, 0, :], ropetmp[:, 1, :], cos_t, ALU.mult))
                v.tensor_tensor(krope, krope, ropetmp[:, 0, :], ALU.add).then_inc(krope_ready, 1)
                dve.wait_ge(krope_ready, 1)

            def scale_k(g):
                dve.wait_ge(qk_root, g + 1)
                if g:
                    dve.wait_ge(qk_ready, g)
                v.reciprocal(rstd[:], root[:]).then_inc(qk_scaled_all, 1)
                dve.wait_ge(qk_scaled_all, g + 1)
                ks = kn[:, 2 * g:2 * g + 2, :]
                v.scalar_tensor_tensor(out=ks, in0=ks, scalar=vcol("gk_nope"),
                                       in1=rstd[:].rearrange("p (a t) -> p a t", t=T), op0=ALU.mult, op1=ALU.mult)
                v.tensor_tensor(kr[0:64, g, :], krope[0:64], rstd[0:64, 0:T], ALU.mult)
                v.tensor_tensor(kr[64:P, g, :], krope[64:P], rstd[64:P, T:2 * T], ALU.mult).then_inc(qk_ready, 1)

            def scale_q(g):
                n = PAIRS + g
                dve.wait_ge(qk_root, n + 1)
                dve.wait_ge(qk_ready, n)
                v.reciprocal(rstd[:], root[:]).then_inc(qk_scaled_all, 1)
                dve.wait_ge(qk_scaled_all, n + 1)
                for a, r in ((0, slice(0, 64)), (1, slice(64, P))):
                    ins = v.scalar_tensor_tensor(out=qr[r, g, :], in0=qr[r, g, :], scalar=V[r, VC["gq_rope"]:VC["gq_rope"] + 1],
                                                 in1=rstd[r, a * T:(a + 1) * T], op0=ALU.mult, op1=ALU.mult)
                ins.then_inc(qk_scaled, 1)
                qs = qn[:, 2 * g:2 * g + 2, :]
                v.scalar_tensor_tensor(out=qs, in0=qs, scalar=vcol("gq_nope"),
                                       in1=rstd[:].rearrange("p (a t) -> p a t", t=T), op0=ALU.mult, op1=ALU.mult)
                dve.wait_ge(qk_scaled, g + 1)
                v.tensor_tensor(ropetmp[:, 0, :], qr[:, g, :], cos_t, ALU.mult)
                dve.wait_ge(q_rot, g + 1)
                step(v.tensor_tensor(ropetmp[:, 1, :], PS[:, 2 + g % 2, 0:T], sin_t, ALU.mult))
                v.tensor_tensor(qr[:, g, :], ropetmp[:, 0, :], ropetmp[:, 1, :], ALU.add).then_inc(qk_ready, 1)

            def softmax(h):
                s, sm = attn_s[:, h % 2, :], attn_sm[:, h % 2, :]
                dve.wait_ge(s_done, h + 1)
                v.scalar_tensor_tensor(out=s, in0=PS[:, h % 2, 0:3 * P], scalar=SCALE, in1=con_("causal", 3 * P),
                                       op0=ALU.mult, op1=ALU.add).then_inc(s_masked, 1)
                dve.wait_ge(s_masked, h + 1)
                v.tensor_reduce(sm[:, 0:1], s[:, 0:P], AX, ALU.max)
                step(v.tensor_reduce(sm[:, 1:2], s[:, P:3 * P], AX, ALU.max))
                v.tensor_scalar(sm[:, 2:4], sm[:, 0:2], -1.0, None, ALU.mult).then_inc(s_max, 1)
                dve.wait_ge(p_exp, 2 * h + 2)
                step(v.reciprocal(sm[:, 6:8], sm[:, 4:6]))
                p = attn_p[:, h % 2, :]
                v.tensor_scalar(p[:, 0:P], p[:, 0:P], sm[:, 6:7], None, ALU.mult)
                v.tensor_scalar(p[:, P:3 * P], p[:, P:3 * P], sm[:, 7:8], None, ALU.mult).then_inc(p_ready, 1)

            def mixer0():
                rope_tables()
                for a in range(4):
                    ada_store(a)
                mods_for(0)
                norm(0)
                dve.wait_ge(con_in, 16)
                dve.wait_ge(rb_in, 16)
                latents()
                for g in range(PAIRS):
                    scale_k(g)
                for g in range(PAIRS):
                    scale_q(g)
                for h in range(HEADS):
                    softmax(h)
                    if h < 7:
                        ada_store(4 + 2 * h)
                        ada_store(5 + 2 * h)
                mods_for(1)
                mods_for(2)
                for k in range(KD):
                    dve.wait_ge(wo_done, k // 2 + 1)
                    residual(k // 2, k, mods[:, 0, 16 + k:17 + k]).then_inc(resid, 1)

            def mixer1():
                step(v.memset(upad[:, :, 0:PADL], 0.0))
                norm(2)
                for c in range(KD):
                    dve.wait_ge(glu_sig, c + 1)
                    v.scalar_tensor_tensor(out=upad[:, c, PADL:], in0=PS[:, c % 2, 0:T], scalar=vcol("pw1_b", c),
                                           in1=sig[:, c % 2, :], op0=ALU.add, op1=ALU.mult).then_inc(glu_ready, 1)
                    dve.wait_ge(glu_ready, c + 1)
                    step(v.tensor_scalar(cacc[:, c, :], upad[:, c, 0:T], vcol("dw_w", c * TAPS), vcol("dw_b", c),
                                         ALU.mult, ALU.add))
                    for j in range(1, TAPS):
                        ins = v.scalar_tensor_tensor(out=cacc[:, c, :], in0=upad[:, c, j:j + T],
                                                     scalar=vcol("dw_w", c * TAPS + j), in1=cacc[:, c, :],
                                                     op0=ALU.mult, op1=ALU.add)
                        if j < TAPS - 1:
                            step(ins)
                    ins.then_inc(conv_ready, 1)
                for a in range(NA_PRE, 24):
                    ada_store(a)
                mods_for(3)
                gb = small_gb
                step(v.tensor_tensor(gb, mods[:, 1, 16:24], vcol("pw2_b", 0, KD), ALU.mult))
                for k in range(KD):
                    v.tensor_scalar(XT[:, k, :], XT[:, k, :], gb[:, k:k + 1], None, ALU.add).then_inc(dve_seq, 1)
                    seq[0] += 1
                dve.wait_ge(ln_mean, 1)
                for i in range(4):
                    ks = slice(2 * i, 2 * i + 2)
                    v.tensor_tensor(cacc[:, ks, :], cacc[:, ks, :], bc(rstd[:, T:2 * T].unsqueeze(1), [P, 2, T]),
                                    ALU.subtract).then_inc(ln_centred, 1)
                dve.wait_ge(ln_root, 1)
                step(v.reciprocal(rstd[:, 0:T], root[:, 0:T]))
                for i in range(4):
                    ks = slice(2 * i, 2 * i + 2)
                    v.tensor_tensor(cacc[:, ks, :], cacc[:, ks, :], bc(rstd[:, 0:T].unsqueeze(1), [P, 2, T]),
                                    ALU.mult).then_inc(ln_scaled, 1)
                for k in range(KD):
                    dve.wait_ge(pw2_done, k // 2 + 1)
                    residual(k // 2, k, mods[:, 1, 16 + k:17 + k]).then_inc(resid, 1)

            def route(l):
                def buf(at, *shape):
                    n = 1
                    for s_ in shape:
                        n *= s_
                    b = small[:, at:at + n]
                    return b if len(shape) == 1 else b.rearrange("p (a b) -> p a b", b=shape[1])
                G8 = NT * GRP
                score, biased = buf(0, NT, E), buf(32, NT, E)
                b4 = buf(32, G8, PER)
                dve.wait_ge(scores_ready[l], 1)
                step(v.tensor_tensor(biased, score, bc(rb[:].unsqueeze(1), [P, NT, E]), ALU.add))
                hi, lo = buf(64, G8, 2), buf(80, G8, 2)
                v.tensor_tensor(hi, b4[:, :, 0::2], b4[:, :, 1::2], ALU.max)
                step(v.tensor_tensor(lo, b4[:, :, 0::2], b4[:, :, 1::2], ALU.min))
                top1, t2a, t2b, gs = buf(96, G8), buf(104, G8), buf(112, G8), buf(120, G8)
                v.tensor_tensor(top1, hi[:, :, 0], hi[:, :, 1], ALU.max)
                v.tensor_tensor(t2a, hi[:, :, 0], hi[:, :, 1], ALU.min)
                step(v.tensor_tensor(t2b, lo[:, :, 0], lo[:, :, 1], ALU.max))
                step(v.tensor_tensor(t2a, t2a, t2b, ALU.max))
                step(v.tensor_tensor(gs, top1, t2a, ALU.add))
                gs2, gmax, eq, eqi = buf(120, NT, GRP), buf(128, NT), buf(136, NT, GRP), buf(144, NT, GRP)
                step(v.tensor_reduce(gmax, gs2, AX, ALU.max))
                step(v.tensor_tensor(eq, gs2, bc(gmax.unsqueeze(2), [P, NT, GRP]), ALU.is_equal))
                step(v.tensor_tensor(eqi, eq, con_("first4", 2 * GRP).rearrange("p (a b) -> p a b", b=GRP), ALU.mult))
                step(v.tensor_reduce(gmax, eqi, AX, ALU.max))
                step(v.tensor_tensor(eq, eqi, bc(gmax.unsqueeze(2), [P, NT, GRP]), ALU.is_equal))
                gt = small[:, 768:768 + G8 * 16].rearrange("p (g i j) -> p g i j", i=PER, j=PER)
                et = small[:, 896:896 + G8 * 16].rearrange("p (g i j) -> p g i j", i=PER, j=PER)
                vj = bc(b4.unsqueeze(2), [P, G8, PER, PER])
                vi = bc(b4.unsqueeze(3), [P, G8, PER, PER])
                v.tensor_tensor(gt, vj, vi, ALU.is_gt)
                step(v.tensor_tensor(et, vj, vi, ALU.is_equal))
                step(v.tensor_tensor(et.rearrange("p g i j -> p g (i j)"), et.rearrange("p g i j -> p g (i j)"),
                                     bc(con_("tri4", 16).unsqueeze(1), [P, G8, 16]), ALU.mult))
                step(v.tensor_tensor(gt, gt, et, ALU.add))
                rank = buf(160, G8, PER)
                step(v.tensor_reduce(rank, gt, AX, ALU.add))
                picks = buf(256, NT, E)
                p4 = buf(256, G8, PER)
                step(v.tensor_scalar(rank, rank, 1.5, None, ALU.is_lt))
                v.tensor_tensor(p4, rank, bc(buf(136, G8).unsqueeze(2), [P, G8, PER]),
                                ALU.mult).then_inc(picks_ready[l], 1)
                dve.wait_ge(picks_ready[l], 1)
                w, ws = buf(288, NT, E), buf(320, NT)
                step(v.tensor_tensor(w, score, picks, ALU.mult))
                step(v.tensor_reduce(ws, w, AX, ALU.add))
                step(v.reciprocal(ws, ws))
                step(v.tensor_tensor(w, w, bc(ws.unsqueeze(2), [P, NT, E]), ALU.mult))
                dve.wait_ge(counts_done[l], 1)
                c16, n16 = small[0:E, 512:512 + P], small[0:E, 640:640 + P]
                cum = buf(336, NT, E)
                v.tensor_copy(cum, PS[:, 1, 0:2 * E].rearrange("p (t e) -> p t e", e=E))
                step(v.tensor_copy(c16, PS[0:E, 1, 64:64 + P]))
                step(v.tensor_scalar(n16, c16, CHUNK + 0.5, 1.0, ALU.is_gt, ALU.add))
                for i in range(2, MAXCH):
                    ins = v.scalar_tensor_tensor(out=n16, in0=c16, scalar=i * CHUNK + 0.5, in1=n16, op0=ALU.is_gt,
                                                 op1=ALU.add)
                    if i < MAXCH - 1:
                        step(ins)
                ins.then_inc(count_rows[l], 1)
                dve.wait_ge(offs_done[l], 1)
                v.tensor_copy(tab[0:1, l, 0:E], PS[0:1, 2, 0:E])
                v.tensor_scalar(tab[0:1, l, E:3 * E], PS[0:1, 2, E:3 * E], 1.0, None,
                                ALU.add).then_inc(table_ready[l], 1)
                pm = buf(368, NT, E)
                step(v.tensor_tensor(pm, cum, bc(PS[:, 2, 0:E].unsqueeze(1), [P, NT, E]), ALU.add))
                step(v.scalar_tensor_tensor(out=pm, in0=pm, scalar=1.0, in1=picks, op0=ALU.add, op1=ALU.mult))
                sa, sb_, wa, wb = buf(400, NT), buf(404, NT), buf(408, NT), buf(412, NT)
                v.tensor_reduce(sa, pm, AX, ALU.max)
                step(v.tensor_reduce(sb_, pm, AX, ALU.add))
                step(v.tensor_tensor(sb_, sb_, sa, ALU.subtract))
                iota = con_("iota", SLOTS)
                for t in range(NT):
                    step(v.tensor_scalar(perm[:, t, :], iota, sa[:, t:t + 1], None, ALU.is_equal))
                    v.scalar_tensor_tensor(out=perm[:, t, :], in0=iota, scalar=sb_[:, t:t + 1], in1=perm[:, t, :],
                                           op0=ALU.is_equal, op1=ALU.add).then_inc(perm_ready[l], 1)
                m = buf(416, NT, E)
                for s_, w_ in ((sa, wa), (sb_, wb)):
                    step(v.tensor_tensor(m, pm, bc(s_.unsqueeze(2), [P, NT, E]), ALU.is_equal))
                    step(v.tensor_tensor(m, m, w, ALU.mult))
                    step(v.tensor_reduce(w_, m, AX, ALU.add))
                for t in range(NT):
                    tmp = small[:, 1024 + t * SLOTS:1024 + (t + 1) * SLOTS]
                    v.tensor_scalar(wperm[:, t, :], iota, sa[:, t:t + 1], wa[:, t:t + 1], ALU.is_equal, ALU.mult)
                    step(v.tensor_scalar(tmp, iota, sb_[:, t:t + 1], wb[:, t:t + 1], ALU.is_equal, ALU.mult))
                    v.tensor_tensor(wperm[:, t, :], wperm[:, t, :], tmp, ALU.add).then_inc(wperm_ready[l], 1)

            def moe(l):
                norm(2 * l + 1)
                route(l)
                dve.wait_ge(norm_sum[2 * l + 1], 1)
                step(v.memset(hgT[:, :, SLOTS:], 0.0))
                for i in range(2):
                    dve.wait_ge(wpt_done[l], i + 1)
                    v.tensor_copy(wpT[:, 2 * i:2 * i + 2, :], PS[:, i, :].rearrange("p (s t) -> p s t", t=T)
                                  ).then_inc(wpt_stored[l], 1)
                dve.wait_ge(gather_stored[l], KD)
                for primed in (act_ready,):
                    dve.sem_inc(primed[l], 1)
                with dve.Fori(0, E) as e:
                    first_slot = dve.value_load(tab[0:1, l, bass.ds(e, 1)], min_val=0, max_val=SLOTS)
                    begin = dve.value_load(tab[0:1, l, bass.ds(e + E, 1)], min_val=1, max_val=E * MAXCH + 1)
                    end = dve.value_load(tab[0:1, l, bass.ds(e + 2 * E, 1)], min_val=1, max_val=E * MAXCH + 1)
                    with dve.Fori(begin, end) as g:
                        s0 = nc.s_assert_within(
                            dve.snap(first_slot + (g - begin) * CHUNK), 0, SLOTS,
                            skip_runtime_bounds_check_because="a chunk starts inside its expert's slots")
                        dve.wait_ge(up_done[l], g)
                        v.tensor_copy(hc[:], hgT[:, :, bass.ds(s0, CHUNK)]).then_inc(hc_ready[l], 1)
                        dve.wait_ge(silu_done[l], g + 1)
                        dve.wait_ge(up_done[l], g + 1)
                        dve.wait_ge(down_done[l], g)
                        v.tensor_tensor(aT[:], PS[:, 1, 0:KF * CHUNK].rearrange("p (m c) -> p m c", c=CHUNK), sg[:],
                                        ALU.mult).then_inc(act_ready[l], 1)
                banks = (5, 0, 1, 2)
                for k in range(KD):
                    dve.wait_ge(moe_done[l], k // 2 + 1)
                    residual(banks[k // 2], k, mods[:, l, 40 + k:41 + k]).then_inc(resid, 1)

            mixer0()
            moe(0)
            mixer1()
            moe(1)


def kernel(**inputs):
    import numpy as np
    import concourse.bacc as bacc
    from concourse.bass_utils import run_bass_kernel_spmd

    f = {k: np.asarray(a) for k, a in inputs.items()}

    def cols(a):
        return a.reshape(-1, P).T

    def rope2(a):
        return np.concatenate([a, a]).reshape(P, 1)

    half = ROPE // 2
    inv_freq = (1.0 / (10000.0 ** (np.arange(half, dtype=np.float32) * np.float32(2.0 / ROPE)))).astype(np.float32)
    dw = f["conv_dw_w"][0]
    vec = np.concatenate([
        cols(f["norm1_g"]), cols(f["norm2_g"]), cols(f["ada_b"]), cols(f["mla_q_norm_g"]), cols(f["mla_kv_norm_g"]),
        f["mla_qk_q_g"][0, :NOPE].reshape(P, 1), f["mla_qk_k_g"][0, :NOPE].reshape(P, 1),
        rope2(f["mla_qk_q_g"][0, NOPE:]), rope2(f["mla_qk_k_g"][0, NOPE:]),
        np.tile(inv_freq, 4).reshape(P, 1),
        cols(f["conv_pw1_b"]), cols(f["conv_dw_b"]), cols(f["conv_ln_g"]), cols(f["conv_ln_b"]),
        cols(f["conv_pw2_b"]), cols(f["c"]),
        dw.T.reshape(KD, P, TAPS).transpose(1, 0, 2).reshape(P, KD * TAPS),
        f["router_w"].reshape(KD, P, E).transpose(1, 0, 2).reshape(P, KD * E),
    ], axis=1)
    i = np.arange(P)
    causal = np.where(i[None, :] <= i[:, None], 0.0, -1e30)
    rot1 = np.zeros((ROPE, ROPE))
    for a in range(half):
        rot1[a + half, a] = -1.0
        rot1[a, a + half] = 1.0
    rot = np.zeros((P, P))
    rot[:ROPE, :ROPE] = rot1
    rot[ROPE:, ROPE:] = rot1
    e = np.arange(P)[:, None]
    tri16 = np.concatenate([e < np.arange(E)[None, :], e <= np.arange(E)[None, :]], axis=1)
    tri4 = (np.arange(PER)[None, :] < np.arange(PER)[:, None]).astype(np.float32).reshape(1, -1)
    con = np.concatenate([
        np.eye(P), np.ones((P, P)), i[:, None] < i[None, :],
        np.concatenate([causal, np.zeros((P, P)), causal], axis=1), rot,
        np.tile((i < ROPE)[:, None], (1, P)), np.tile((i >= ROPE)[:, None], (1, P)),
        np.tile(np.arange(1, SLOTS + 1)[None, :], (P, 1)), tri16,
        np.tile(np.array([4, 3, 2, 1, 4, 3, 2, 1])[None, :], (P, 1)), np.tile(tri4, (P, 1)),
    ], axis=1).astype(np.float32)
    uq = f["mla_w_uq"][0].reshape(QR, HEADS, QK)
    arrays = {
        "xT": f["x"][0].T.reshape(KD, P, T).transpose(1, 0, 2),
        "vec": vec,
        "con": con,
        "rbias": np.tile(f["router_bias"][None, :], (P, 1)),
        "pos": np.tile(f["positions"], (P, 1)),
        "ada_w": f["ada_w"],
        "w_dqkv": f["mla_w_dqkv"][0],
        "w_uq": np.concatenate([uq[:, :, :NOPE].reshape(QR, -1), uq[:, :, NOPE:].reshape(QR, -1)], axis=1),
        "w_ukv": f["mla_w_ukv"][0],
        "w_o": f["mla_w_o"][0],
        "pw1": f["conv_pw1_w"][0],
        "pw2": f["conv_pw2_w"][0],
        "w_gate": f["moe_w_gate"],
        "w_up": f["moe_w_up"],
        "w_down": f["moe_w_down"],
    }
    nc = bacc.Bacc("TRN2", target_bir_lowering=False, num_devices=1)
    args = []
    for name in arrays:
        arrays[name] = np.ascontiguousarray(arrays[name])
        args.append(nc.dram_tensor(name, arrays[name].shape, mybir.dt.from_np(arrays[name].dtype),
                                   kind="ExternalInput").ap())
    out = nc.dram_tensor("out", (P, KD, T), F32, kind="ExternalOutput").ap()
    build(nc, *args, out)
    r = run_bass_kernel_spmd(nc, [arrays], core_ids=[0])
    o = r.results[0]["out"]
    return np.ascontiguousarray(o.transpose(1, 0, 2).reshape(D, T).T).reshape(1, T, D)
```

```python
from contextlib import ExitStack

import concourse.bass as bass
from concourse import mybir

P = 128
D = 1024
T = 256
KD = D // P
NT = T // P
HEADS = 8
PAIRS = HEADS // 2
NOPE = 128
ROPE = 64
QK = NOPE + ROPE
VD = 128
QR = 768
KVR = 256
KQ = QR // P
KKV = KVR // P
TAPS = 31
PADL = TAPS - 1
E = 16
GRP = 4
PER = E // GRP
FF = 512
KF = FF // P
SLOTS = 2 * T
SB = SLOTS // P
EPS = 1e-6
SCALE = float(QK) ** -0.5

RING = 3
SLOT_F = KD * 576
PIECE = 2048
PBUF = 3
MAXB = E + 3
NTAB = 2 * MAXB + 2
NWORK = 14864
PE_TAPS = 10

VC = {}
_at = 0
for _name, _n in (("norm1", 2 * KD), ("norm2", 2 * KD), ("ada_b", 2 * 48), ("q_norm", KQ), ("kv_norm", KKV),
                  ("gq_nope", 1), ("gk_nope", 1), ("gq_rope", 1), ("gk_rope", 1), ("inv_freq", 1),
                  ("pw1_b", 2 * KD), ("dw_b", KD), ("ln_g", KD), ("ln_b", KD), ("pw2_b", KD), ("c", KD),
                  ("dw_w", KD * TAPS), ("router_w", KD * E)):
    VC[_name] = _at
    _at += _n
NVEC = _at

CC = {}
_at = 0
for _name, _n in (("ident", P), ("ones", P), ("before", P), ("causal", 3 * P), ("rot", P), ("iota", SLOTS),
                  ("hsel", HEADS * HEADS), ("kpesel", HEADS), ("psel", PAIRS * HEADS),
                  ("tri16", 2 * E), ("first4", 2 * GRP), ("tri4", PER * PER)):
    CC[_name] = _at
    _at += _n
NCON = _at

ALU = mybir.AluOpType
ACT = mybir.ActivationFunctionType
AX = mybir.AxisListType.X
F32 = mybir.dt.float32
I32 = mybir.dt.int32
F32R = mybir.dt.float32r

TWO_PI = 6.283185307179586
PI_A = 6.28125
PI_B = 0.0019350051879882812
PI_C = TWO_PI - PI_A - PI_B
MAGIC = 12582912.0

NA_PRE = 18
POOL_ADA = [5, 8, 11, 14, 17, 19, 22]
ADA_ORDER = ([4, 6, 7, 5, 9, 10, 8, 12, 13, 11, 15, 16, 14, 17], [18, 20, 21, 19, 23, 22])
ADA_ALL = [0, 1, 2, 3] + ADA_ORDER[0] + ADA_ORDER[1]


def ada_acc_id(a):
    return (a < 4, a % 2)


def pieces_of(u):
    return 3 if u == ("dqkv", 1) else 2


def unit_plan():
    first = [("ada", j) for j in range(4)] + [("dqkv", 0), ("dqkv", 1), ("ukv", 0)]
    first += [("uq", i) for i in range(3)] + [("ada", j) for j in range(4, NA_PRE)] + [("wo", 0), ("wo", 1)]
    second = [("pw1", i) for i in range(4)] + [("ada", j) for j in range(NA_PRE, 24)] + [("pw2", 0), ("pw2", 1)]
    return first, second


def build(nc, xT, vec, con, rbias, pos, ada_w, w_dqkv, w_uq, w_ukv, w_o, pw1, pw2, w_gate, w_up, w_down, out):
    ctx = ExitStack()
    with ctx:
        def sb(name, shape, dt=F32):
            return ctx.enter_context(nc.sbuf_tensor(name, shape, dt))

        def sem(name):
            return ctx.enter_context(nc.semaphore(name))

        PS = ctx.enter_context(nc.psum_tensor("ps", [P, 8, 512], F32))
        ring = [sb(f"ring{s}", [P, SLOT_F]) for s in range(RING)]
        piece_hi = [sb(f"piece_hi{s}", [P, PIECE], F32R) for s in range(PBUF)]
        piece_lo = [sb(f"piece_lo{s}", [P, PIECE], F32R) for s in range(PBUF)]
        RX = sb("acts_split", [P, 2 * KD * T], F32R)
        XT = sb("XT", [P, KD, T])
        hT = sb("hT", [P, KD, T])
        V = sb("vecs", [P, NVEC])
        C = sb("consts", [P, NCON])
        rb = sb("router_bias", [P, E])
        mods = sb("mods", [P, 2, 48])
        gsc = sb("norm_gain", [P, 4, KD])
        sc = sb("silu_c", [P, KD])
        rstd = sb("rstd", [P, 512])
        root = sb("root", [P, 512])
        eps = sb("eps", [P, 2])
        tab = sb("block_table", [1, 2, NTAB], I32)
        WORK = sb("work", [P, NWORK])

        def view(at, *shape, of=None):
            n = 1
            for s in shape:
                n *= s
            v = (WORK if of is None else of)[:, at:at + n]
            if len(shape) == 2:
                v = v.rearrange("p (a b) -> p a b", b=shape[1])
            if len(shape) == 3:
                v = v.rearrange("p (a b c) -> p a b c", b=shape[1], c=shape[2])
            return v

        xh, xl = view(0, KD, T, of=RX), view(KD * T, KD, T, of=RX)
        sq = view(0, KD, T)
        sq_rope = view(2048, PAIRS, T)
        kpe_sq = view(2048, T)
        latT = view(3072, 9, T)
        kn = view(5376, HEADS, T)
        kr = view(7424, PAIRS, T)
        vt = view(8448, NT, HEADS * VD)
        qn = view(10496, HEADS, T)
        qr = view(12544, PAIRS, T)
        sin_t, cos_t = view(13568, T), view(13824, T)
        ropetmp = view(14080, 2, T)
        krope = view(14592, T)
        posi = krope.bitcast(I32)
        kq_rstd = view(14848, 16)
        attn_s = view(0, 2, 3 * P)
        attn_p = view(768, 2, 3 * P)
        attn_pt = view(1536, 2, 3 * P)
        attn_sm = view(2304, 2, 8)
        hgT = view(0, KD, SLOTS + P)
        yT = view(5120, KD, SLOTS + P)
        small = view(5120, 2048)
        wperm = view(7168, NT, SLOTS)
        ysl = view(0, SB, D)
        wpT = view(10240, SB, T)
        sg = view(11264, FF)
        act = view(11776, FF)
        yb = view(12288, D)
        perm = view(0, NT, SLOTS, of=piece_hi[PBUF - 1])
        hch, hcl = view(0, KD, P, of=RX), view(KD * P, KD, P, of=RX)
        aTh, aTl = view(2048, KF, P, of=RX), view(2560, KF, P, of=RX)
        htokh, htokl = view(0, NT, D, of=RX), view(2048, NT, D, of=RX)
        upad = view(2048, KD, PADL + T)
        cacc = view(4352, KD, T)
        sig = view(6400, 4, T)
        diag = view(7424, 2, PE_TAPS, P)
        gate_bias = view(9984, KD)
        hflat = hT[:].rearrange("p k t -> p (k t)")

        def ada_acc(a):
            if a < 4:
                return WORK[:, 10496 + 512 * (a % 2):10496 + 512 * (a % 2) + 512]
            if a in POOL_ADA:
                return hflat[:, 1024:1536]
            return hflat[:, 512 * (a % 2):512 * (a % 2) + 512]

        def vcol(name, i=0, n=1):
            return V[:, VC[name] + i:VC[name] + i + n]

        def con_(name, n=P, at=0, rows=P):
            return C[0:rows, CC[name] + at:CC[name] + at + n]

        ident, ones = con_("ident"), con_("ones")
        LT = range(2)

        def sems(names, times=None):
            names = names.split()
            return [sem(n) if times is None else [sem(f"{n}{i}") for i in range(times)] for n in names]

        x_in, vec_in, con_in, rb_in, pos_in = sems("x_in vec_in con_in rb_in pos_in")
        landed = [[sem(f"landed{ph}_{s}") for s in range(RING)] for ph in range(4)]
        hi_ready, lo_ready, piece_used = sems("hi_ready lo_ready piece_used", 4)
        raw_used, pool_used = sems("raw_used pool_used", 2)
        ada_summed, ada_pooled = sems("ada_summed ada_pooled")
        silu_c, ada_done, ada_stored, mods_ready = sems("silu_c ada_done ada_stored mods_ready")
        dve_seq, pool_seq, eps_ready = sems("dve_seq pool_seq eps_ready")
        resid = sem("residual_updated")
        norm_sq, norm_sum, norm_root, norm_scaled, h_ready, xh_ready, xl_ready = sems(
            "norm_sq norm_sum norm_root norm_scaled h_ready xh_ready xl_ready")
        angles, tables = sems("rope_angles rope_tables")
        item_done, item_stored = sems("item_done item_stored")
        lat_sum, lat_root, lat_ready, lath_ready, latl_ready = sems("lat_sum lat_root lat_ready lath_ready latl_ready")
        kpe_scaled, kpe_rot, krope_ready = sems("kpe_scaled kpe_rot krope_ready")
        k_sum, k_root, k_recip, bc_done, bc_used = sems("k_sum k_root k_recip bc_done bc_used")
        q_sum, q_root, q_recip, q_turned, rq_ready, q_rot, q_ready = sems(
            "q_sum q_root q_recip q_turned rq_ready q_rot q_ready")
        s_done, s_masked, s_max, p_exp, p_ready, pt_done, pt_stored, o_done, oh_ready, ol_ready = sems(
            "s_done s_masked s_max p_exp p_ready pt_done pt_stored o_done oh_ready ol_ready")
        proj_done = sems("wo_done pw2_done")
        glu_done, glu_sig, glu_ready, diag_ready, conv_pe, conv_ready = sems(
            "glu_done glu_sig glu_ready diag_ready conv_pe conv_ready")
        ln_sum, ln_mean, ln_centred, ln_sq, ln_var, ln_root, ln_scaled, ln_silu = sems(
            "ln_sum ln_mean ln_centred ln_sq ln_var ln_root ln_scaled ln_silu")
        logits_done, scores_ready, picks_ready, counts_done, count_rows, offs_done, slots_ready, rows_done, table_ready = sems(
            "logits_done scores_ready picks_ready counts_done count_rows offs_done slots_ready rows_done table_ready")
        htok_done, htokh_ready, htokl_ready, perm_ready, wperm_ready, gather_done, gather_stored, wpt_done, wpt_stored = sems(
            "htok_done htokh_ready htokl_ready perm_ready wperm_ready gather_done gather_stored wpt_done wpt_stored")
        hch_ready, hcl_ready, silu_done, act_ready, att_done, ath_ready, atl_ready = sems(
            "hch_ready hcl_ready silu_done act_ready att_done ath_ready atl_ready", 2)
        y_stored, ytt_done, yta_stored, ytd_stored = sems("y_stored ytt_done yta_stored ytd_stored", 2)
        ysl_done, ysl_stored, moe_done = sems("ysl_done ysl_stored moe_done")
        stored = sem("out_stored")

        units = unit_plan()
        at_of = {u: n for ph in (0, 1) for n, u in enumerate(units[ph])}
        pieces = [[(u, i) for u in units[ph] if u[0] != "ada" for i in range(pieces_of(u))] for ph in (0, 1)]

        def unit_shape(kind, i):
            if kind == "dqkv":
                return (KD, (512, 576)[i])
            return {"ada": (KD, 512), "ukv": (2, 2048), "uq": (KQ, 512), "wo": (KD, 512), "pw1": (KD, 512),
                    "pw2": (KD, 512)}[kind]

        def unit_ap(kind, i):
            k, n = unit_shape(kind, i)
            return ring[at_of[(kind, i)] % RING][:, 0:k * n].rearrange("p (k n) -> p k n", n=n)

        def unit_source(kind, i):
            if kind == "ada":
                l, j = divmod(i, 12)
                return ada_w[l].rearrange("(k p) n -> p k n", p=P)[:, :, j * 512:(j + 1) * 512]
            w = {"dqkv": w_dqkv, "ukv": w_ukv, "uq": w_uq, "wo": w_o, "pw1": pw1, "pw2": pw2}[kind]
            w = w.rearrange("(k p) n -> p k n", p=P)
            n = unit_shape(kind, i)[1]
            return w[:, :, 512 * i:512 * i + n]

        def piece_cols(kind, i, j):
            if kind == "dqkv" and i == 1:
                return (0, 256), (256, 512), (512, 576)
            return {"ukv": ((0, 1024), (1024, 2048))}.get(kind, ((0, 256), (256, 512)))

        def piece_raw(kind, i, j):
            a, b = piece_cols(kind, i, j)[j]
            return unit_ap(kind, i)[:, :, a:b]

        def piece_bufs(n, k, w):
            return tuple(x[n % PBUF][:, 0:k * w].rearrange("p (k n) -> p k n", n=w) for x in (piece_hi, piece_lo))

        def mixer_piece(mx, n):
            (kind, i), j = pieces[mx][n]
            raw = piece_raw(kind, i, j)
            if raw.shape[2] == ROPE:
                raw = raw.unsqueeze(2).to_broadcast([P, KD, 2, ROPE])
                hi, lo = (x.rearrange("p k (a n) -> p k a n", n=ROPE) for x in piece_bufs(n, KD, P))
            else:
                hi, lo = piece_bufs(n, raw.shape[1], raw.shape[2])
            return raw, hi, lo, (kind, i), j

        def moe_piece(i):
            u, j = divmod(i, 2)
            if u < 2:
                raw = ring[u][:, 0:KD * FF].rearrange("p (k n) -> p k n", n=FF)[:, 4 * j:4 * j + 4, :]
            else:
                raw = ring[u][:, 0:KF * D].rearrange("p (k n) -> p k n", n=D)[:, :, 512 * j:512 * j + 512]
            hi, lo = piece_bufs(i, 4, 512)
            return raw, hi, lo

        expert_w = (w_gate, w_up, w_down)
        WHY = "computed from at most 512 picks of 16 experts"

        def inner_blocks(eng, l):
            return nc.s_assert_within(eng.value_load(tab[0:1, l, 0:1], min_val=E - 2, max_val=MAXB - 2), E - 2,
                                      MAXB - 2, skip_runtime_bounds_check_because=WHY)

        def nth(j, per=1, more=0):
            r, o = j
            if r is None:
                return per * o + more
            return (r * per if per > 1 else r) + (per * o + more)

        def after(j, n=1):
            return (j[0], j[1] + n)

        def block_slot(eng, l, j):
            return eng.value_load(tab[0:1, l, bass.ds(nth(j) + (MAXB + 1), 1)] if j[0] is not None else
                                  tab[0:1, l, j[1] + MAXB + 1:j[1] + MAXB + 2], min_val=0, max_val=SLOTS)

        block = ctx.enter_context(nc.Block())

        @block.sync
        def _(sp):
            def wait_consumed(mx, n):
                ph = 2 * mx
                us = units[mx]
                if us[n][0] == "ada" and us[n][1] in POOL_ADA:
                    sp.wait_ge(pool_used[mx], sum(u[0] == "ada" and u[1] in POOL_ADA for u in us[:n + 1]))
                else:
                    sp.wait_ge(raw_used[mx], sum(not (u[0] == "ada" and u[1] in POOL_ADA) for u in us[:n + 1]))

            def mixer_units(mx):
                ph = 2 * mx
                if mx:
                    inner = inner_blocks(sp, 0)
                for n, (kind, i) in enumerate(units[mx]):
                    s = n % RING
                    if n >= RING:
                        wait_consumed(mx, n - RING)
                    elif mx:
                        sp.wait_ge(lo_ready[1], nth((inner, 2), 6, 2 * s - 4))
                    if kind == "pw1":
                        src = pw1.rearrange("(k p) (h n) -> h p k n", p=P, h=2)[:, :, :, 256 * i:256 * i + 256]
                        for half in range(2):
                            sp.dma_start(unit_ap(kind, i)[:, :, 256 * half:256 * half + 256],
                                         src[half]).then_inc(landed[ph][s], 16)
                    else:
                        sp.dma_start(unit_ap(kind, i), unit_source(kind, i)).then_inc(landed[ph][s], 16)

            def expert_unit(l, e, i):
                src = expert_w[i][l].rearrange("e (k p) n -> e p k n", p=P)
                src = src[bass.ds(e, 1)].rearrange("e p k n -> (e p) k n") if not isinstance(e, int) else src[e]
                k, n = (KD, FF) if i < 2 else (KF, D)
                sp.dma_start(ring[i][:, 0:k * n].rearrange("p (k n) -> p k n", n=n),
                             src).then_inc(landed[2 * l + 1][i], 16)

            def moe_units(l):
                last = len(units[l])
                for i in range(RING):
                    wait_consumed(l, max(n for n in range(last) if n % RING == i))
                    expert_unit(l, 0, i)
                sp.wait_ge(table_ready, l + 1)
                with sp.Fori(0, inner_blocks(sp, l) + 1) as r:
                    e = sp.value_load(tab[0:1, l, bass.ds(r + 2, 1)], min_val=0, max_val=E - 1)
                    for i in range(3):
                        sp.wait_ge(lo_ready[2 * l + 1], nth((r, 1), 6, 2 * i + 2 - 6))
                        expert_unit(l, e, i)

            mixer_units(0)
            moe_units(0)
            mixer_units(1)
            moe_units(1)
            for k in range(0, KD, 2):
                sp.wait_ge(resid, 3 * KD + k + 2)
                sp.dma_start(out[:, k:k + 2, :], XT[:, k:k + 2, :]).then_inc(stored, 16)
            sp.wait_ge(stored, 16 * (KD // 2))

        def wait_unit(eng, mx, u):
            n = at_of[u]
            per = [2 if v[0] == "pw1" else 1 for v in units[mx]]
            count = sum(per[m] for m in range(n + 1) if m % RING == n % RING)
            eng.wait_ge(landed[2 * mx][n % RING], 16 * count)

        @block.tensor
        def _(pe):
            mm = nc.tensor.matmul
            tr = nc.tensor.transpose

            def mm3(dst, lhs, rhs, start, stop):
                mm(dst, lhs[0], rhs[0], start=start, stop=False)
                mm(dst, lhs[1], rhs[0], start=False, stop=False)
                return mm(dst, lhs[0], rhs[1], start=False, stop=stop)

            ada_n = [0]

            def ada(a):
                if a in POOL_ADA:
                    pe.wait_ge(ada_pooled, POOL_ADA.index(a) + 1)
                else:
                    pe.wait_ge(ada_summed, sum(b not in POOL_ADA for b in range(a + 1)))
                if ada_n[0]:
                    pe.wait_ge(ada_stored, ada_n[0])
                for m in range(4):
                    ins = mm(PS[:, 7, m:m + 1], ada_acc(a)[:, m * P:(m + 1) * P], ones[:, 0:1], start=True, stop=True)
                ins.then_inc(ada_done, 1)
                ada_n[0] += 1

            def norm_sums(n):
                for i in range(4):
                    pe.wait_ge(norm_sq, 4 * n + i + 1)
                    for k in (2 * i, 2 * i + 1):
                        ins = mm(PS[:, 4, 0:T], ones, sq[:, k, :], start=(k == 0), stop=(k == KD - 1))
                ins.then_inc(norm_sum, 1)

            item = [0]

            def item_bank():
                n = item[0]
                item[0] += 1
                if n >= 4:
                    pe.wait_ge(item_stored, n - 3)
                return n % 4

            def piece_in(ph, n):
                pe.wait_ge(lo_ready[ph], n + 1)

            def lat():
                for n in range(5):
                    hi, lo = piece_bufs(n, KD, 256 if n < 4 else P)
                    piece_in(0, n)
                    b = item_bank() if n < 4 else 4
                    if n == 4:
                        item[0] += 1
                        pe.wait_ge(norm_root, 1)
                    for m in range(2 if n < 4 else 1):
                        for k in range(KD):
                            if n == 0 and m == 0:
                                pe.wait_ge(xl_ready, k // 2 + 1)
                            x = (xh[:, k, :], xl[:, k, :])
                            if n < 4:
                                ins = mm3(PS[:, b, m * T:(m + 1) * T],
                                          (hi[:, k, m * P:(m + 1) * P], lo[:, k, m * P:(m + 1) * P]), x,
                                          k == 0, k == KD - 1)
                            else:
                                ins = mm3(PS[:, 4, 0:T], (hi[:, k, :], lo[:, k, :]), x, k == 0, k == KD - 1)
                    ins.then_inc(item_done, 1)
                    pe.wait_ge(item_done, item[0])
                    pe.sem_inc(piece_used[0], 1)
                pe.wait_ge(item_stored, 5)
                for m in range(KQ):
                    mm(PS[:, 5, 0:T], ones, sq[:, m, :], start=(m == 0), stop=(m == KQ - 1))
                for m in range(KKV):
                    ins = mm(PS[:, 5, T:2 * T], ones, sq[:, KQ + m, :], start=(m == 0), stop=(m == KKV - 1))
                ins.then_inc(lat_sum, 1)
                pe.wait_ge(kpe_scaled, 1)
                mm(PS[:, 6, 0:T], con_("rot"), ropetmp[:, 1, :], start=True, stop=True).then_inc(kpe_rot, 1)

            def kv_piece(half):
                n = 5 + half
                _, hi, lo, _, _ = mixer_piece(0, n)
                piece_in(0, n)
                if half == 0:
                    pe.wait_ge(latl_ready, 1)
                lat = lambda k, c: (xh[:, KQ + k, c], xl[:, KQ + k, c])
                for pair in range(2):
                    b = item_bank()
                    for a in range(2):
                        c = 256 * (2 * pair + a)
                        for k in range(KKV):
                            ins = mm3(PS[:, b, a * T:(a + 1) * T], (hi[:, k, c:c + NOPE], lo[:, k, c:c + NOPE]),
                                      lat(k, slice(0, T)), k == 0, k == KKV - 1)
                    ins.then_inc(item_done, 1)
                for t in range(NT):
                    b = item_bank()
                    for k in range(KKV):
                        w = [x[:, k, :].rearrange("p (h c) -> p h c", c=256)[:, :, NOPE:] for x in (hi, lo)]
                        ins = mm3(PS[:, b, :].rearrange("p (h c) -> p h c", c=VD), lat(k, slice(t * P, (t + 1) * P)),
                                  w, k == 0, k == KKV - 1)
                    ins.then_inc(item_done, 1)
                pe.wait_ge(item_done, item[0])
                pe.sem_inc(piece_used[0], 1)

            def q_piece(i):
                n = 7 + i
                _, hi, lo, _, _ = mixer_piece(0, n)
                piece_in(0, n)
                if i == 0:
                    pe.wait_ge(latl_ready, 4)
                b = item_bank()
                for a in range(2):
                    for k in range(KQ):
                        ins = mm3(PS[:, b, a * T:(a + 1) * T], (hi[:, k, a * P:(a + 1) * P], lo[:, k, a * P:(a + 1) * P]),
                                  (xh[:, k, :], xl[:, k, :]), k == 0, k == KQ - 1)
                ins.then_inc(item_done, 1)
                pe.wait_ge(item_done, item[0])
                pe.sem_inc(piece_used[0], 1)

            def k_stats():
                pe.wait_ge(item_stored, 13)
                pe.wait_ge(krope_ready, 1)
                for h in range(HEADS):
                    mm(PS[0:HEADS, 5, 0:T], con_("hsel", HEADS, HEADS * h), sq[:, h, :], start=(h == 0), stop=False)
                mm(PS[0:HEADS, 5, 0:T], con_("kpesel", HEADS), kpe_sq, start=False, stop=True).then_inc(k_sum, 1)

            def k_broadcast():
                pe.wait_ge(k_recip, 1)
                for i in range(PAIRS):
                    if i >= 2:
                        pe.wait_ge(bc_used, i - 1)
                    for a in range(2):
                        row = con_("ident", 1, 2 * i + a, HEADS).to_broadcast([HEADS, P])
                        ins = mm(PS[:, 5 + i % 2, a * T:(a + 1) * T], row, rstd[0:HEADS, 0:T], start=True, stop=True)
                    ins.then_inc(bc_done, 1)

            def q_stats():
                pe.wait_ge(item_stored, 19)
                pe.wait_ge(bc_used, PAIRS)
                for h in range(HEADS):
                    mm(PS[0:HEADS, 5, 0:T], con_("hsel", HEADS, HEADS * h), sq[:, h, :], start=(h == 0), stop=False)
                for g in range(PAIRS):
                    ins = mm(PS[0:HEADS, 5, 0:T], con_("psel", HEADS, HEADS * g), sq_rope[:, g, :], start=False,
                             stop=(g == PAIRS - 1))
                ins.then_inc(q_sum, 1)
                for i in range(2):
                    for a in range(2):
                        ins = mm(PS[:, i, a * T:(a + 1) * T], con_("rot"), qr[:, 2 * i + a, :], start=True, stop=True)
                    ins.then_inc(q_rot, 1)
                pe.wait_ge(q_recip, 1)
                for t in range(NT):
                    ins = tr(PS[:, 6, t * HEADS:(t + 1) * HEADS], rstd[0:HEADS, t * P:(t + 1) * P],
                             C[0:HEADS, CC["ident"]:CC["ident"] + HEADS])
                ins.then_inc(q_turned, 1)

            def attn_scores(h):
                g, a = divmod(h, 2)
                if h == 0:
                    pe.wait_ge(q_ready, 2)
                if h >= 2:
                    pe.wait_ge(s_masked, h - 1)
                r = slice(64 * a, 64 * a + 64)
                b = PS[:, h % 2, :]
                for qb, at, n in ((0, 0, P), (1, P, 2 * P)):
                    q = slice(qb * P, (qb + 1) * P)
                    mm(b[:, at:at + n], qn[:, h, q], kn[:, h, 0:n], start=True, stop=False)
                    ins = mm(b[:, at:at + n], qr[r, g, q], kr[r, g, 0:n], start=False, stop=True)
                ins.then_inc(s_done, 1)

            def attn_values(h):
                pe.wait_ge(p_ready, h + 1)
                if h >= 2:
                    pe.wait_ge(pt_stored, h - 1)
                for i in range(3):
                    ins = tr(PS[:, 2 + h % 2, i * P:(i + 1) * P], attn_p[:, h % 2, i * P:(i + 1) * P], ident)
                ins.then_inc(pt_done, 1)
                pe.wait_ge(pt_stored, h + 1)
                if h >= 2:
                    pe.wait_ge(ol_ready, h - 1)
                else:
                    pe.wait_ge(rq_ready, 1)
                pt = attn_pt[:, h % 2, :]
                b = PS[:, 5 + h % 2, :]
                mm(b[:, 0:T], vt[:, 0, h * VD:(h + 1) * VD], pt[:, 0:T], start=True, stop=False)
                mm(b[:, P:T], vt[:, 1, h * VD:(h + 1) * VD], pt[:, T:T + P], start=False,
                   stop=True).then_inc(o_done, 1)

            def project(mx, first, free):
                for i in range(4):
                    _, hi, lo, _, _ = mixer_piece(mx, first + i)
                    piece_in(2 * mx, first + i)
                    for m in range(2):
                        for k in range(KD):
                            if i == 0 and m == 0:
                                free(k)
                            ins = mm3(PS[:, i, m * T:(m + 1) * T],
                                      (hi[:, k, m * P:(m + 1) * P], lo[:, k, m * P:(m + 1) * P]),
                                      (xh[:, k, :], xl[:, k, :]), k == 0, k == KD - 1)
                    ins.then_inc(proj_done[mx], 1)
                    pe.wait_ge(proj_done[mx], i + 1)
                    pe.sem_inc(piece_used[2 * mx], 1)

            def mixer0():
                pe.wait_ge(con_in, 16)
                pe.wait_ge(vec_in, 16)
                norm_sums(0)
                for a in range(4):
                    ada(a)
                lat()
                kv_piece(0)
                kv_piece(1)
                k_stats()
                for i in range(6):
                    q_piece(i)
                    if i == 1:
                        k_broadcast()
                q_stats()
                for h in range(HEADS):
                    attn_scores(h)
                    if h:
                        attn_values(h - 1)
                    for a in ADA_ORDER[0][2 * h:2 * h + 2]:
                        ada(a)
                attn_values(HEADS - 1)
                project(0, 13, lambda k: pe.wait_ge(ol_ready, k + 1))

            def conv(c):
                pe.wait_ge(diag_ready, c + 1)
                pe.wait_ge(glu_ready, c + 1)
                if c >= 2:
                    pe.wait_ge(conv_ready, c // 2 * 2)
                for j in range(PE_TAPS):
                    ins = mm(PS[:, 5 + c % 2, 0:T], diag[:, c % 2, j, :], upad[:, c, j:j + T], start=(j == 0),
                             stop=(j == PE_TAPS - 1))
                ins.then_inc(conv_pe, 1)

            def mixer1():
                norm_sums(2)
                for n in range(8):
                    i, half = divmod(n, 2)
                    _, hi, lo, _, _ = mixer_piece(1, n)
                    piece_in(2, n)
                    b = n % 4
                    if n >= 4:
                        pe.wait_ge(glu_ready, 2 * (i - 1))
                    for m in range(2):
                        for k in range(KD):
                            if n == 0 and m == 0:
                                pe.wait_ge(xl_ready, 4 + k // 2 + 1)
                            ins = mm3(PS[:, b, m * T:(m + 1) * T],
                                      (hi[:, k, m * P:(m + 1) * P], lo[:, k, m * P:(m + 1) * P]),
                                      (xh[:, k, :], xl[:, k, :]), k == 0, k == KD - 1)
                    ins.then_inc(glu_done, 1)
                    pe.wait_ge(glu_done, n + 1)
                    pe.sem_inc(piece_used[2], 1)
                    if half and i:
                        conv(2 * i - 2)
                        conv(2 * i - 1)
                conv(6)
                conv(7)
                for a in ADA_ORDER[1]:
                    ada(a)
                for k in range(KD):
                    pe.wait_ge(conv_ready, k + 1)
                    ins = mm(PS[:, 4, 0:T], ones, cacc[:, k, :], start=(k == 0), stop=(k == KD - 1))
                ins.then_inc(ln_sum, 1)
                for k in range(KD):
                    pe.wait_ge(ln_sq, k // 2 + 1)
                    ins = mm(PS[:, 5, 0:T], ones, sq[:, k, :], start=(k == 0), stop=(k == KD - 1))
                ins.then_inc(ln_var, 1)
                project(1, 8, lambda k: pe.wait_ge(xl_ready, 8 + k // 2 + 1))

            def moe(l):
                ph, n = 2 * l + 1, 2 * l + 1
                norm_sums(n)
                for t in range(NT):
                    for k in range(KD):
                        if t == 0:
                            pe.wait_ge(h_ready, 8 * n + k + 1)
                        ins = mm(PS[:, 0, t * E:(t + 1) * E], hT[:, k, t * P:(t + 1) * P],
                                 vcol("router_w", k * E, E), start=(k == 0), stop=(k == KD - 1))
                ins.then_inc(logits_done, 1)
                for i in range(4):
                    t, half = divmod(i, 2)
                    if i >= 2:
                        pe.wait_ge(htokl_ready, 4 * l + i - 1)
                    for j in range(4):
                        ins = tr(PS[:, 5 + i % 2, j * P:(j + 1) * P],
                                 hT[:, half * 4 + j, t * P:(t + 1) * P], ident)
                    ins.then_inc(htok_done, 1)
                pe.wait_ge(picks_ready, l + 1)
                picks = [small[:, 256 + t * E:256 + (t + 1) * E] for t in range(NT)]
                b = PS[:, 1, :]
                mm(b[:, 0:E], con_("before"), picks[0], start=True, stop=True)
                mm(b[:, E:2 * E], con_("before"), picks[1], start=True, stop=False)
                mm(b[:, E:2 * E], ones, picks[0], start=False, stop=True)
                for t in range(NT):
                    ins = mm(b[0:E, 64:64 + P], picks[t], ones, start=(t == 0), stop=(t == NT - 1))
                ins.then_inc(counts_done, 1)
                pe.wait_ge(count_rows, l + 1)
                c16, n16 = small[0:E, 512:512 + P], small[0:E, 640:641]
                b = PS[:, 2, :]
                mm(b[:, 0:E], c16, con_("tri16", E, 0, E), start=True, stop=True)
                mm(b[0:E, 64:65], con_("tri16", E, 0, E), c16[:, 0:1], start=True, stop=True)
                mm(b[0:E, 65:66], con_("tri16", E, 0, E), n16, start=True, stop=True).then_inc(offs_done, 1)
                pe.wait_ge(slots_ready, l + 1)
                mm(PS[0:1, 3, 0:NTAB], ones[0:E, 0:1], small[0:E, 1024:1024 + NTAB], start=True,
                   stop=True).then_inc(rows_done, 1)
                pe.wait_ge(htokl_ready, 4 * l + 4)
                banks = (5, 6, 4, 0)
                for k in range(KD):
                    if k == 0:
                        pe.wait_ge(perm_ready, 2 * l + NT)
                    if k >= 4:
                        pe.wait_ge(gather_stored, 8 * l + k - 3)
                    c = slice(k * P, (k + 1) * P)
                    for t in range(NT):
                        mm(PS[:, banks[k % 4], :], htokh[:, t, c], perm[:, t, :], start=(t == 0), stop=False)
                        ins = mm(PS[:, banks[k % 4], :], htokl[:, t, c], perm[:, t, :], start=False,
                                 stop=(t == NT - 1))
                    ins.then_inc(gather_done, 1)
                pe.wait_ge(wperm_ready, 2 * l + NT)
                for s in range(SB):
                    for t in range(NT):
                        ins = tr(PS[:, 1 + s // 2, (s % 2) * T + t * P:(s % 2) * T + (t + 1) * P],
                                 wperm[:, t, s * P:(s + 1) * P], ident)
                    if s % 2:
                        ins.then_inc(wpt_done, 1)
                pe.wait_ge(wpt_stored, 2 * l + 2)
                pe.wait_ge(gather_stored, 8 * l + KD)
                pe.wait_ge(table_ready, l + 1)
                inner = inner_blocks(pe, l)

                def y_turn(j):
                    pe.wait_ge(y_stored[l], nth(j, 2))
                    for half in range(2):
                        for i in range(4):
                            ins = tr(PS[:, 5 + half, i * P:(i + 1) * P], yb[:, (4 * half + i) * P:(4 * half + i + 1) * P],
                                     ident)
                        ins.then_inc(ytt_done[l], 1)

                def one(j, first, last):
                    pe.wait_ge(hcl_ready[l], nth(j))
                    if not first:
                        pe.wait_ge(silu_done[l], nth(j, 1, -1))
                    for i in range(4):
                        u, half = divmod(i, 2)
                        if i == 2 and not first:
                            pe.wait_ge(act_ready[l], nth(j, 1, -1))
                        _, hi, lo = moe_piece(i)
                        pe.wait_ge(lo_ready[ph], nth(j, 6, i - 5))
                        for k in range(4):
                            kk = 4 * half + k
                            ins = mm3(PS[:, u, :], (hch[:, kk, :], hcl[:, kk, :]), (hi[:, k, :], lo[:, k, :]),
                                      kk == 0, kk == KD - 1)
                        ins.then_inc(piece_used[ph], 1)
                    if not first:
                        y_turn(after(j, -1))
                    pe.wait_ge(act_ready[l], nth(j))
                    if not first:
                        pe.wait_ge(atl_ready[l], nth(j, 2, -2))
                    for half in range(2):
                        for i in (2 * half, 2 * half + 1):
                            ins = tr(PS[:, 2, i * P:(i + 1) * P], act[:, i * P:(i + 1) * P], ident)
                    ins.then_inc(att_done[l], 1)
                    for i in (4, 5):
                        _, hi, lo = moe_piece(i)
                        pe.wait_ge(lo_ready[ph], nth(j, 6, i - 5))
                        if not first:
                            pe.wait_ge(y_stored[l], nth(j, 2, i - 7))
                        for k in range(KF):
                            if i == 4 and k % 2 == 0:
                                pe.wait_ge(atl_ready[l], nth(j, 2, k // 2 - 1))
                            ins = mm3(PS[:, i - 1, :], (aTh[:, k, :], aTl[:, k, :]), (hi[:, k, :], lo[:, k, :]),
                                      k == 0, k == KF - 1)
                        ins.then_inc(piece_used[ph], 1)

                one((None, 1), True, False)
                with pe.Fori(0, inner) as r:
                    one((r, 2), False, False)
                final = (inner, 2)
                one(final, False, True)
                y_turn(final)
                pe.wait_ge(yta_stored[l], nth(final))
                pe.wait_ge(ytd_stored[l], nth(final))
                for i in range(8):
                    s, half = divmod(i, 2)
                    if i >= 2:
                        pe.wait_ge(ysl_stored, 8 * l + i - 1)
                    for j in range(4):
                        k = half * 4 + j
                        ins = tr(PS[:, 5 + i % 2, j * P:(j + 1) * P], yT[:, k, s * P:(s + 1) * P], ident)
                    ins.then_inc(ysl_done, 1)
                pe.wait_ge(ysl_stored, 8 * l + 8)
                for k in range(KD):
                    for s in range(SB):
                        ins = mm(PS[:, k // 2, (k % 2) * T:(k % 2 + 1) * T], ysl[:, s, k * P:(k + 1) * P],
                                 wpT[:, s, :], start=(s == 0), stop=(s == SB - 1))
                    if k % 2:
                        ins.then_inc(moe_done, 1)

            mixer0()
            moe(0)
            mixer1()
            moe(1)

        @block.scalar
        def _(act_e):
            A = nc.scalar.activation
            act_e.dma_start(V[:], vec).then_inc(vec_in, 16)
            act_e.dma_start(XT[:], xT).then_inc(x_in, 16)
            act_e.dma_start(C[:], con).then_inc(con_in, 16)
            act_e.dma_start(posi, pos).then_inc(pos_in, 16)
            act_e.dma_start(rb[:], rbias).then_inc(rb_in, 16)
            act_e.wait_ge(eps_ready, 2)
            act_e.wait_ge(vec_in, 16)
            A(sc[:], vcol("c", 0, KD), ACT.Silu).then_inc(silu_c, 1)

            def norm(n):
                for i in range(4):
                    if n == 0:
                        act_e.wait_ge(x_in, 16)
                    else:
                        act_e.wait_ge(resid, KD * (n - 1) + 2 * i + 2)
                    if n == 2 and i == 0:
                        act_e.wait_ge(moe_done, 4)
                    A(sq[:, 2 * i:2 * i + 2, :], XT[:, 2 * i:2 * i + 2, :], ACT.Square).then_inc(norm_sq, 1)
                act_e.wait_ge(norm_sum, n + 1)
                A(root[:, 0:T], PS[:, 4, 0:T], ACT.Sqrt, bias=eps[:, 0:1], scale=1.0 / D).then_inc(norm_root, 1)
                l, w = divmod(n, 2)
                act_e.wait_ge(mods_ready, n + 1)
                for k in range(KD):
                    act_e.wait_ge(norm_scaled, 4 * n + k // 2 + 1)
                    A(hT[:, k, :], hT[:, k, :], ACT.Identity, bias=mods[:, l, 24 * w + k:24 * w + k + 1],
                      scale=gsc[:, n, k:k + 1]).then_inc(h_ready, 1)

            def split_x(src, done, base):
                for i in range(4):
                    act_e.wait_ge(done, base + 2 * i + 2)
                    A(xh[:, 2 * i:2 * i + 2, :], src[:, 2 * i:2 * i + 2, :], ACT.Copy).then_inc(xh_ready, 1)

            def hi(mx, n):
                raw, h, _, u, _ = mixer_piece(mx, n)
                wait_unit(act_e, mx, u)
                if n >= PBUF:
                    act_e.wait_ge(piece_used[2 * mx], n - PBUF + 1)
                elif mx:
                    act_e.wait_ge(piece_used[1], nth((inner_blocks(act_e, 0), 2), 6))
                A(h, raw, ACT.Copy).then_inc(hi_ready[2 * mx], 1)

            def root_of(dst, src, n):
                return A(dst, src, ACT.Sqrt, bias=eps[0:dst.shape[0], 0:1], scale=1.0 / n)

            def two(b):
                return PS[:, b, :].rearrange("p (a t) -> p a t", t=T)

            def store_lat(n):
                act_e.wait_ge(item_done, n + 1)
                if n < 4:
                    A(latT[:, 2 * n:2 * n + 2, :], two(n), ACT.Copy)
                    A(sq[:, 2 * n:2 * n + 2, :], two(n), ACT.Square).then_inc(item_stored, 1)
                else:
                    A(latT[:, 8, :], PS[:, 4, 0:T], ACT.Copy)
                    A(kpe_sq, PS[:, 4, 0:T], ACT.Square).then_inc(item_stored, 1)

            def store_k(n, pair):
                act_e.wait_ge(item_done, n + 1)
                ks = slice(2 * pair, 2 * pair + 2)
                if n == 5:
                    act_e.wait_ge(lat_sum, 1)
                A(kn[:, ks, :], two(n % 4), ACT.Identity, scale=vcol("gk_nope"))
                A(sq[:, ks, :], two(n % 4), ACT.Square).then_inc(item_stored, 1)

            def store_v(n, t, half):
                act_e.wait_ge(item_done, n + 1)
                A(vt[:, t, half * 512:(half + 1) * 512], PS[:, n % 4, :], ACT.Copy).then_inc(item_stored, 1)

            def store_q(i):
                n = 13 + i
                act_e.wait_ge(item_done, n + 1)
                if i == 0:
                    act_e.wait_ge(k_sum, 1)
                g = i % 4
                dst, s, gain = ((qn[:, 2 * g:2 * g + 2, :], sq[:, 2 * g:2 * g + 2, :], "gq_nope") if i < 4 else
                                (qr[:, 2 * g:2 * g + 2, :], sq_rope[:, 2 * g:2 * g + 2, :], "gq_rope"))
                A(dst, two(n % 4), ACT.Identity, scale=vcol(gain))
                A(s, two(n % 4), ACT.Square).then_inc(item_stored, 1)

            def mixer0():
                norm(0)
                split_x(hT, h_ready, 0)
                for n in range(3):
                    hi(0, n)
                for n in range(5):
                    hi(0, n + 3)
                    store_lat(n)
                act_e.wait_ge(lat_sum, 1)
                root_of(root[:, 0:T], PS[:, 5, 0:T], QR).then_inc(lat_root, 1)
                root_of(root[:, T:2 * T], PS[:, 5, T:2 * T], KVR).then_inc(lat_root, 1)
                act_e.wait_ge(angles, 2)
                A(sin_t, sin_t, ACT.Sin).then_inc(tables, 1)
                A(cos_t, cos_t, ACT.Sin, bias=eps[:, 1:2], scale=-1.0).then_inc(tables, 1)
                for i in (3, 0, 1, 2):
                    act_e.wait_ge(lat_ready, {3: 1, 0: 2, 1: 3, 2: 4}[i])
                    A(xh[:, 2 * i:2 * i + 2, :], latT[:, 2 * i:2 * i + 2, :], ACT.Copy).then_inc(lath_ready, 1)
                n = 5
                for half in range(2):
                    for pair in range(2):
                        store_k(n, 2 * half + pair)
                        n += 1
                    for t in range(NT):
                        store_v(n, t, half)
                        n += 1
                    hi(0, 8 + half)
                act_e.wait_ge(k_sum, 1)
                root_of(root[0:HEADS, 0:T], PS[0:HEADS, 5, 0:T], QK).then_inc(k_root, 1)
                for i in range(6):
                    if i < 3:
                        hi(0, 10 + i)
                    store_q(i)
                act_e.wait_ge(q_sum, 1)
                act_e.wait_ge(k_recip, 1)
                root_of(root[0:HEADS, 0:T], PS[0:HEADS, 5, 0:T], QK).then_inc(q_root, 1)
                for h in range(HEADS):
                    act_e.wait_ge(s_max, h + 1)
                    if h >= 2:
                        act_e.wait_ge(pt_done, h - 1)
                    sm = attn_sm[:, h % 2, :]
                    for i, (at, n) in enumerate(((0, P), (P, 2 * P))):
                        A(attn_p[:, h % 2, at:at + n], attn_s[:, h % 2, at:at + n], ACT.Exp,
                          bias=sm[:, 2 + i:3 + i], accum_out=sm[:, 4 + i:5 + i]).then_inc(p_exp, 1)
                    act_e.wait_ge(pt_done, h + 1)
                    if h >= 2:
                        act_e.wait_ge(o_done, h - 1)
                    A(attn_pt[:, h % 2, :], PS[:, 2 + h % 2, 0:3 * P], ACT.Copy).then_inc(pt_stored, 1)
                    act_e.wait_ge(o_done, h + 1)
                    A(xh[:, h, :], PS[:, 5 + h % 2, 0:T], ACT.Copy).then_inc(oh_ready, 1)
                for n in range(13, 17):
                    hi(0, n)

            def mixer1():
                norm(2)
                split_x(hT, h_ready, 2 * KD)
                for n in range(3):
                    hi(1, n)
                for i in range(4):
                    for n in (2 * i + 3, 2 * i + 4):
                        if n < 8:
                            hi(1, n)
                    act_e.wait_ge(glu_done, 2 * i + 2)
                    for a in range(2):
                        c = 2 * i + a
                        if c >= 4:
                            act_e.wait_ge(glu_ready, c - 3)
                        A(sig[:, c % 4, :], PS[:, (2 * i + 1) % 4, a * T:(a + 1) * T], ACT.Sigmoid,
                          bias=vcol("pw1_b", KD + c)).then_inc(glu_sig, 1)
                act_e.wait_ge(ln_sum, 1)
                A(rstd[:, T:2 * T], PS[:, 4, 0:T], ACT.Copy, scale=1.0 / D).then_inc(ln_mean, 1)
                for i in range(4):
                    act_e.wait_ge(ln_centred, i + 1)
                    A(sq[:, 2 * i:2 * i + 2, :], cacc[:, 2 * i:2 * i + 2, :], ACT.Square).then_inc(ln_sq, 1)
                act_e.wait_ge(ln_var, 1)
                A(root[:, 0:T], PS[:, 5, 0:T], ACT.Sqrt, bias=eps[:, 0:1], scale=1.0 / D).then_inc(ln_root, 1)
                for k in range(KD):
                    act_e.wait_ge(ln_scaled, k // 2 + 1)
                    A(cacc[:, k, :], cacc[:, k, :], ACT.Silu, bias=vcol("ln_b", k),
                      scale=vcol("ln_g", k)).then_inc(ln_silu, 1)
                split_x(cacc, ln_silu, 0)
                for n in range(8, 12):
                    hi(1, n)

            def moe(l):
                ph = 2 * l + 1
                norm(ph)
                act_e.wait_ge(logits_done, l + 1)
                A(small[:, 0:2 * E], PS[:, 0, 0:2 * E], ACT.Sigmoid).then_inc(scores_ready, 1)
                for i in range(4):
                    t, half = divmod(i, 2)
                    act_e.wait_ge(htok_done, 4 * l + i + 1)
                    A(htokh[:, t, half * 512:(half + 1) * 512], PS[:, 5 + i % 2, :],
                      ACT.Copy).then_inc(htokh_ready, 1)

                def hi_m(j, i):
                    raw, h, _ = moe_piece(i)
                    if i % 2 == 0:
                        act_e.wait_ge(landed[ph][i // 2], nth(j, 16))
                    if j[0] is None and i < PBUF:
                        if i == 0:
                            act_e.wait_ge(piece_used[2 * l], len(pieces[l]))
                    else:
                        act_e.wait_ge(piece_used[ph], nth(j, 6, i - 5 - PBUF))
                    A(h, raw, ACT.Copy).then_inc(hi_ready[ph], 1)

                hi_m((None, 1), 0)
                hi_m((None, 1), 1)
                for k in range(KD):
                    act_e.wait_ge(gather_done, 8 * l + k + 1)
                    A(hgT[:, k, 0:SLOTS], PS[:, (5, 6, 4, 0)[k % 4], :], ACT.Copy).then_inc(gather_stored, 1)
                act_e.wait_ge(table_ready, l + 1)
                inner = inner_blocks(act_e, l)

                def slot_in(j):
                    s0 = block_slot(act_e, l, j)
                    A(hch, hgT[:, :, bass.ds(s0, P)], ACT.Copy).then_inc(hch_ready[l], 1)

                def y_out(j):
                    act_e.wait_ge(ytt_done[l], nth(j, 2, -1))
                    s0 = block_slot(act_e, l, j)
                    A(yT[:, 0:4, bass.ds(s0, P)], PS[:, 5, :].rearrange("p (m c) -> p m c", c=P),
                      ACT.Copy).then_inc(yta_stored[l], 1)

                def one(j, first, last):
                    hi_m(j, 2)
                    hi_m(j, 3)
                    act_e.wait_ge(piece_used[ph], nth(j, 6, -4))
                    if not first:
                        act_e.wait_ge(act_ready[l], nth(j, 1, -1))
                    A(sg, PS[:, 0, :], ACT.Silu).then_inc(silu_done[l], 1)
                    hi_m(j, 4)
                    hi_m(j, 5)
                    if not last:
                        act_e.wait_ge(piece_used[ph], nth(j, 6, -2))
                        slot_in(after(j))
                    if not first:
                        y_out(after(j, -1))
                    act_e.wait_ge(att_done[l], nth(j))
                    for half in range(2):
                        A(aTh[:, 2 * half:2 * half + 2, :],
                          PS[:, 2, 256 * half:256 * half + 256].rearrange("p (m c) -> p m c", c=P),
                          ACT.Copy).then_inc(ath_ready[l], 1)
                    if not last:
                        hi_m(after(j), 0)
                    for half in range(2):
                        act_e.wait_ge(piece_used[ph], nth(j, 6, half - 1))
                        if not first:
                            act_e.wait_ge(ytt_done[l], nth(j, 2, -2))
                        A(yb[:, 512 * half:512 * half + 512], PS[:, 3 + half, :], ACT.Copy).then_inc(y_stored[l], 1)
                        if half == 0 and not last:
                            hi_m(after(j), 1)

                act_e.wait_ge(gather_stored, 8 * l + KD)
                act_e.wait_ge(wpt_stored, 2 * l + 2)
                slot_in((None, 1))
                one((None, 1), True, False)
                with act_e.Fori(0, inner) as r:
                    one((r, 2), False, False)
                final = (inner, 2)
                one(final, False, True)
                y_out(final)
                for i in range(8):
                    s, half = divmod(i, 2)
                    act_e.wait_ge(ysl_done, 8 * l + i + 1)
                    A(ysl[:, s, half * 512:(half + 1) * 512], PS[:, 5 + i % 2, :],
                      ACT.Copy).then_inc(ysl_stored, 1)

            mixer0()
            moe(0)
            mixer1()
            moe(1)

        @block.gpsimd
        def _(pool):
            nc.gpsimd.memset(eps[:, 0:1], EPS).then_inc(eps_ready, 1)
            nc.gpsimd.memset(eps[:, 1:2], TWO_PI / 4).then_inc(eps_ready, 1)
            seq = [0]

            def step(ins):
                seq[0] += 1
                ins.then_inc(pool_seq, 1)
                pool.wait_ge(pool_seq, seq[0])

            def ada(mx, a):
                wait_unit(pool, mx, ("ada", a))
                n = POOL_ADA.index(a)
                if n:
                    pool.wait_ge(ada_done, max(ADA_ALL.index(POOL_ADA[n - 1]) + 1, 1))
                if a == min(x for x in ADA_ORDER[mx] if x in POOL_ADA):
                    pool.wait_ge(xl_ready, 4 * mx + 4)
                w = unit_ap("ada", a)
                acc, tmp = ada_acc(a), hflat[:, 1536:2048]
                step(nc.gpsimd.tensor_scalar(acc, w[:, 0, :], sc[:, 0:1], 1.0, ALU.mult, ALU.mult))
                for k in range(1, KD):
                    step(nc.gpsimd.tensor_scalar(tmp, w[:, k, :], sc[:, k:k + 1], 1.0, ALU.mult, ALU.mult))
                    if k < KD - 1:
                        step(nc.gpsimd.tensor_tensor(acc, acc, tmp, ALU.add))
                nc.gpsimd.tensor_tensor(acc, acc, tmp, ALU.add).then_inc(ada_pooled, 1)
                pool.wait_ge(ada_pooled, n + 1)
                pool.sem_inc(pool_used[mx], 1)

            pool.wait_ge(silu_c, 1)
            for a in POOL_ADA:
                if a < NA_PRE:
                    ada(0, a)
            pool.wait_ge(con_in, 16)
            pool.wait_ge(resid, 2 * KD)
            for c in range(KD):
                if c >= 2:
                    pool.wait_ge(conv_pe, c - 1)
                for j in range(PE_TAPS):
                    ins = nc.gpsimd.tensor_scalar(diag[:, c % 2, j, :], ident, vcol("dw_w", c * TAPS + j), 1.0,
                                                  ALU.mult, ALU.mult)
                ins.then_inc(diag_ready, 1)
            for a in POOL_ADA:
                if a >= NA_PRE:
                    ada(1, a)

        @block.vector
        def _(dve):
            v = nc.vector
            seq = [0]

            def tick(ins):
                seq[0] += 1
                ins.then_inc(dve_seq, 1)

            def step(ins):
                tick(ins)
                dve.wait_ge(dve_seq, seq[0])

            def bc(ap, shape):
                return ap.to_broadcast(shape)

            ada_sums, ada_stores = [0], [0]

            def ada_sum(mx, a):
                wait_unit(dve, mx, ("ada", a))
                if a == 0:
                    dve.wait_ge(silu_c, 1)
                mine = [b for b in range(24) if b not in POOL_ADA]
                n = mine.index(a)
                if n >= 2:
                    before = [b for b in mine[:n] if ada_acc_id(b) == ada_acc_id(a)]
                    if before:
                        dve.wait_ge(ada_done, ADA_ALL.index(before[-1]) + 1)
                w, acc = unit_ap("ada", a), ada_acc(a)
                step(v.tensor_scalar(acc, w[:, 0, :], sc[:, 0:1], None, ALU.mult))
                for k in range(1, KD):
                    ins = v.scalar_tensor_tensor(out=acc, in0=w[:, k, :], scalar=sc[:, k:k + 1], in1=acc,
                                                 op0=ALU.mult, op1=ALU.add)
                    if k < KD - 1:
                        step(ins)
                ins.then_inc(ada_summed, 1)
                dve.wait_ge(ada_summed, n + 1)
                dve.sem_inc(raw_used[mx], 1)

            def ada_store(a):
                l, j = divmod(a, 12)
                ada_stores[0] += 1
                dve.wait_ge(ada_done, ada_stores[0])
                v.tensor_tensor(mods[:, l, 4 * j:4 * j + 4], PS[:, 7, 0:4],
                                vcol("ada_b", 48 * l + 4 * j, 4), ALU.add).then_inc(ada_stored, 1)

            def mods_for(n, upto):
                l, w = divmod(n, 2)
                dve.wait_ge(ada_stored, upto)
                v.scalar_tensor_tensor(out=gsc[:, n, :], in0=mods[:, l, 24 * w + 8:24 * w + 16], scalar=1.0,
                                       in1=vcol(("norm1", "norm2")[w], KD * l, KD), op0=ALU.add,
                                       op1=ALU.mult).then_inc(mods_ready, 1)

            def norm(n):
                dve.wait_ge(norm_root, n + 1)
                step(v.reciprocal(rstd[:, 0:T], root[:, 0:T]))
                for i in range(4):
                    ks = slice(2 * i, 2 * i + 2)
                    v.tensor_tensor(hT[:, ks, :], XT[:, ks, :], bc(rstd[:, 0:T].unsqueeze(1), [P, 2, T]),
                                    ALU.mult).then_inc(norm_scaled, 1)

            def split_x(src, his, base, signal, order=(0, 1, 2, 3)):
                for n, i in enumerate(order):
                    dve.wait_ge(his, base + n + 1)
                    ks = slice(2 * i, 2 * i + 2)
                    v.tensor_tensor(xl[:, ks, :], src[:, ks, :], xh[:, ks, :].bitcast(F32),
                                    ALU.subtract).then_inc(signal, 1)

            def lo(mx, n):
                raw, h, l_, u, j = mixer_piece(mx, n)
                dve.wait_ge(hi_ready[2 * mx], n + 1)
                v.tensor_tensor(l_, raw, h.bitcast(F32), ALU.subtract).then_inc(lo_ready[2 * mx], 1)
                if j == pieces_of(u) - 1:
                    dve.wait_ge(lo_ready[2 * mx], n + 1)
                    dve.sem_inc(raw_used[mx], 1)

            def residual(bank, k, gate):
                at = (k % 2) * T
                return v.scalar_tensor_tensor(out=XT[:, k, :], in0=PS[:, bank, at:at + T], scalar=gate,
                                              in1=XT[:, k, :], op0=ALU.mult, op1=ALU.add)

            def rope_tables():
                dve.wait_ge(pos_in, 16)
                dve.wait_ge(vec_in, 16)
                ang, n = ropetmp[:, 0, :], ropetmp[:, 1, :]
                step(v.tensor_copy(sin_t, posi))
                step(v.tensor_scalar(ang, sin_t, vcol("inv_freq"), None, ALU.mult))
                step(v.tensor_scalar(n, ang, 1.0 / TWO_PI, MAGIC, ALU.mult, ALU.add))
                step(v.tensor_scalar(n, n, MAGIC, None, ALU.subtract))
                for part in (PI_A, PI_B, PI_C):
                    step(v.scalar_tensor_tensor(out=ang, in0=n, scalar=-part, in1=ang, op0=ALU.mult, op1=ALU.add))
                step(v.tensor_scalar(ang, ang, 3.1415925, -3.1415925, ALU.min, ALU.max))
                v.tensor_copy(sin_t, ang).then_inc(angles, 1)
                step(v.tensor_scalar(n, ang, -1.0, None, ALU.mult))
                v.tensor_tensor(cos_t, ang, n, ALU.max).then_inc(angles, 1)

            def latents():
                dve.wait_ge(item_stored, 5)
                dve.wait_ge(angles, 2)
                v.tensor_scalar(ropetmp[:, 1, :], latT[:, 8, :], vcol("gk_rope"), None,
                                ALU.mult).then_inc(kpe_scaled, 1)
                dve.wait_ge(lat_root, 2)
                step(v.reciprocal(rstd[:], root[:]))
                for m in (6, 7, 0, 1, 2, 3, 4, 5):
                    g = vcol("q_norm", m) if m < KQ else vcol("kv_norm", m - KQ)
                    r = rstd[:, 0:T] if m < KQ else rstd[:, T:2 * T]
                    ins = v.scalar_tensor_tensor(out=latT[:, m, :], in0=latT[:, m, :], scalar=g, in1=r, op0=ALU.mult,
                                                 op1=ALU.mult)
                    if m % 2:
                        ins.then_inc(lat_ready, 1)
                split_x(latT, lath_ready, 0, latl_ready, (3, 0, 1, 2))
                dve.wait_ge(tables, 2)
                dve.wait_ge(kpe_rot, 1)
                step(v.tensor_tensor(krope, PS[:, 6, 0:T], sin_t, ALU.mult))
                step(v.tensor_tensor(ropetmp[:, 0, :], ropetmp[:, 1, :], cos_t, ALU.mult))
                v.tensor_tensor(krope, krope, ropetmp[:, 0, :], ALU.add).then_inc(krope_ready, 1)

            def scale_keys():
                dve.wait_ge(krope_ready, 1)
                for i in range(PAIRS):
                    dve.wait_ge(bc_done, i + 1)
                    b = PS[:, 5 + i % 2, :].rearrange("p (a t) -> p a t", t=T)
                    ks = kn[:, 2 * i:2 * i + 2, :]
                    v.tensor_tensor(ks, ks, b, ALU.mult)
                    for a in range(2):
                        r = slice(ROPE * a, ROPE * a + ROPE)
                        ins = v.tensor_tensor(kr[r, i, :], krope[r, :], b[r, a, :], ALU.mult)
                    ins.then_inc(bc_used, 1)

            def queries():
                dve.wait_ge(q_root, 1)
                v.reciprocal(rstd[0:HEADS, 0:T], root[0:HEADS, 0:T]).then_inc(q_recip, 1)
                for i in range(2):
                    dve.wait_ge(q_rot, i + 1)
                    qs = qr[:, 2 * i:2 * i + 2, :]
                    step(v.tensor_tensor(ropetmp, PS[:, i, :].rearrange("p (a t) -> p a t", t=T),
                                         bc(sin_t.unsqueeze(1), [P, 2, T]), ALU.mult))
                    step(v.tensor_tensor(qs, qs, bc(cos_t.unsqueeze(1), [P, 2, T]), ALU.mult))
                    v.tensor_tensor(qs, qs, ropetmp, ALU.add).then_inc(q_ready, 1)
                    dve.wait_ge(q_ready, i + 1)
                dve.wait_ge(q_turned, 1)
                v.tensor_scalar(kq_rstd, PS[:, 6, 0:2 * HEADS], SCALE, None, ALU.mult).then_inc(rq_ready, 1)
                dve.wait_ge(rq_ready, 1)

            def softmax(h):
                s, sm = attn_s[:, h % 2, :], attn_sm[:, h % 2, :]
                dve.wait_ge(s_done, h + 1)
                for t, c in ((0, slice(0, P)), (1, slice(P, 3 * P))):
                    ins = v.scalar_tensor_tensor(out=s[:, c], in0=PS[:, h % 2, c],
                                                 scalar=kq_rstd[:, t * HEADS + h:t * HEADS + h + 1],
                                                 in1=con_("causal", 3 * P)[:, c], op0=ALU.mult, op1=ALU.add)
                ins.then_inc(s_masked, 1)
                dve.wait_ge(s_masked, h + 1)
                v.tensor_reduce(sm[:, 0:1], s[:, 0:P], AX, ALU.max)
                step(v.tensor_reduce(sm[:, 1:2], s[:, P:3 * P], AX, ALU.max))
                v.tensor_scalar(sm[:, 2:4], sm[:, 0:2], -1.0, None, ALU.mult).then_inc(s_max, 1)

            def normalise(h):
                sm = attn_sm[:, h % 2, :]
                dve.wait_ge(p_exp, 2 * h + 2)
                step(v.reciprocal(sm[:, 6:8], sm[:, 4:6]))
                p = attn_p[:, h % 2, :]
                v.tensor_scalar(p[:, 0:P], p[:, 0:P], sm[:, 6:7], None, ALU.mult)
                v.tensor_scalar(p[:, P:3 * P], p[:, P:3 * P], sm[:, 7:8], None, ALU.mult).then_inc(p_ready, 1)

            def o_low(h):
                dve.wait_ge(oh_ready, h + 1)
                v.tensor_tensor(xl[:, h, :], PS[:, 5 + h % 2, 0:T], xh[:, h, :].bitcast(F32),
                                ALU.subtract).then_inc(ol_ready, 1)

            def mixer0():
                rope_tables()
                norm(0)
                ada_sum(0, 0)
                for a in range(4):
                    if a < 3:
                        ada_sum(0, a + 1)
                    ada_store(a)
                mods_for(0, 4)
                split_x(hT, xh_ready, 0, xl_ready)
                dve.wait_ge(con_in, 16)
                dve.wait_ge(rb_in, 16)
                for n in range(5):
                    lo(0, n)
                for n in range(5, 8):
                    lo(0, n)
                latents()
                for n in range(8, 10):
                    lo(0, n)
                dve.wait_ge(k_root, 1)
                dve.wait_ge(lat_ready, 4)
                v.reciprocal(rstd[0:HEADS, 0:T], root[0:HEADS, 0:T]).then_inc(k_recip, 1)
                for n in range(10, 11):
                    lo(0, n)
                scale_keys()
                for n in range(11, 13):
                    lo(0, n)
                dve.wait_ge(bc_used, PAIRS)
                queries()
                for h in range(HEADS):
                    softmax(h)
                    for a in ADA_ORDER[0][2 * h:2 * h + 2][:1]:
                        if a not in POOL_ADA:
                            ada_sum(0, a)
                    normalise(h)
                    if h:
                        o_low(h - 1)
                    for a in ADA_ORDER[0][2 * h:2 * h + 2][1:]:
                        if a not in POOL_ADA:
                            ada_sum(0, a)
                    for a in ADA_ORDER[0][2 * h:2 * h + 2]:
                        ada_store(a)
                o_low(HEADS - 1)
                mods_for(1, NA_PRE)
                mods_for(2, NA_PRE)
                for n in range(13, 17):
                    lo(0, n)
                for k in range(KD):
                    dve.wait_ge(proj_done[0], k // 2 + 1)
                    residual(k // 2, k, mods[:, 0, 16 + k:17 + k]).then_inc(resid, 1)

            def conv_pair(i):
                cs = (2 * i, 2 * i + 1)
                for c in cs:
                    a = c % 2
                    dve.wait_ge(glu_sig, c + 1)
                    v.scalar_tensor_tensor(out=upad[:, c, PADL:], in0=PS[:, (2 * i) % 4, a * T:(a + 1) * T],
                                           scalar=vcol("pw1_b", c), in1=sig[:, c % 4, :], op0=ALU.add,
                                           op1=ALU.mult).then_inc(glu_ready, 1)
                dve.wait_ge(glu_ready, cs[1] + 1)
                for c in cs:
                    j = PE_TAPS
                    tick(v.tensor_scalar(cacc[:, c, :], upad[:, c, j:j + T], vcol("dw_w", c * TAPS + j),
                                         vcol("dw_b", c), ALU.mult, ALU.add))
                for j in range(PE_TAPS + 1, TAPS):
                    for c in cs:
                        dve.wait_ge(dve_seq, seq[0] - 1)
                        tick(v.scalar_tensor_tensor(out=cacc[:, c, :], in0=upad[:, c, j:j + T],
                                                    scalar=vcol("dw_w", c * TAPS + j), in1=cacc[:, c, :],
                                                    op0=ALU.mult, op1=ALU.add))
                dve.wait_ge(dve_seq, seq[0])
                for c in cs:
                    dve.wait_ge(conv_pe, c + 1)
                    v.tensor_tensor(cacc[:, c, :], cacc[:, c, :], PS[:, 5 + c % 2, 0:T],
                                    ALU.add).then_inc(conv_ready, 1)

            def mixer1():
                step(v.memset(upad[:, :, 0:PADL], 0.0))
                norm(2)
                split_x(hT, xh_ready, 4, xl_ready)
                for n in range(5):
                    lo(1, n)
                for i in range(4):
                    for n in (2 * i + 5, 2 * i + 6):
                        if n < 8:
                            lo(1, n)
                    conv_pair(i)
                for n, a in enumerate(ADA_ORDER[1]):
                    if a not in POOL_ADA:
                        ada_sum(1, a)
                    if n:
                        ada_store(ADA_ORDER[1][n - 1])
                ada_store(ADA_ORDER[1][-1])
                mods_for(3, 24)
                step(v.tensor_tensor(gate_bias, mods[:, 1, 16:24], vcol("pw2_b", 0, KD), ALU.mult))
                dve.wait_ge(ln_mean, 1)
                for i in range(4):
                    ks = slice(2 * i, 2 * i + 2)
                    v.tensor_tensor(cacc[:, ks, :], cacc[:, ks, :], bc(rstd[:, T:2 * T].unsqueeze(1), [P, 2, T]),
                                    ALU.subtract).then_inc(ln_centred, 1)
                for k in range(KD):
                    tick(v.tensor_scalar(XT[:, k, :], XT[:, k, :], gate_bias[:, k:k + 1], None, ALU.add))
                dve.wait_ge(ln_root, 1)
                step(v.reciprocal(rstd[:, 0:T], root[:, 0:T]))
                for i in range(4):
                    ks = slice(2 * i, 2 * i + 2)
                    v.tensor_tensor(cacc[:, ks, :], cacc[:, ks, :], bc(rstd[:, 0:T].unsqueeze(1), [P, 2, T]),
                                    ALU.mult).then_inc(ln_scaled, 1)
                split_x(cacc, xh_ready, 8, xl_ready)
                for n in range(8, 12):
                    lo(1, n)
                for k in range(KD):
                    dve.wait_ge(proj_done[1], k // 2 + 1)
                    residual(k // 2, k, mods[:, 1, 16 + k:17 + k]).then_inc(resid, 1)

            def route(l):
                def buf(at, *shape):
                    n = 1
                    for s_ in shape:
                        n *= s_
                    b = small[:, at:at + n]
                    return b if len(shape) == 1 else b.rearrange("p (a b) -> p a b", b=shape[1])
                G8 = NT * GRP
                score, biased = buf(0, NT, E), buf(32, NT, E)
                b4 = buf(32, G8, PER)
                dve.wait_ge(scores_ready, l + 1)
                step(v.tensor_tensor(biased, score, bc(rb[:].unsqueeze(1), [P, NT, E]), ALU.add))
                hi2, lo2 = buf(64, G8, 2), buf(80, G8, 2)
                v.tensor_tensor(hi2, b4[:, :, 0::2], b4[:, :, 1::2], ALU.max)
                step(v.tensor_tensor(lo2, b4[:, :, 0::2], b4[:, :, 1::2], ALU.min))
                top1, t2a, t2b, gs = buf(96, G8), buf(104, G8), buf(112, G8), buf(120, G8)
                v.tensor_tensor(top1, hi2[:, :, 0], hi2[:, :, 1], ALU.max)
                v.tensor_tensor(t2a, hi2[:, :, 0], hi2[:, :, 1], ALU.min)
                step(v.tensor_tensor(t2b, lo2[:, :, 0], lo2[:, :, 1], ALU.max))
                step(v.tensor_tensor(t2a, t2a, t2b, ALU.max))
                step(v.tensor_tensor(gs, top1, t2a, ALU.add))
                gs2, gmax, eq, eqi = buf(120, NT, GRP), buf(128, NT), buf(136, NT, GRP), buf(144, NT, GRP)
                step(v.tensor_reduce(gmax, gs2, AX, ALU.max))
                step(v.tensor_tensor(eq, gs2, bc(gmax.unsqueeze(2), [P, NT, GRP]), ALU.is_equal))
                step(v.tensor_tensor(eqi, eq, con_("first4", 2 * GRP).rearrange("p (a b) -> p a b", b=GRP), ALU.mult))
                step(v.tensor_reduce(gmax, eqi, AX, ALU.max))
                step(v.tensor_tensor(eq, eqi, bc(gmax.unsqueeze(2), [P, NT, GRP]), ALU.is_equal))
                gt = small[:, 768:768 + G8 * 16].rearrange("p (g i j) -> p g i j", i=PER, j=PER)
                et = small[:, 896:896 + G8 * 16].rearrange("p (g i j) -> p g i j", i=PER, j=PER)
                vj = bc(b4.unsqueeze(2), [P, G8, PER, PER])
                vi = bc(b4.unsqueeze(3), [P, G8, PER, PER])
                v.tensor_tensor(gt, vj, vi, ALU.is_gt)
                step(v.tensor_tensor(et, vj, vi, ALU.is_equal))
                step(v.tensor_tensor(et.rearrange("p g i j -> p g (i j)"), et.rearrange("p g i j -> p g (i j)"),
                                     bc(con_("tri4", 16).unsqueeze(1), [P, G8, 16]), ALU.mult))
                step(v.tensor_tensor(gt, gt, et, ALU.add))
                rank = buf(160, G8, PER)
                step(v.tensor_reduce(rank, gt, AX, ALU.add))
                picks = buf(256, NT, E)
                p4 = buf(256, G8, PER)
                step(v.tensor_scalar(rank, rank, 1.5, None, ALU.is_lt))
                v.tensor_tensor(p4, rank, bc(buf(136, G8).unsqueeze(2), [P, G8, PER]),
                                ALU.mult).then_inc(picks_ready, 1)
                dve.wait_ge(picks_ready, l + 1)
                w, ws = buf(288, NT, E), buf(320, NT)
                step(v.tensor_tensor(w, score, picks, ALU.mult))
                step(v.tensor_reduce(ws, w, AX, ALU.add))
                step(v.reciprocal(ws, ws))
                step(v.tensor_tensor(w, w, bc(ws.unsqueeze(2), [P, NT, E]), ALU.mult))
                dve.wait_ge(counts_done, l + 1)
                c16, n16 = small[0:E, 512:512 + P], small[0:E, 640:641]
                cum = buf(336, NT, E)
                v.tensor_copy(cum, PS[:, 1, 0:2 * E].rearrange("p (t e) -> p t e", e=E))
                step(v.tensor_copy(c16, PS[0:E, 1, 64:64 + P]))
                v.tensor_scalar(n16, c16[:, 0:1], P + 0.5, 1.0, ALU.is_gt, ALU.add).then_inc(count_rows, 1)
                dve.wait_ge(offs_done, l + 1)
                pm = buf(368, NT, E)
                step(v.tensor_tensor(pm, cum, bc(PS[:, 2, 0:E].unsqueeze(1), [P, NT, E]), ALU.add))
                step(v.scalar_tensor_tensor(out=pm, in0=pm, scalar=1.0, in1=picks, op0=ALU.add, op1=ALU.mult))
                sa, sb_, wa, wb = buf(400, NT), buf(404, NT), buf(408, NT), buf(412, NT)
                v.tensor_reduce(sa, pm, AX, ALU.max)
                step(v.tensor_reduce(sb_, pm, AX, ALU.add))
                step(v.tensor_tensor(sb_, sb_, sa, ALU.subtract))
                iota = con_("iota", SLOTS)
                pf = perm.bitcast(F32)
                for t in range(NT):
                    step(v.tensor_scalar(perm[:, t, :], iota, sa[:, t:t + 1], None, ALU.is_equal))
                    v.scalar_tensor_tensor(out=perm[:, t, :], in0=iota, scalar=sb_[:, t:t + 1], in1=pf[:, t, :],
                                           op0=ALU.is_equal, op1=ALU.add).then_inc(perm_ready, 1)
                off, beg, end = small[0:E, 660:661], small[0:E, 661:662], small[0:E, 662:663]
                v.tensor_copy(small[0:E, 660:662], PS[0:E, 2, 64:66])
                step(v.tensor_copy(buf(664, 1)[0:E], n16))
                step(v.tensor_tensor(end, beg, n16, ALU.add))
                js = con_("iota", MAXB + 1, 0, E)
                b0 = small[0:E, 672:672 + MAXB + 1]
                t0 = small[0:E, 704:704 + MAXB + 1]
                tb = small[0:E, 1024:1024 + NTAB]
                step(v.tensor_scalar(b0, js, -1.0, None, ALU.add))
                step(v.tensor_scalar(t0, b0, end[:, 0:1], None, ALU.is_gt))
                step(v.tensor_copy(tb[:, 0:MAXB + 1], t0))
                step(v.tensor_scalar(t0, b0, beg[:, 0:1], None, ALU.is_gt))
                step(v.tensor_tensor(t0, t0, tb[:, 0:MAXB + 1], ALU.subtract))
                step(v.tensor_scalar(b0, b0, beg[:, 0:1], -1.0, ALU.subtract, ALU.add))
                step(v.tensor_scalar(b0, b0, float(P), off[:, 0:1], ALU.mult, ALU.add))
                step(v.tensor_tensor(tb[:, MAXB + 1:2 * MAXB + 2], b0, t0, ALU.mult))
                v.tensor_scalar(tb[:, 0:1], n16, 2.0 / E, None, ALU.subtract).then_inc(slots_ready, 1)
                dve.wait_ge(rows_done, l + 1)
                v.tensor_copy(tab[0:1, l, :], PS[0:1, 3, 0:NTAB]).then_inc(table_ready, 1)
                m = buf(416, NT, E)
                for s_, w_ in ((sa, wa), (sb_, wb)):
                    step(v.tensor_tensor(m, pm, bc(s_.unsqueeze(2), [P, NT, E]), ALU.is_equal))
                    step(v.tensor_tensor(m, m, w, ALU.mult))
                    step(v.tensor_reduce(w_, m, AX, ALU.add))
                for t in range(NT):
                    wp = wperm[:, t, :]
                    step(v.tensor_scalar(wp, iota, sa[:, t:t + 1], wa[:, t:t + 1], ALU.is_equal, ALU.mult))
                    tmp = rstd if t == 0 else root
                    step(v.tensor_scalar(tmp[:], iota, sb_[:, t:t + 1], wb[:, t:t + 1], ALU.is_equal, ALU.mult))
                    v.tensor_tensor(wp, wp, tmp[:], ALU.add).then_inc(wperm_ready, 1)

            def moe(l):
                ph = 2 * l + 1
                norm(ph)
                for i in range(4):
                    t, half = divmod(i, 2)
                    dve.wait_ge(htokh_ready, 4 * l + i + 1)
                    c = slice(half * 512, (half + 1) * 512)
                    v.tensor_tensor(htokl[:, t, c], PS[:, 5 + i % 2, :], htokh[:, t, c].bitcast(F32),
                                    ALU.subtract).then_inc(htokl_ready, 1)
                route(l)
                dve.wait_ge(norm_sum, (2 * l + 1) + 1)
                step(v.memset(hgT[:, :, SLOTS:], 0.0))
                for i in range(2):
                    dve.wait_ge(wpt_done, 2 * l + i + 1)
                    v.tensor_copy(wpT[:, 2 * i:2 * i + 2, :], PS[:, 1 + i, :].rearrange("p (s t) -> p s t", t=T)
                                  ).then_inc(wpt_stored, 1)
                dve.wait_ge(gather_stored, 8 * l + KD)
                inner = inner_blocks(dve, l)

                def lo_m(i, j):
                    raw, h, l_ = moe_piece(i)
                    dve.wait_ge(hi_ready[ph], nth(j, 6, i - 5))
                    v.tensor_tensor(l_, raw, h.bitcast(F32), ALU.subtract).then_inc(lo_ready[ph], 1)

                def slot_in(j):
                    dve.wait_ge(hch_ready[l], nth(j))
                    s0 = block_slot(dve, l, j)
                    v.tensor_tensor(hcl, hgT[:, :, bass.ds(s0, P)], hch.bitcast(F32),
                                    ALU.subtract).then_inc(hcl_ready[l], 1)

                def y_out(j):
                    dve.wait_ge(ytt_done[l], nth(j, 2))
                    s0 = block_slot(dve, l, j)
                    v.tensor_copy(yT[:, 4:8, bass.ds(s0, P)],
                                  PS[:, 6, :].rearrange("p (m c) -> p m c", c=P)).then_inc(ytd_stored[l], 1)

                def one(j, first, last):
                    for i in (2, 3, 4):
                        lo_m(i, j)
                    dve.wait_ge(silu_done[l], nth(j))
                    dve.wait_ge(piece_used[ph], nth(j, 6, -2))
                    if not first:
                        dve.wait_ge(att_done[l], nth(j, 1, -1))
                    v.tensor_tensor(act, PS[:, 1, :], sg, ALU.mult).then_inc(act_ready[l], 1)
                    if not first:
                        y_out(after(j, -1))
                    for half in range(2):
                        dve.wait_ge(ath_ready[l], nth(j, 2, half - 1))
                        if half == 0:
                            dve.wait_ge(ath_ready[l], nth(j, 2))
                        hs = slice(2 * half, 2 * half + 2)
                        v.tensor_tensor(aTl[:, hs, :],
                                        PS[:, 2, 256 * half:256 * half + 256].rearrange("p (m c) -> p m c", c=P),
                                        aTh[:, hs, :].bitcast(F32), ALU.subtract).then_inc(atl_ready[l], 1)
                    lo_m(5, j)
                    if not last:
                        slot_in(after(j))
                        lo_m(0, after(j))
                        lo_m(1, after(j))

                slot_in((None, 1))
                lo_m(0, (None, 1))
                lo_m(1, (None, 1))
                one((None, 1), True, False)
                with dve.Fori(0, inner) as r:
                    one((r, 2), False, False)
                final = (inner, 2)
                one(final, False, True)
                y_out(final)
                for k in range(KD):
                    dve.wait_ge(moe_done, 4 * l + k // 2 + 1)
                    residual(k // 2, k, mods[:, l, 40 + k:41 + k]).then_inc(resid, 1)

            mixer0()
            moe(0)
            mixer1()
            moe(1)


def kernel(**inputs):
    import numpy as np
    import concourse.bacc as bacc
    from concourse.bass_utils import run_bass_kernel_spmd

    f = {k: np.asarray(a) for k, a in inputs.items()}

    def cols(a):
        return a.reshape(-1, P).T

    def rope2(a):
        return np.concatenate([a, a]).reshape(P, 1)

    half = ROPE // 2
    inv_freq = (1.0 / (10000.0 ** (np.arange(half, dtype=np.float32) * np.float32(2.0 / ROPE)))).astype(np.float32)
    dw = f["conv_dw_w"][0]
    vec = np.concatenate([
        cols(f["norm1_g"]), cols(f["norm2_g"]), cols(f["ada_b"]), cols(f["mla_q_norm_g"]), cols(f["mla_kv_norm_g"]),
        f["mla_qk_q_g"][0, :NOPE].reshape(P, 1), f["mla_qk_k_g"][0, :NOPE].reshape(P, 1),
        rope2(f["mla_qk_q_g"][0, NOPE:]), rope2(f["mla_qk_k_g"][0, NOPE:]),
        np.tile(inv_freq, 4).reshape(P, 1),
        cols(f["conv_pw1_b"]), cols(f["conv_dw_b"]), cols(f["conv_ln_g"]), cols(f["conv_ln_b"]),
        cols(f["conv_pw2_b"]), cols(f["c"]),
        dw.T.reshape(KD, P, TAPS).transpose(1, 0, 2).reshape(P, KD * TAPS),
        f["router_w"].reshape(KD, P, E).transpose(1, 0, 2).reshape(P, KD * E),
    ], axis=1)
    i = np.arange(P)
    causal = np.where(i[None, :] <= i[:, None], 0.0, -1e30)
    rot1 = np.zeros((ROPE, ROPE))
    for a in range(half):
        rot1[a + half, a] = -1.0
        rot1[a, a + half] = 1.0
    rot = np.zeros((P, P))
    rot[:ROPE, :ROPE] = rot1
    rot[ROPE:, ROPE:] = rot1
    e = np.arange(P)[:, None]
    tri16 = np.concatenate([e < np.arange(E)[None, :], e <= np.arange(E)[None, :]], axis=1)
    tri4 = (np.arange(PER)[None, :] < np.arange(PER)[:, None]).astype(np.float32).reshape(1, -1)
    head = np.arange(HEADS)
    hsel = np.tile(np.eye(HEADS).reshape(1, -1), (P, 1))
    kpesel = np.tile((i < ROPE)[:, None], (1, HEADS))
    psel = np.concatenate([head[None, :] == 2 * g + (i[:, None] >= ROPE) for g in range(PAIRS)], axis=1)
    con = np.concatenate([
        np.eye(P), np.ones((P, P)), i[:, None] < i[None, :],
        np.concatenate([causal, np.zeros((P, P)), causal], axis=1), rot,
        np.tile(np.arange(1, SLOTS + 1)[None, :], (P, 1)), hsel, kpesel, psel, tri16,
        np.tile(np.array([4, 3, 2, 1, 4, 3, 2, 1])[None, :], (P, 1)), np.tile(tri4, (P, 1)),
    ], axis=1).astype(np.float32)
    uq = f["mla_w_uq"][0].reshape(QR, HEADS, QK)
    arrays = {
        "xT": f["x"][0].T.reshape(KD, P, T).transpose(1, 0, 2),
        "vec": vec,
        "con": con,
        "rbias": np.tile(f["router_bias"][None, :], (P, 1)),
        "pos": np.tile(f["positions"], (P, 1)),
        "ada_w": f["ada_w"],
        "w_dqkv": f["mla_w_dqkv"][0],
        "w_uq": np.concatenate([uq[:, :, :NOPE].reshape(QR, -1), uq[:, :, NOPE:].reshape(QR, -1)], axis=1),
        "w_ukv": f["mla_w_ukv"][0],
        "w_o": f["mla_w_o"][0],
        "pw1": f["conv_pw1_w"][0],
        "pw2": f["conv_pw2_w"][0],
        "w_gate": f["moe_w_gate"],
        "w_up": f["moe_w_up"],
        "w_down": f["moe_w_down"],
    }
    nc = bacc.Bacc("TRN2", target_bir_lowering=False, num_devices=1)
    args = []
    for name in arrays:
        arrays[name] = np.ascontiguousarray(arrays[name])
        args.append(nc.dram_tensor(name, arrays[name].shape, mybir.dt.from_np(arrays[name].dtype),
                                   kind="ExternalInput").ap())
    out = nc.dram_tensor("out", (P, KD, T), F32, kind="ExternalOutput").ap()
    build(nc, *args, out)
    r = run_bass_kernel_spmd(nc, [arrays], core_ids=[0])
    o = r.results[0]["out"]
    return np.ascontiguousarray(o.transpose(1, 0, 2).reshape(D, T).T).reshape(1, T, D)
```

```python
from contextlib import ExitStack

import concourse.bass as bass
from concourse import mybir

P = 128
D = 1024
T = 256
KD = D // P
NT = T // P
HEADS = 8
PAIRS = HEADS // 2
NOPE = 128
ROPE = 64
QK = NOPE + ROPE
VD = 128
QR = 768
KVR = 256
KQ = QR // P
KKV = KVR // P
TAPS = 31
PADL = TAPS - 1
E = 16
GRP = 4
PER = E // GRP
FF = 512
KF = FF // P
SLOTS = 2 * T
SB = SLOTS // P
EPS = 1e-6
SCALE = float(QK) ** -0.5

RING = 3
SLOT_F = KD * 576
PIECE = 2048
PBUF = 3
MAXB = E + 3
NTAB = 2 * MAXB + 2
NWORK = 13840
PE_TAPS = 13

VC = {}
_at = 0
for _name, _n in (("norm1", 2 * KD), ("norm2", 2 * KD), ("ada_b", 2 * 48), ("q_norm", KQ), ("kv_norm", KKV),
                  ("gq_nope", 1), ("gk_nope", 1), ("gq_rope", 1), ("gk_rope", 1), ("inv_freq", 1),
                  ("pw1_b", 2 * KD), ("dw_b", KD), ("ln_g", KD), ("ln_b", KD), ("pw2_b", KD), ("c", KD),
                  ("dw_w", KD * TAPS), ("router_w", KD * E)):
    VC[_name] = _at
    _at += _n
NVEC = _at

CC = {}
_at = 0
for _name, _n in (("ident", P), ("ones", P), ("before", P), ("causal", 3 * P), ("rot", P), ("iota", SLOTS),
                  ("hsel", HEADS * HEADS), ("kpesel", HEADS), ("psel", PAIRS * HEADS),
                  ("tri16", 2 * E), ("first4", 2 * GRP), ("tri4", PER * PER),
                  ("expert", 1)):
    CC[_name] = _at
    _at += _n
NCON = _at

ALU = mybir.AluOpType
ACT = mybir.ActivationFunctionType
AX = mybir.AxisListType.X
F32 = mybir.dt.float32
I32 = mybir.dt.int32
F32R = mybir.dt.float32r

TWO_PI = 6.283185307179586
PI_A = 6.28125
PI_B = 0.0019350051879882812
PI_C = TWO_PI - PI_A - PI_B
MAGIC = 12582912.0

POOL_ADA = [4, 6, 8, 10, 12, 14, 16, 18, 19, 20, 22]
DVE_ADA = [a for a in range(24) if a not in POOL_ADA]
ADA_GROUPS = ((0, 4), (4, 12), (12, 17), (17, 24))
ADA_ORDER = (0, 1, 2, 3, 5, 4, 7, 6, 9, 8, 11, 10, 13, 12, 15, 14, 16, 17, 18, 19, 20, 21, 22, 23)
ADA_MIXER1 = 18


def pieces_of(u):
    return 3 if u == ("dqkv", 1) else 2


def unit_plan():
    def ada(*a):
        return [("ada", i) for i in a]
    first = ada(0, 1, 2, 3) + [("dqkv", 0), ("dqkv", 1)] + ada(4, 5) + [("ukv", 0)] + ada(6, 7) + [("uq", 0)]
    first += ada(8) + [("uq", 1)] + ada(9) + [("uq", 2)] + ada(10, 11) + [("wo", 0)] + ada(12, 13)
    first += [("wo", 1)] + ada(14, 16, 15)
    second = [("pw1", 0)] + ada(17, 18) + [("pw1", 1)] + ada(19) + [("pw1", 2)] + ada(20) + [("pw1", 3)] + ada(21, 22, 23)
    second += [("pw2", 0), ("pw2", 1)]
    return first, second


def build(nc, xT, vec, con, rbias, pos, ada_w, w_dqkv, w_uq, w_ukv, w_o, pw1, pw2, w_gate, w_up, w_down, out):
    ctx = ExitStack()
    with ctx:
        def sb(name, shape, dt=F32):
            return ctx.enter_context(nc.sbuf_tensor(name, shape, dt))

        def sem(name):
            return ctx.enter_context(nc.semaphore(name))

        PS = ctx.enter_context(nc.psum_tensor("ps", [P, 8, 512], F32))
        ring = [sb(f"ring{s}", [P, SLOT_F]) for s in range(RING)]
        piece_hi = [sb(f"piece_hi{s}", [P, PIECE], F32R) for s in range(PBUF)]
        piece_lo = [sb(f"piece_lo{s}", [P, PIECE], F32R) for s in range(PBUF)]
        RX = sb("acts_split", [P, 2 * KD * T], F32R)
        XT = sb("XT", [P, KD, T])
        hT = sb("hT", [P, KD, T])
        V = sb("vecs", [P, NVEC])
        C = sb("consts", [P, NCON])
        rb = sb("router_bias", [P, E])
        mods = sb("mods", [P, 2, 48])
        gsc = sb("norm_gain", [P, 4, KD])
        sc = sb("silu_c", [P, KD])
        rstd = sb("rstd", [P, 512])
        root = sb("root", [P, 512])
        eps = sb("eps", [P, 2])
        tab = sb("block_table", [1, 2, NTAB], I32)
        pool_acc = sb("pool_acc", [P, 3, 512])
        WORK = sb("work", [P, NWORK])

        def view(at, *shape, of=None):
            n = 1
            for s in shape:
                n *= s
            v = (WORK if of is None else of)[:, at:at + n]
            if len(shape) == 2:
                v = v.rearrange("p (a b) -> p a b", b=shape[1])
            if len(shape) == 3:
                v = v.rearrange("p (a b c) -> p a b c", b=shape[1], c=shape[2])
            return v

        xh, xl = view(0, KD, T, of=RX), view(KD * T, KD, T, of=RX)

        def norm_squares(n):
            return view(5120 if n == 2 else 0, KD, T)

        sq = view(0, KD, T)
        sq_rope = view(2048, PAIRS, T)
        kpe_sq = view(2048, T)
        latT = view(3072, 9, T)
        kn = view(5376, HEADS, T)
        kr = view(3072, PAIRS, T)
        vt = view(7424, NT, HEADS * VD)
        qn = view(9472, HEADS, T)
        qr = view(11520, PAIRS, T)
        sin_t, cos_t = view(12544, T), view(12800, T)
        ropetmp = view(13056, 2, T)
        krope = view(13568, T)
        posi = krope.bitcast(I32)
        kq_rstd = view(13824, 16)
        attn_s = view(0, 2, 3 * P)
        attn_p = view(768, 2, 3 * P)
        attn_pt = view(1536, 2, 3 * P)
        attn_sm = view(2304, 2, 8)
        hgT = view(0, KD, SLOTS + P)
        yT = view(5120, KD, SLOTS + P)
        small = view(5120, 2048)
        wperm = view(7168, NT, SLOTS)
        ysl = view(0, SB, D)
        wpT = view(10240, SB, T)
        sg = view(11264, FF)
        act = view(11776, FF)
        yb = view(12288, D)
        perm = view(0, NT, SLOTS, of=piece_hi[PBUF - 1])
        hch, hcl = view(0, KD, P, of=RX), view(KD * P, KD, P, of=RX)
        aTh, aTl = view(2048, KF, P, of=RX), view(2560, KF, P, of=RX)
        htokh, htokl = view(0, NT, D, of=RX), view(2048, NT, D, of=RX)
        upad = view(2048, KD, PADL + T)
        cacc = view(4352, KD, T)
        sig = view(6400, 4, T)
        diag = view(7424, 2, PE_TAPS, P)
        gate_bias = view(7424 + 2 * PE_TAPS * P, KD)
        hflat = hT[:].rearrange("p k t -> p (k t)")

        def ada_acc(a):
            if a in POOL_ADA:
                return pool_acc[:, POOL_ADA.index(a) % 2, :]
            b = DVE_ADA.index(a) % 2
            return WORK[:, 9472 + 512 * b:9472 + 512 * b + 512] if a < 4 else hflat[:, 512 * b:512 * b + 512]

        def vcol(name, i=0, n=1):
            return V[:, VC[name] + i:VC[name] + i + n]

        def con_(name, n=P, at=0, rows=P):
            return C[0:rows, CC[name] + at:CC[name] + at + n]

        ident, ones = con_("ident"), con_("ones")
        LT = range(2)

        def sems(names, times=None):
            names = names.split()
            return [sem(n) if times is None else [sem(f"{n}{i}") for i in range(times)] for n in names]

        x_in, vec_in, con_in, rb_in, pos_in = sems("x_in vec_in con_in rb_in pos_in")
        landed = [[sem(f"landed{ph}_{s}") for s in range(RING)] for ph in range(4)]
        hi_ready, lo_ready, piece_used = sems("hi_ready lo_ready piece_used", 4)
        raw_used, pool_used = sems("raw_used pool_used", 2)
        ada_summed, ada_pooled = sems("ada_summed ada_pooled")
        silu_c, ada_done, ada_rows, ada_turned, ada_stored, mods_ready = sems(
            "silu_c ada_done ada_rows ada_turned ada_stored mods_ready")
        dve_seq, pool_seq, eps_ready = sems("dve_seq pool_seq eps_ready")
        resid = sem("residual_updated")
        norm_sq, norm_sum, norm_root, norm_scaled, h_ready, xh_ready, xl_ready = sems(
            "norm_sq norm_sum norm_root norm_scaled h_ready xh_ready xl_ready")
        angles, tables = sems("rope_angles rope_tables")
        item_done, item_stored = sems("item_done item_stored")
        lat_sum, lat_root, lat_ready, lath_ready, latl_ready = sems("lat_sum lat_root lat_ready lath_ready latl_ready")
        kpe_scaled, kpe_rot, krope_ready = sems("kpe_scaled kpe_rot krope_ready")
        k_sum, k_root, k_recip, bc_done, bc_used = sems("k_sum k_root k_recip bc_done bc_used")
        q_sum, q_root, q_recip, q_turned, rq_ready, q_rot, q_ready = sems(
            "q_sum q_root q_recip q_turned rq_ready q_rot q_ready")
        s_done, s_masked, s_max, p_exp, p_ready, pt_done, pt_stored, o_done, oh_ready, ol_ready = sems(
            "s_done s_masked s_max p_exp p_ready pt_done pt_stored o_done oh_ready ol_ready")
        proj_done = sems("wo_done pw2_done")
        glu_done, glu_sig, glu_ready, diag_ready, conv_pe, conv_ready = sems(
            "glu_done glu_sig glu_ready diag_ready conv_pe conv_ready")
        ln_sum, ln_mean, ln_centred, ln_sq, ln_var, ln_root, ln_scaled, ln_silu = sems(
            "ln_sum ln_mean ln_centred ln_sq ln_var ln_root ln_scaled ln_silu")
        logits_done, scores_ready, picks_ready, counts_done, count_rows, offs_done, slots_ready, rows_done, table_ready = sems(
            "logits_done scores_ready picks_ready counts_done count_rows offs_done slots_ready rows_done table_ready")
        half_high, half_low, htok_done, htokh_ready, htokl_ready, perm_ready, wperm_ready, gather_done, gather_stored, wpt_done, wpt_stored = sems(
            "half_high half_low htok_done htokh_ready htokl_ready perm_ready wperm_ready gather_done gather_stored wpt_done wpt_stored")
        hch_ready, hcl_ready, silu_done, act_ready, att_done, ath_ready, atl_ready = sems(
            "hch_ready hcl_ready silu_done act_ready att_done ath_ready atl_ready", 2)
        y_stored, ytt_done, yta_stored, ytd_stored = sems("y_stored ytt_done yta_stored ytd_stored", 2)
        ysl_done, ysl_stored, moe_done = sems("ysl_done ysl_stored moe_done")
        stored = sem("out_stored")

        units = unit_plan()
        at_of = {u: n for ph in (0, 1) for n, u in enumerate(units[ph])}
        pieces = [[(u, i) for u in units[ph] if u[0] != "ada" for i in range(pieces_of(u))] for ph in (0, 1)]

        def unit_shape(kind, i):
            if kind == "dqkv":
                return (KD, (512, 576)[i])
            return {"ada": (KD, 512), "ukv": (2, 2048), "uq": (KQ, 512), "wo": (KD, 512), "pw1": (KD, 512),
                    "pw2": (KD, 512)}[kind]

        def unit_ap(kind, i):
            k, n = unit_shape(kind, i)
            return ring[at_of[(kind, i)] % RING][:, 0:k * n].rearrange("p (k n) -> p k n", n=n)

        def unit_source(kind, i):
            if kind == "ada":
                l, j = divmod(i, 12)
                return ada_w[l].rearrange("(k p) n -> p k n", p=P)[:, :, j * 512:(j + 1) * 512]
            w = {"dqkv": w_dqkv, "ukv": w_ukv, "uq": w_uq, "wo": w_o, "pw1": pw1, "pw2": pw2}[kind]
            w = w.rearrange("(k p) n -> p k n", p=P)
            n = unit_shape(kind, i)[1]
            return w[:, :, 512 * i:512 * i + n]

        def piece_cols(kind, i, j):
            if kind == "dqkv" and i == 1:
                return (0, 256), (256, 512), (512, 576)
            return {"ukv": ((0, 1024), (1024, 2048))}.get(kind, ((0, 256), (256, 512)))

        def piece_raw(kind, i, j):
            a, b = piece_cols(kind, i, j)[j]
            return unit_ap(kind, i)[:, :, a:b]

        def piece_bufs(n, k, w):
            return tuple(x[n % PBUF][:, 0:k * w].rearrange("p (k n) -> p k n", n=w) for x in (piece_hi, piece_lo))

        def mixer_piece(mx, n):
            (kind, i), j = pieces[mx][n]
            raw = piece_raw(kind, i, j)
            if raw.shape[2] == ROPE:
                raw = raw.unsqueeze(2).to_broadcast([P, KD, 2, ROPE])
                hi, lo = (x.rearrange("p k (a n) -> p k a n", n=ROPE) for x in piece_bufs(n, KD, P))
            else:
                hi, lo = piece_bufs(n, raw.shape[1], raw.shape[2])
            return raw, hi, lo, (kind, i), j

        def moe_piece(j, i, end=False):
            u, q = (0, i) if end else divmod(i, 4)
            if u < 2 and not end:
                raw = ring[u][:, 0:KD * FF].rearrange("p (k n) -> p k n", n=FF)[:, 2 * q:2 * q + 2, :]
            else:
                raw = ring[u][:, 0:KF * D].rearrange("p (k n) -> p k n", n=D)[:, 2 * (q % 2):2 * (q % 2) + 2,
                                                                             512 * (q // 2):512 * (q // 2) + 512]
            b = (i if j[0] is None and j[1] == 1 else i + 2) % (2 * PBUF)
            at = (b % 2) * (PIECE // 2)
            hi, lo = (x[b // 2][:, at:at + PIECE // 2].rearrange("p (k n) -> p k n", n=512)
                      for x in (piece_hi, piece_lo))
            return raw, hi, lo

        def upto(j, i, less=0):
            return i + 1 - less if j[0] is None and j[1] == 1 else nth(j, 12, i - 15 - less)

        expert_w = (w_gate, w_up, w_down)
        WHY = "computed from at most 512 picks of 16 experts"

        def inner_blocks(eng, l):
            return nc.s_assert_within(eng.value_load(tab[0:1, l, 0:1], min_val=E - 3, max_val=MAXB - 3), E - 3,
                                      MAXB - 3, skip_runtime_bounds_check_because=WHY)

        def nth(j, per=1, more=0):
            r, o = j
            if r is None:
                return per * o + more
            return (r * per if per > 1 else r) + (per * o + more)

        def after(j, n=1):
            return (j[0], j[1] + n)

        def block_slot(eng, l, j):
            return eng.value_load(tab[0:1, l, bass.ds(nth(j) + (MAXB + 1), 1)] if j[0] is not None else
                                  tab[0:1, l, j[1] + MAXB + 1:j[1] + MAXB + 2], min_val=0, max_val=SLOTS)

        HTOK_BANKS = (5, 6, 4, 3)
        CONV_BANKS = (5, 6, 4, 5)

        block = ctx.enter_context(nc.Block())

        @block.sync
        def _(sp):
            def wait_consumed(mx, n):
                ph = 2 * mx
                us = units[mx]
                if us[n][0] == "ada" and us[n][1] in POOL_ADA:
                    sp.wait_ge(pool_used[mx], sum(u[0] == "ada" and u[1] in POOL_ADA for u in us[:n + 1]))
                else:
                    sp.wait_ge(raw_used[mx], sum(not (u[0] == "ada" and u[1] in POOL_ADA) for u in us[:n + 1]))

            def mixer_units(mx):
                ph = 2 * mx
                if mx:
                    inner = inner_blocks(sp, 0)
                for n, (kind, i) in enumerate(units[mx]):
                    s = n % RING
                    if n >= RING:
                        wait_consumed(mx, n - RING)
                    elif mx:
                        sp.wait_ge(lo_ready[1], upto((inner, 3), 4 * s + 3) if s else upto((inner, 4), 3))
                    if kind == "pw1":
                        src = pw1.rearrange("(k p) (h n) -> h p k n", p=P, h=2)[:, :, :, 256 * i:256 * i + 256]
                        for half in range(2):
                            sp.dma_start(unit_ap(kind, i)[:, :, 256 * half:256 * half + 256],
                                         src[half]).then_inc(landed[ph][s], 16)
                    else:
                        sp.dma_start(unit_ap(kind, i), unit_source(kind, i)).then_inc(landed[ph][s], 16)
                    if not mx and n == 0:
                        sp.dma_start(XT[:], xT).then_inc(x_in, 16)
                        sp.dma_start(C[:], con).then_inc(con_in, 16)
                        sp.dma_start(posi, pos).then_inc(pos_in, 16)
                        sp.dma_start(rb[:], rbias).then_inc(rb_in, 16)

            def expert_unit(l, e, i, half, slot=None):
                src = expert_w[i][l].rearrange("e (k p) n -> e p k n", p=P)
                src = src[bass.ds(e, 1)].rearrange("e p k n -> (e p) k n") if not isinstance(e, int) else src[e]
                k, n = (KD, FF) if i < 2 else (KF, D)
                slot = i if slot is None else slot
                dst = ring[slot][:, 0:k * n].rearrange("p (k n) -> p k n", n=n)
                part = ((slice(0, P), slice(4 * half, 4 * half + 4), slice(0, FF)) if i < 2 else
                        (slice(0, P), slice(0, KF), slice(512 * half, 512 * half + 512)))
                sp.dma_start(dst[part], src[part]).then_inc(landed[2 * l + 1][slot], 16)

            def moe_units(l):
                last = len(units[l])
                for i in range(RING):
                    wait_consumed(l, max(n for n in range(last) if n % RING == i))
                    for half in range(2):
                        expert_unit(l, 0, i, half)
                def step(j, final=False):
                    def expert(j):
                        if j[0] is None:
                            return j[1] - 1
                        return sp.value_load(tab[0:1, l, bass.ds(nth(j), 1)], min_val=0, max_val=E - 1)
                    if not final:
                        e = expert(after(j))
                    for i in range(3):
                        if (i == 2 and j[0] is None and j[1] == 1) or (i < 2 and final):
                            continue
                        if i == 2:
                            e = expert(j)
                        for half in range(2):
                            sp.wait_ge(lo_ready[2 * l + 1], upto(j, 3 if final else 4 * i + 2 * half + 1))
                            expert_unit(l, e, i, half, 0 if final else i)

                step((None, 1))
                step((None, 2))
                sp.wait_ge(table_ready, l + 1)
                inner = inner_blocks(sp, l)
                with sp.Fori(0, inner) as r:
                    step((r, 3))
                step((inner, 3), True)

            sp.dma_start(V[:], vec).then_inc(vec_in, 16)
            mixer_units(0)
            moe_units(0)
            mixer_units(1)
            moe_units(1)
            for k in range(0, KD, 2):
                sp.wait_ge(resid, 3 * KD + k + 2)
                sp.dma_start(out[:, k:k + 2, :], XT[:, k:k + 2, :]).then_inc(stored, 16)
            sp.wait_ge(stored, 16 * (KD // 2))

        def wait_unit(eng, mx, u):
            n = at_of[u]
            per = [2 if v[0] == "pw1" else 1 for v in units[mx]]
            count = sum(per[m] for m in range(n + 1) if m % RING == n % RING)
            eng.wait_ge(landed[2 * mx][n % RING], 16 * count)

        @block.tensor
        def _(pe):
            mm = nc.tensor.matmul
            tr = nc.tensor.transpose

            def mm3(dst, lhs, rhs, start, stop):
                mm(dst, lhs[0], rhs[0], start=start, stop=False)
                mm(dst, lhs[1], rhs[0], start=False, stop=False)
                return mm(dst, lhs[0], rhs[1], start=False, stop=stop)

            def ada(i):
                a = ADA_ORDER[i]
                if a in POOL_ADA:
                    pe.wait_ge(ada_pooled, POOL_ADA.index(a) + 1)
                else:
                    pe.wait_ge(ada_summed, DVE_ADA.index(a) + 1)
                group = [g for g, (first, _) in enumerate(ADA_GROUPS) if first == i]
                if group and group[0]:
                    pe.wait_ge(ada_stored, group[0])
                g = [first <= i < end for first, end in ADA_GROUPS].index(True)
                if g == 0:
                    for m in range(4):
                        ins = mm(PS[:, 7, 4 * a + m:4 * a + m + 1], ada_acc(a)[:, m * P:(m + 1) * P], ones[:, 0:1],
                                 start=True, stop=True)
                else:
                    first, end = ADA_GROUPS[g]
                    ins = mm(PS[0:HEADS, 7, :], con_("hsel", HEADS, HEADS * (a - first)), ada_acc(a),
                             start=(i == first), stop=(i == end - 1))
                ins.then_inc(ada_done, 1)

            def ada_turn(g):
                pe.wait_ge(ada_rows, g)
                for m in range(4):
                    ins = tr(PS[:, 7, m * HEADS:(m + 1) * HEADS], root[0:HEADS, m * P:(m + 1) * P],
                             C[0:HEADS, CC["ident"]:CC["ident"] + HEADS])
                ins.then_inc(ada_turned, 1)

            def norm_sums(n):
                for i in range(4):
                    pe.wait_ge(norm_sq, 4 * n + i + 1)
                    for k in (2 * i, 2 * i + 1):
                        ins = mm(PS[:, 4, 0:T], ones, norm_squares(n)[:, k, :], start=(k == 0), stop=(k == KD - 1))
                ins.then_inc(norm_sum, 1)

            item = [0]

            def item_bank():
                n = item[0]
                item[0] += 1
                if n >= 4:
                    pe.wait_ge(item_stored, n - 3)
                return n % 4

            def piece_in(ph, n):
                pe.wait_ge(lo_ready[ph], n + 1)

            def lat():
                for n in range(5):
                    hi, lo = piece_bufs(n, KD, 256 if n < 4 else P)
                    piece_in(0, n)
                    b = item_bank() if n < 4 else 4
                    if n == 4:
                        item[0] += 1
                        pe.wait_ge(norm_root, 1)
                    for m in range(2 if n < 4 else 1):
                        for k in range(KD):
                            if n == 0 and m == 0:
                                pe.wait_ge(xl_ready, k // 2 + 1)
                            x = (xh[:, k, :], xl[:, k, :])
                            if n < 4:
                                ins = mm3(PS[:, b, m * T:(m + 1) * T],
                                          (hi[:, k, m * P:(m + 1) * P], lo[:, k, m * P:(m + 1) * P]), x,
                                          k == 0, k == KD - 1)
                            else:
                                ins = mm3(PS[:, 4, 0:T], (hi[:, k, :], lo[:, k, :]), x, k == 0, k == KD - 1)
                    ins.then_inc(item_done, 1)
                    pe.wait_ge(item_done, item[0])
                    pe.sem_inc(piece_used[0], 1)
                pe.wait_ge(item_stored, 5)
                for m in range(KQ):
                    mm(PS[:, 5, 0:T], ones, sq[:, m, :], start=(m == 0), stop=(m == KQ - 1))
                for m in range(KKV):
                    ins = mm(PS[:, 5, T:2 * T], ones, sq[:, KQ + m, :], start=(m == 0), stop=(m == KKV - 1))
                ins.then_inc(lat_sum, 1)
                pe.wait_ge(kpe_scaled, 1)
                mm(PS[:, 6, 0:T], con_("rot"), ropetmp[:, 1, :], start=True, stop=True).then_inc(kpe_rot, 1)

            def kv_piece(half):
                n = 5 + half
                _, hi, lo, _, _ = mixer_piece(0, n)
                piece_in(0, n)
                if half == 0:
                    pe.wait_ge(latl_ready, 1)
                lat = lambda k, c: (xh[:, KQ + k, c], xl[:, KQ + k, c])
                for pair in range(2):
                    b = item_bank()
                    for a in range(2):
                        c = 256 * (2 * pair + a)
                        for k in range(KKV):
                            ins = mm3(PS[:, b, a * T:(a + 1) * T], (hi[:, k, c:c + NOPE], lo[:, k, c:c + NOPE]),
                                      lat(k, slice(0, T)), k == 0, k == KKV - 1)
                    ins.then_inc(item_done, 1)
                for t in range(NT):
                    b = item_bank()
                    for k in range(KKV):
                        w = [x[:, k, :].rearrange("p (h c) -> p h c", c=256)[:, :, NOPE:] for x in (hi, lo)]
                        ins = mm3(PS[:, b, :].rearrange("p (h c) -> p h c", c=VD), lat(k, slice(t * P, (t + 1) * P)),
                                  w, k == 0, k == KKV - 1)
                    ins.then_inc(item_done, 1)
                pe.wait_ge(item_done, item[0])
                pe.sem_inc(piece_used[0], 1)

            def q_piece(i):
                n = 7 + i
                _, hi, lo, _, _ = mixer_piece(0, n)
                piece_in(0, n)
                if i == 0:
                    pe.wait_ge(latl_ready, 4)
                b = item_bank()
                for a in range(2):
                    for k in range(KQ):
                        ins = mm3(PS[:, b, a * T:(a + 1) * T], (hi[:, k, a * P:(a + 1) * P], lo[:, k, a * P:(a + 1) * P]),
                                  (xh[:, k, :], xl[:, k, :]), k == 0, k == KQ - 1)
                ins.then_inc(item_done, 1)
                pe.wait_ge(item_done, item[0])
                pe.sem_inc(piece_used[0], 1)

            def k_stats():
                pe.wait_ge(item_stored, 13)
                pe.wait_ge(krope_ready, 1)
                for h in range(HEADS):
                    mm(PS[0:HEADS, 5, 0:T], con_("hsel", HEADS, HEADS * h), sq[:, h, :], start=(h == 0), stop=False)
                mm(PS[0:HEADS, 5, 0:T], con_("kpesel", HEADS), kpe_sq, start=False, stop=True).then_inc(k_sum, 1)

            def k_broadcast():
                pe.wait_ge(k_recip, 1)
                for i in range(PAIRS):
                    if i >= 2:
                        pe.wait_ge(bc_used, i - 1)
                    for a in range(2):
                        row = con_("ident", 1, 2 * i + a, HEADS).to_broadcast([HEADS, P])
                        ins = mm(PS[:, 5 + i % 2, a * T:(a + 1) * T], row, rstd[0:HEADS, 0:T], start=True, stop=True)
                    ins.then_inc(bc_done, 1)

            def q_stats():
                pe.wait_ge(item_stored, 19)
                pe.wait_ge(bc_used, PAIRS)
                for h in range(HEADS):
                    mm(PS[0:HEADS, 5, 0:T], con_("hsel", HEADS, HEADS * h), sq[:, h, :], start=(h == 0), stop=False)
                for g in range(PAIRS):
                    ins = mm(PS[0:HEADS, 5, 0:T], con_("psel", HEADS, HEADS * g), sq_rope[:, g, :], start=False,
                             stop=(g == PAIRS - 1))
                ins.then_inc(q_sum, 1)
                for i in range(2):
                    for a in range(2):
                        ins = mm(PS[:, i, a * T:(a + 1) * T], con_("rot"), qr[:, 2 * i + a, :], start=True, stop=True)
                    ins.then_inc(q_rot, 1)
                pe.wait_ge(q_recip, 1)
                for t in range(NT):
                    ins = tr(PS[:, 6, t * HEADS:(t + 1) * HEADS], rstd[0:HEADS, t * P:(t + 1) * P],
                             C[0:HEADS, CC["ident"]:CC["ident"] + HEADS])
                ins.then_inc(q_turned, 1)

            def attn_scores(h):
                g, a = divmod(h, 2)
                if h == 0:
                    pe.wait_ge(q_ready, 2)
                if h >= 2:
                    pe.wait_ge(s_masked, h - 1)
                r = slice(64 * a, 64 * a + 64)
                b = PS[:, h % 2, :]
                for qb, at, n in ((0, 0, P), (1, P, 2 * P)):
                    q = slice(qb * P, (qb + 1) * P)
                    mm(b[:, at:at + n], qn[:, h, q], kn[:, h, 0:n], start=True, stop=False)
                    ins = mm(b[:, at:at + n], qr[r, g, q], kr[r, g, 0:n], start=False, stop=True)
                ins.then_inc(s_done, 1)

            def attn_values(h):
                pe.wait_ge(p_ready, h + 1)
                if h >= 2:
                    pe.wait_ge(pt_stored, h - 1)
                for i in range(3):
                    ins = tr(PS[:, 2 + h % 2, i * P:(i + 1) * P], attn_p[:, h % 2, i * P:(i + 1) * P], ident)
                ins.then_inc(pt_done, 1)
                pe.wait_ge(pt_stored, h + 1)
                if h >= 2:
                    pe.wait_ge(ol_ready, h - 1)
                else:
                    pe.wait_ge(rq_ready, 1)
                pt = attn_pt[:, h % 2, :]
                b = PS[:, 5 + h % 2, :]
                mm(b[:, 0:T], vt[:, 0, h * VD:(h + 1) * VD], pt[:, 0:T], start=True, stop=False)
                mm(b[:, P:T], vt[:, 1, h * VD:(h + 1) * VD], pt[:, T:T + P], start=False,
                   stop=True).then_inc(o_done, 1)

            def project(mx, first, free):
                for i in range(4):
                    if mx == 0 and i in (1, 2):
                        ada(11 + i)
                    if mx == 1 and i == 3:
                        ada_turn(3)
                    _, hi, lo, _, _ = mixer_piece(mx, first + i)
                    piece_in(2 * mx, first + i)
                    for m in range(2):
                        for k in range(KD):
                            if i == 0 and m == 0:
                                free(k)
                            ins = mm3(PS[:, i, m * T:(m + 1) * T],
                                      (hi[:, k, m * P:(m + 1) * P], lo[:, k, m * P:(m + 1) * P]),
                                      (xh[:, k, :], xl[:, k, :]), k == 0, k == KD - 1)
                    ins.then_inc(proj_done[mx], 1)
                    pe.wait_ge(proj_done[mx], i + 1)
                    pe.sem_inc(piece_used[2 * mx], 1)

            def mixer0():
                pe.wait_ge(con_in, 16)
                pe.wait_ge(vec_in, 16)
                norm_sums(0)
                for a in range(4):
                    ada(a)
                lat()
                kv_piece(0)
                ada(4)
                kv_piece(1)
                ada(5)
                k_stats()
                for i in range(6):
                    q_piece(i)
                    if i == 1:
                        k_broadcast()
                    if i:
                        ada(5 + i)
                q_stats()
                for h in range(HEADS):
                    attn_scores(h)
                    if h:
                        attn_values(h - 1)
                    if h == 2:
                        ada(11)
                    if h == 4:
                        ada_turn(1)
                attn_values(HEADS - 1)
                project(0, 13, lambda k: pe.wait_ge(ol_ready, k + 1))

            def conv(c):
                pe.wait_ge(diag_ready, c + 1)
                pe.wait_ge(glu_ready, c + 1)
                if c == 6:
                    pe.wait_ge(conv_ready, 1)
                at = (c % 2) * T
                for j in range(PE_TAPS):
                    ins = mm(PS[:, CONV_BANKS[c // 2], at:at + T], diag[:, c % 2, j, :], upad[:, c, j:j + T], start=(j == 0),
                             stop=(j == PE_TAPS - 1))
                ins.then_inc(conv_pe, 1)

            def mixer1():
                norm_sums(2)
                ada(17)
                ada(18)
                for n in range(8):
                    i, half = divmod(n, 2)
                    _, hi, lo, _, _ = mixer_piece(1, n)
                    piece_in(2, n)
                    b = n % 4
                    if n >= 4:
                        pe.wait_ge(glu_ready, 2 * (i - 1))
                    for m in range(2):
                        for k in range(KD):
                            if n == 0 and m == 0:
                                pe.wait_ge(xl_ready, 4 + k // 2 + 1)
                            ins = mm3(PS[:, b, m * T:(m + 1) * T],
                                      (hi[:, k, m * P:(m + 1) * P], lo[:, k, m * P:(m + 1) * P]),
                                      (xh[:, k, :], xl[:, k, :]), k == 0, k == KD - 1)
                    ins.then_inc(glu_done, 1)
                    pe.wait_ge(glu_done, n + 1)
                    pe.sem_inc(piece_used[2], 1)
                    if half and i in (1, 2):
                        conv(2 * i - 2)
                        conv(2 * i - 1)
                        if i == 2:
                            ada(19)
                conv(4)
                conv(5)
                ada(20)
                conv(6)
                conv(7)
                for k in range(KD):
                    pe.wait_ge(conv_ready, max(k // 2, 1) + 1)
                    ins = mm(PS[:, 6, 0:T], ones, cacc[:, k, :], start=(k == 0), stop=(k == KD - 1))
                ins.then_inc(ln_sum, 1)
                for k in range(KD):
                    pe.wait_ge(ln_sq, k // 2 + 1)
                    ins = mm(PS[:, 5, 0:T], ones, sq[:, k, :], start=(k == 0), stop=(k == KD - 1))
                ins.then_inc(ln_var, 1)
                for i in (21, 22, 23):
                    ada(i)
                project(1, 8, lambda k: pe.wait_ge(xl_ready, 8 + k // 2 + 1))

            def moe(l):
                ph, n = 2 * l + 1, 2 * l + 1
                norm_sums(n)
                if l == 0:
                    ada(14)
                    ada(15)
                for t in range(NT):
                    for k in range(KD):
                        if t == 0:
                            pe.wait_ge(h_ready, 8 * n + k + 1)
                        ins = mm(PS[:, 0, t * E:(t + 1) * E], hT[:, k, t * P:(t + 1) * P],
                                 vcol("router_w", k * E, E), start=(k == 0), stop=(k == KD - 1))
                ins.then_inc(logits_done, 1)
                for i in range(4):
                    t, half = divmod(i, 2)
                    for j in range(4):
                        ins = tr(PS[:, HTOK_BANKS[i], j * P:(j + 1) * P],
                                 hT[:, half * 4 + j, t * P:(t + 1) * P], ident)
                    ins.then_inc(htok_done, 1)
                pe.wait_ge(picks_ready, l + 1)
                picks = [small[:, 256 + t * E:256 + (t + 1) * E] for t in range(NT)]
                b = PS[:, 1, :]
                mm(b[:, 0:E], con_("before"), picks[0], start=True, stop=True)
                mm(b[:, E:2 * E], con_("before"), picks[1], start=True, stop=False)
                mm(b[:, E:2 * E], ones, picks[0], start=False, stop=True)
                for t in range(NT):
                    ins = mm(b[0:E, 64:64 + P], picks[t], ones, start=(t == 0), stop=(t == NT - 1))
                ins.then_inc(counts_done, 1)
                if l == 0:
                    ada(16)
                pe.wait_ge(count_rows, l + 1)
                c16, n16 = small[0:E, 512:512 + P], small[0:E, 640:641]
                b = PS[:, 2, :]
                mm(b[:, 0:E], c16, con_("tri16", E, 0, E), start=True, stop=True)
                mm(b[0:E, 64:65], con_("tri16", E, 0, E), c16[:, 0:1], start=True, stop=True)
                mm(b[0:E, 65:66], con_("tri16", E, 0, E), n16, start=True, stop=True).then_inc(offs_done, 1)
                pe.wait_ge(htokl_ready, 4 * l + 4)
                banks = (0, 5, 6, 4)
                for k in range(KD):
                    if k == 0:
                        pe.wait_ge(perm_ready, 2 * l + NT)
                    if k >= 4:
                        pe.wait_ge(gather_stored, 8 * l + k - 3)
                    if k == 4:
                        pe.wait_ge(slots_ready, l + 1)
                        mm(PS[0:1, 3, 0:NTAB], ones[0:E, 0:1], small[0:E, 1024:1024 + NTAB], start=True,
                           stop=True).then_inc(rows_done, 1)
                    c = slice(k * P, (k + 1) * P)
                    for t in range(NT):
                        mm(PS[:, banks[k % 4], :], htokh[:, t, c], perm[:, t, :], start=(t == 0), stop=False)
                        ins = mm(PS[:, banks[k % 4], :], htokl[:, t, c], perm[:, t, :], start=False,
                                 stop=(t == NT - 1))
                    ins.then_inc(gather_done, 1)
                pe.wait_ge(gather_stored, 8 * l + 5)
                pe.wait_ge(table_ready, l + 1)
                inner = inner_blocks(pe, l)

                def y_turn(j):
                    pe.wait_ge(y_stored[l], nth(j, 2))
                    for half in range(2):
                        for i in range(4):
                            ins = tr(PS[:, 5 + half, i * P:(i + 1) * P], yb[:, (4 * half + i) * P:(4 * half + i + 1) * P],
                                     ident)
                        ins.then_inc(ytt_done[l], 1)

                def gate_up(j, first, second=False):
                    if not first:
                        pe.wait_ge(hcl_ready[l], nth(j, 1, -1))
                        pe.wait_ge(silu_done[l], nth(j, 1, -1))
                    for i in range(8):
                        u, q = divmod(i, 4)
                        if i in (0, 2) and first:
                            pe.wait_ge(half_low, 2 * l + i // 2 + 1)
                        if i == 1 and not first:
                            act_turn(after(j, -1))
                        if i == 6 and not (first or second):
                            y_turn(after(j, -2))
                        _, hi, lo = moe_piece(j, i)
                        pe.wait_ge(lo_ready[ph], upto(j, i))
                        for k in range(2):
                            kk = 2 * q + k
                            ins = mm3(PS[:, u, :], (hch[:, kk, :], hcl[:, kk, :]), (hi[:, k, :], lo[:, k, :]),
                                      kk == 0, kk == KD - 1)
                        ins.then_inc(piece_used[ph], 1)

                def act_turn(j):
                    pe.wait_ge(act_ready[l], nth(j))
                    for i in range(KF):
                        ins = tr(PS[:, 2, i * P:(i + 1) * P], act[:, i * P:(i + 1) * P], ident)
                    ins.then_inc(att_done[l], 1)

                def down(j, of, end=False):
                    for i in range(4):
                        half, q = divmod(i, 2)
                        p = i if end else i + 8
                        _, hi, lo = moe_piece(j, p, end)
                        pe.wait_ge(lo_ready[ph], upto(j, p))
                        if half == 0:
                            pe.wait_ge(atl_ready[l], nth(of, 2, q - 1))
                        for k in (2 * q, 2 * q + 1):
                            ins = mm3(PS[:, 3 + half, :], (aTh[:, k, :], aTl[:, k, :]), (hi[:, k % 2, :], lo[:, k % 2, :]),
                                      k == 0, k == KF - 1)
                        ins.then_inc(piece_used[ph], 1)

                gate_up((None, 1), True)
                pe.wait_ge(wperm_ready, 2 * l + NT)
                for s in range(SB):
                    for t in range(NT):
                        ins = tr(PS[:, 5 + s // 2, (s % 2) * T + t * P:(s % 2) * T + (t + 1) * P],
                                 wperm[:, t, s * P:(s + 1) * P], ident)
                    if s % 2:
                        ins.then_inc(wpt_done, 1)
                gate_up((None, 2), False, True)
                down((None, 2), (None, 1))
                with pe.Fori(0, inner + 1) as r:
                    gate_up((r, 3), False)
                    down((r, 3), (r, 2))
                final = (inner, 3)
                act_turn(final)
                y_turn(after(final, -1))
                down(after(final), final, True)
                pe.wait_ge(yta_stored[l], nth(final, 1, -1))
                pe.wait_ge(ytd_stored[l], nth(final, 1, -1))
                y_turn(final)
                if l == 0:
                    ada_turn(2)
                pe.wait_ge(yta_stored[l], nth(final))
                pe.wait_ge(ytd_stored[l], nth(final))
                for i in range(8):
                    s, half = divmod(i, 2)
                    if i >= 2:
                        pe.wait_ge(ysl_stored, 8 * l + i - 1)
                    for j in range(4):
                        k = half * 4 + j
                        ins = tr(PS[:, 5 + i % 2, j * P:(j + 1) * P], yT[:, k, s * P:(s + 1) * P], ident)
                    ins.then_inc(ysl_done, 1)
                pe.wait_ge(ysl_stored, 8 * l + 8)
                for k in range(KD):
                    for s in range(SB):
                        ins = mm(PS[:, k // 2, (k % 2) * T:(k % 2 + 1) * T], ysl[:, s, k * P:(k + 1) * P],
                                 wpT[:, s, :], start=(s == 0), stop=(s == SB - 1))
                    if k % 2:
                        ins.then_inc(moe_done, 1)

            mixer0()
            moe(0)
            mixer1()
            moe(1)

        @block.scalar
        def _(act_e):
            A = nc.scalar.activation
            act_e.wait_ge(eps_ready, 2)
            act_e.wait_ge(vec_in, 16)
            A(sc[:], vcol("c", 0, KD), ACT.Silu).then_inc(silu_c, 1)

            def norm(n):
                if n == 2:
                    hi(1, 0)
                    hi(1, 1)
                for i in range(4):
                    if n == 0:
                        act_e.wait_ge(x_in, 16)
                    else:
                        act_e.wait_ge(resid, KD * (n - 1) + 2 * i + 2)
                    A(norm_squares(n)[:, 2 * i:2 * i + 2, :], XT[:, 2 * i:2 * i + 2, :], ACT.Square).then_inc(norm_sq, 1)
                act_e.wait_ge(norm_sum, n + 1)
                A(root[:, 0:T], PS[:, 4, 0:T], ACT.Sqrt, bias=eps[:, 0:1], scale=1.0 / D).then_inc(norm_root, 1)
                if n == 0:
                    hi(0, 0)
                    hi(0, 1)
                elif n != 2:
                    hi_m(n // 2, (None, 1), 0)
                    hi_m(n // 2, (None, 1), 1)
                l, w = divmod(n, 2)
                act_e.wait_ge(mods_ready, n + 1)
                for k in range(KD):
                    if k % 2 == 0 and n % 2 == 0 and k:
                        split_pair(hT, h_ready, KD * n, k // 2 - 1)
                    act_e.wait_ge(norm_scaled, 4 * n + k // 2 + 1)
                    A(hT[:, k, :], hT[:, k, :], ACT.Identity, bias=mods[:, l, 24 * w + k:24 * w + k + 1],
                      scale=gsc[:, n, k:k + 1]).then_inc(h_ready, 1)
                if n % 2 == 0:
                    split_pair(hT, h_ready, KD * n, 3)

            def split_pair(src, done, base, i):
                act_e.wait_ge(done, base + 2 * i + 2)
                A(xh[:, 2 * i:2 * i + 2, :], src[:, 2 * i:2 * i + 2, :], ACT.Copy).then_inc(xh_ready, 1)

            def hi(mx, n):
                raw, h, _, u, _ = mixer_piece(mx, n)
                wait_unit(act_e, mx, u)
                if n >= PBUF:
                    act_e.wait_ge(piece_used[2 * mx], n - PBUF + 1)
                elif mx:
                    act_e.wait_ge(piece_used[1], upto((inner_blocks(act_e, 0), 4), 3))
                A(h, raw, ACT.Copy).then_inc(hi_ready[2 * mx], 1)

            def root_of(dst, src, n):
                return A(dst, src, ACT.Sqrt, bias=eps[0:dst.shape[0], 0:1], scale=1.0 / n)

            def hi_m(l, j, i, end=False):
                ph = 2 * l + 1
                raw, h, _ = moe_piece(j, i, end)
                u = 0 if end else i // 4
                if i % 4 == 0:
                    act_e.wait_ge(landed[ph][u], nth(after(j, -1) if u == 2 else j, 32))
                if j[0] is None and j[1] == 1 and i < 2 * PBUF:
                    if i == 0:
                        act_e.wait_ge(piece_used[2 * l], len(pieces[l]))
                else:
                    act_e.wait_ge(piece_used[ph], upto(j, i, 2 * PBUF))
                A(h, raw, ACT.Copy).then_inc(hi_ready[ph], 1)

            def ada_row_copy(g):
                act_e.wait_ge(ada_done, ADA_GROUPS[g][1])
                A(root[0:HEADS, :], PS[0:HEADS, 7, :], ACT.Copy).then_inc(ada_rows, 1)

            def two(b):
                return PS[:, b, :].rearrange("p (a t) -> p a t", t=T)

            def store_lat(n):
                act_e.wait_ge(item_done, n + 1)
                if n < 4:
                    A(latT[:, 2 * n:2 * n + 2, :], two(n), ACT.Copy)
                    A(sq[:, 2 * n:2 * n + 2, :], two(n), ACT.Square).then_inc(item_stored, 1)
                else:
                    A(latT[:, 8, :], PS[:, 4, 0:T], ACT.Copy)
                    A(kpe_sq, PS[:, 4, 0:T], ACT.Square).then_inc(item_stored, 1)

            def store_k(n, pair):
                act_e.wait_ge(item_done, n + 1)
                ks = slice(2 * pair, 2 * pair + 2)
                if n == 5:
                    act_e.wait_ge(lat_sum, 1)
                A(kn[:, ks, :], two(n % 4), ACT.Identity, scale=vcol("gk_nope"))
                A(sq[:, ks, :], two(n % 4), ACT.Square).then_inc(item_stored, 1)

            def store_v(n, t, half):
                act_e.wait_ge(item_done, n + 1)
                A(vt[:, t, half * 512:(half + 1) * 512], PS[:, n % 4, :], ACT.Copy).then_inc(item_stored, 1)

            def store_q(i):
                n = 13 + i
                act_e.wait_ge(item_done, n + 1)
                if i == 0:
                    act_e.wait_ge(k_sum, 1)
                g = i % 4
                dst, s, gain = ((qn[:, 2 * g:2 * g + 2, :], sq[:, 2 * g:2 * g + 2, :], "gq_nope") if i < 4 else
                                (qr[:, 2 * g:2 * g + 2, :], sq_rope[:, 2 * g:2 * g + 2, :], "gq_rope"))
                A(dst, two(n % 4), ACT.Identity, scale=vcol(gain))
                A(s, two(n % 4), ACT.Square).then_inc(item_stored, 1)

            def mixer0():
                norm(0)
                hi(0, 2)
                for n in range(5):
                    store_lat(n)
                    if n < 4:
                        hi(0, n + 3)
                act_e.wait_ge(lat_sum, 1)
                root_of(root[:, T:2 * T], PS[:, 5, T:2 * T], KVR).then_inc(lat_root, 1)
                root_of(root[:, 0:T], PS[:, 5, 0:T], QR).then_inc(lat_root, 1)
                act_e.wait_ge(angles, 2)
                A(sin_t, sin_t, ACT.Sin).then_inc(tables, 1)
                A(cos_t, cos_t, ACT.Sin, bias=eps[:, 1:2], scale=-1.0).then_inc(tables, 1)
                for i in (3, 0, 1, 2):
                    act_e.wait_ge(lat_ready, {3: 1, 0: 2, 1: 3, 2: 4}[i])
                    A(xh[:, 2 * i:2 * i + 2, :], latT[:, 2 * i:2 * i + 2, :], ACT.Copy).then_inc(lath_ready, 1)
                hi(0, 7)
                n = 5
                for half in range(2):
                    for pair in range(2):
                        store_k(n, 2 * half + pair)
                        n += 1
                    for t in range(NT):
                        store_v(n, t, half)
                        n += 1
                    if half == 0:
                        hi(0, 8)
                act_e.wait_ge(k_sum, 1)
                root_of(root[0:HEADS, 0:T], PS[0:HEADS, 5, 0:T], QK).then_inc(k_root, 1)
                hi(0, 9)
                for i in range(6):
                    if i < 3:
                        hi(0, 10 + i)
                    store_q(i)
                act_e.wait_ge(q_sum, 1)
                act_e.wait_ge(k_recip, 1)
                root_of(root[0:HEADS, 0:T], PS[0:HEADS, 5, 0:T], QK).then_inc(q_root, 1)
                for h in range(HEADS):
                    act_e.wait_ge(s_max, h + 1)
                    if h >= 2:
                        act_e.wait_ge(pt_done, h - 1)
                    sm = attn_sm[:, h % 2, :]
                    for i, (at, n) in enumerate(((0, P), (P, 2 * P))):
                        A(attn_p[:, h % 2, at:at + n], attn_s[:, h % 2, at:at + n], ACT.Exp,
                          bias=sm[:, 2 + i:3 + i], accum_out=sm[:, 4 + i:5 + i]).then_inc(p_exp, 1)
                    act_e.wait_ge(pt_done, h + 1)
                    if h >= 2:
                        act_e.wait_ge(o_done, h - 1)
                    A(attn_pt[:, h % 2, :], PS[:, 2 + h % 2, 0:3 * P], ACT.Copy).then_inc(pt_stored, 1)
                    act_e.wait_ge(o_done, h + 1)
                    A(xh[:, h, :], PS[:, 5 + h % 2, 0:T], ACT.Copy).then_inc(oh_ready, 1)
                    if h == 0:
                        hi(0, 13)
                        hi(0, 14)
                    if h == 3:
                        act_e.wait_ge(q_recip, 1)
                        ada_row_copy(1)
                    if h == 6:
                        hi(0, 15)
                hi(0, 16)

            def mixer1():
                norm(2)
                hi(1, 2)
                hi(1, 3)
                for i in range(4):
                    if i:
                        for n in (2 * i + 2, 2 * i + 3):
                            if n < 8:
                                hi(1, n)
                    act_e.wait_ge(glu_done, 2 * i + 2)
                    for a in range(2):
                        c = 2 * i + a
                        if c >= 4:
                            act_e.wait_ge(glu_ready, c - 3)
                        A(sig[:, c % 4, :], PS[:, (2 * i + 1) % 4, a * T:(a + 1) * T], ACT.Sigmoid,
                          bias=vcol("pw1_b", KD + c)).then_inc(glu_sig, 1)
                for n in range(8, 11):
                    hi(1, n)
                act_e.wait_ge(ln_sum, 1)
                A(rstd[:, T:2 * T], PS[:, 6, 0:T], ACT.Copy, scale=1.0 / D).then_inc(ln_mean, 1)
                for i in range(4):
                    act_e.wait_ge(ln_centred, i + 1)
                    A(sq[:, 2 * i:2 * i + 2, :], cacc[:, 2 * i:2 * i + 2, :], ACT.Square).then_inc(ln_sq, 1)
                act_e.wait_ge(ln_var, 1)
                A(root[:, 0:T], PS[:, 5, 0:T], ACT.Sqrt, bias=eps[:, 0:1], scale=1.0 / D).then_inc(ln_root, 1)
                for k in range(KD):
                    act_e.wait_ge(ln_scaled, k // 2 + 1)
                    A(cacc[:, k, :], cacc[:, k, :], ACT.Silu, bias=vcol("ln_b", k),
                      scale=vcol("ln_g", k)).then_inc(ln_silu, 1)
                    if k % 2:
                        split_pair(cacc, ln_silu, 0, k // 2)
                ada_row_copy(3)
                hi(1, 11)

            def moe(l):
                ph = 2 * l + 1
                norm(ph)
                hi_m(l, (None, 1), 2)
                hi_m(l, (None, 1), 3)
                act_e.wait_ge(logits_done, l + 1)
                A(small[:, 0:2 * E], PS[:, 0, 0:2 * E], ACT.Sigmoid).then_inc(scores_ready, 1)
                for i in range(4):
                    t, half = divmod(i, 2)
                    act_e.wait_ge(htok_done, 4 * l + i + 1)
                    A(htokh[:, t, half * 512:(half + 1) * 512], PS[:, HTOK_BANKS[i], :],
                      ACT.Copy).then_inc(htokh_ready, 1)

                for k in range(KD):
                    act_e.wait_ge(gather_done, 8 * l + k + 1)
                    A(hgT[:, k, 0:SLOTS], PS[:, (0, 5, 6, 4)[k % 4], :], ACT.Copy).then_inc(gather_stored, 1)
                    if k % 4 == 3:
                        act_e.wait_ge(gather_stored, 8 * l + k + 1)
                        ks = slice(k - 3, k + 1)
                        A(hch[:, ks, :], hgT[:, ks, 0:P], ACT.Copy).then_inc(half_high, 1)
                act_e.wait_ge(table_ready, l + 1)
                inner = inner_blocks(act_e, l)

                def slot_in(j):
                    s0 = block_slot(act_e, l, j)
                    A(hch, hgT[:, :, bass.ds(s0, P)], ACT.Copy).then_inc(hch_ready[l], 1)

                def y_out(j):
                    act_e.wait_ge(ytt_done[l], nth(j, 2, -1))
                    s0 = block_slot(act_e, l, j)
                    A(yT[:, 0:4, bass.ds(s0, P)], PS[:, 5, :].rearrange("p (m c) -> p m c", c=P),
                      ACT.Copy).then_inc(yta_stored[l], 1)

                def act_high(j):
                    act_e.wait_ge(att_done[l], nth(j))
                    for half in range(2):
                        A(aTh[:, 2 * half:2 * half + 2, :],
                          PS[:, 2, 256 * half:256 * half + 256].rearrange("p (m c) -> p m c", c=P),
                          ACT.Copy).then_inc(ath_ready[l], 1)

                def y_store(j, half, piece):
                    act_e.wait_ge(piece_used[ph], piece)
                    A(yb[:, 512 * half:512 * half + 512], PS[:, 3 + half, :], ACT.Copy).then_inc(y_stored[l], 1)

                def silu(j):
                    act_e.wait_ge(piece_used[ph], upto(j, 3))
                    A(sg, PS[:, 0, :], ACT.Silu).then_inc(silu_done[l], 1)

                def ahead(j, i, last=False):
                    hi_m(l, after(j), i, last)
                    hi_m(l, after(j), i + 1, last)

                def step(j, second=False, last=False):
                    hi_m(l, j, 4)
                    hi_m(l, j, 5)
                    act_high(after(j, -1))
                    hi_m(l, j, 6)
                    hi_m(l, j, 7)
                    if not second:
                        act_e.wait_ge(act_ready[l], nth(j, 1, -1))
                    silu(j)
                    hi_m(l, j, 8)
                    hi_m(l, j, 9)
                    if not second:
                        y_out(after(j, -2))
                    hi_m(l, j, 10)
                    hi_m(l, j, 11)
                    if not last:
                        act_e.wait_ge(piece_used[ph], upto(j, 7))
                        slot_in(after(j))
                    ahead(j, 0, last)
                    y_store(after(j, -1), 0, upto(j, 9))
                    ahead(j, 2, last)
                    y_store(after(j, -1), 1, upto(j, 11))

                one = (None, 1)
                for i in range(4, 8):
                    hi_m(l, one, i)
                hi_m(l, after(one), 0)
                silu(one)
                hi_m(l, after(one), 1)
                act_e.wait_ge(piece_used[ph], upto(one, 7))
                slot_in(after(one))
                ahead(one, 2)
                act_e.wait_ge(act_ready[l], 1)
                step((None, 2), second=True)
                act_e.wait_ge(wpt_stored, 2 * l + 2)
                with act_e.Fori(0, inner) as r:
                    step((r, 3))
                final = (inner, 3)
                step(final, last=True)
                act_high(final)
                y_out(after(final, -1))
                for half in range(2):
                    y_store(final, half, upto(after(final), 2 * half + 1))
                y_out(final)
                if l == 0:
                    ada_row_copy(2)
                for i in range(8):
                    s, half = divmod(i, 2)
                    act_e.wait_ge(ysl_done, 8 * l + i + 1)
                    A(ysl[:, s, half * 512:(half + 1) * 512], PS[:, 5 + i % 2, :],
                      ACT.Copy).then_inc(ysl_stored, 1)

            mixer0()
            moe(0)
            mixer1()
            moe(1)

        @block.gpsimd
        def _(pool):
            nc.gpsimd.memset(eps[:, 0:1], EPS).then_inc(eps_ready, 1)
            nc.gpsimd.memset(eps[:, 1:2], TWO_PI / 4).then_inc(eps_ready, 1)
            seq = [0]

            def step(ins):
                seq[0] += 1
                ins.then_inc(pool_seq, 1)
                pool.wait_ge(pool_seq, seq[0])

            def ada(mx, a):
                wait_unit(pool, mx, ("ada", a))
                n = POOL_ADA.index(a)
                if n >= 2:
                    pool.wait_ge(ada_done, ADA_ORDER.index(POOL_ADA[n - 2]) + 1)
                w = unit_ap("ada", a)
                acc, tmp = ada_acc(a), pool_acc[:, 2, :]
                step(nc.gpsimd.tensor_scalar(acc, w[:, 0, :], sc[:, 0:1], 1.0, ALU.mult, ALU.mult))
                for k in range(1, KD):
                    step(nc.gpsimd.tensor_scalar(tmp, w[:, k, :], sc[:, k:k + 1], 1.0, ALU.mult, ALU.mult))
                    if k < KD - 1:
                        step(nc.gpsimd.tensor_tensor(acc, acc, tmp, ALU.add))
                nc.gpsimd.tensor_tensor(acc, acc, tmp, ALU.add).then_inc(ada_pooled, 1)
                pool.wait_ge(ada_pooled, n + 1)
                pool.sem_inc(pool_used[mx], 1)

            pool.wait_ge(silu_c, 1)
            for a in POOL_ADA:
                if a < ADA_MIXER1:
                    ada(0, a)
            pool.wait_ge(con_in, 16)
            ada(1, 18)
            pool.wait_ge(resid, 2 * KD)
            for c in range(KD):
                if c >= 2:
                    pool.wait_ge(conv_pe, c - 1)
                for j in range(PE_TAPS):
                    ins = nc.gpsimd.tensor_scalar(diag[:, c % 2, j, :], ident, vcol("dw_w", c * TAPS + j), 1.0,
                                                  ALU.mult, ALU.mult)
                ins.then_inc(diag_ready, 1)
                if c in (1, 3, 5):
                    ada(1, (19, 20, 22)[c // 2])

        @block.vector
        def _(dve):
            v = nc.vector
            seq = [0]

            def tick(ins):
                seq[0] += 1
                ins.then_inc(dve_seq, 1)

            def step(ins):
                tick(ins)
                dve.wait_ge(dve_seq, seq[0])

            def bc(ap, shape):
                return ap.to_broadcast(shape)

            def ada_sum(mx, a):
                wait_unit(dve, mx, ("ada", a))
                if a == 0:
                    dve.wait_ge(silu_c, 1)
                n = DVE_ADA.index(a)
                if n >= 2 and a != 5:
                    dve.wait_ge(ada_done, ADA_ORDER.index(DVE_ADA[n - 2]) + 1)
                w, acc = unit_ap("ada", a), ada_acc(a)
                step(v.tensor_scalar(acc, w[:, 0, :], sc[:, 0:1], None, ALU.mult))
                for k in range(1, KD):
                    ins = v.scalar_tensor_tensor(out=acc, in0=w[:, k, :], scalar=sc[:, k:k + 1], in1=acc,
                                                 op0=ALU.mult, op1=ALU.add)
                    if k < KD - 1:
                        step(ins)
                ins.then_inc(ada_summed, 1)
                dve.wait_ge(ada_summed, n + 1)
                dve.sem_inc(raw_used[mx], 1)

            def ada_store(g):
                a, b = ADA_GROUPS[g]
                dst, sums = mods[:].rearrange("p l c -> p (l c)")[:, 4 * a:4 * b], PS[:, 7, 4 * a:4 * b]
                bias = vcol("ada_b", 4 * a, 4 * (b - a))
                dve.wait_ge(ada_done, b)
                if g:
                    dve.wait_ge(ada_turned, g)
                    sums = PS[:, 7, 0:4 * HEADS].rearrange("p (m r) -> p r m", r=HEADS)[:, 0:b - a, :]
                    dst, bias = (x.rearrange("p (r m) -> p r m", m=4) for x in (dst, bias))
                v.tensor_tensor(dst, sums, bias, ALU.add).then_inc(ada_stored, 1)
                dve.wait_ge(ada_stored, g + 1)

            def mods_for(n):
                l, w = divmod(n, 2)
                v.scalar_tensor_tensor(out=gsc[:, n, :], in0=mods[:, l, 24 * w + 8:24 * w + 16], scalar=1.0,
                                       in1=vcol(("norm1", "norm2")[w], KD * l, KD), op0=ALU.add,
                                       op1=ALU.mult).then_inc(mods_ready, 1)

            def norm(n):
                dve.wait_ge(norm_root, n + 1)
                step(v.reciprocal(rstd[:, 0:T], root[:, 0:T]))
                if n in (1, 2):
                    dve.wait_ge(ada_done, ADA_ORDER.index(15 if n == 1 else 17) + 1)
                for i in range(4):
                    ks = slice(2 * i, 2 * i + 2)
                    v.tensor_tensor(hT[:, ks, :], XT[:, ks, :], bc(rstd[:, 0:T].unsqueeze(1), [P, 2, T]),
                                    ALU.mult).then_inc(norm_scaled, 1)

            def split_x(src, his, base, signal, order=(0, 1, 2, 3)):
                for n, i in enumerate(order):
                    dve.wait_ge(his, base + n + 1)
                    ks = slice(2 * i, 2 * i + 2)
                    v.tensor_tensor(xl[:, ks, :], src[:, ks, :], xh[:, ks, :].bitcast(F32),
                                    ALU.subtract).then_inc(signal, 1)

            def lo(mx, n):
                raw, h, l_, u, j = mixer_piece(mx, n)
                dve.wait_ge(hi_ready[2 * mx], n + 1)
                v.tensor_tensor(l_, raw, h.bitcast(F32), ALU.subtract).then_inc(lo_ready[2 * mx], 1)
                if j == pieces_of(u) - 1:
                    dve.wait_ge(lo_ready[2 * mx], n + 1)
                    dve.sem_inc(raw_used[mx], 1)

            def residual(bank, k, gate):
                at = (k % 2) * T
                return v.scalar_tensor_tensor(out=XT[:, k, :], in0=PS[:, bank, at:at + T], scalar=gate,
                                              in1=XT[:, k, :], op0=ALU.mult, op1=ALU.add)

            def rope_tables():
                dve.wait_ge(pos_in, 16)
                dve.wait_ge(vec_in, 16)
                ang, n = ropetmp[:, 0, :], ropetmp[:, 1, :]
                step(v.tensor_copy(sin_t, posi))
                step(v.tensor_scalar(ang, sin_t, vcol("inv_freq"), None, ALU.mult))
                step(v.tensor_scalar(n, ang, 1.0 / TWO_PI, MAGIC, ALU.mult, ALU.add))
                step(v.tensor_scalar(n, n, MAGIC, None, ALU.subtract))
                for part in (PI_A, PI_B, PI_C):
                    step(v.scalar_tensor_tensor(out=ang, in0=n, scalar=-part, in1=ang, op0=ALU.mult, op1=ALU.add))
                step(v.tensor_scalar(ang, ang, 3.1415925, -3.1415925, ALU.min, ALU.max))
                v.tensor_copy(sin_t, ang).then_inc(angles, 1)
                step(v.tensor_scalar(n, ang, -1.0, None, ALU.mult))
                v.tensor_tensor(cos_t, ang, n, ALU.max).then_inc(angles, 1)

            def latents():
                dve.wait_ge(item_stored, 5)
                dve.wait_ge(angles, 2)
                v.tensor_scalar(ropetmp[:, 1, :], latT[:, 8, :], vcol("gk_rope"), None,
                                ALU.mult).then_inc(kpe_scaled, 1)
                dve.wait_ge(lat_root, 1)
                step(v.reciprocal(rstd[:, T:2 * T], root[:, T:2 * T]))
                for m in (6, 7, 0, 1, 2, 3, 4, 5):
                    if m == 0:
                        dve.wait_ge(lat_root, 2)
                        step(v.reciprocal(rstd[:, 0:T], root[:, 0:T]))
                    g = vcol("q_norm", m) if m < KQ else vcol("kv_norm", m - KQ)
                    r = rstd[:, 0:T] if m < KQ else rstd[:, T:2 * T]
                    ins = v.scalar_tensor_tensor(out=latT[:, m, :], in0=latT[:, m, :], scalar=g, in1=r, op0=ALU.mult,
                                                 op1=ALU.mult)
                    if m % 2:
                        ins.then_inc(lat_ready, 1)
                    if m == 1:
                        split_x(latT, lath_ready, 0, latl_ready, (3,))
                split_x(latT, lath_ready, 1, latl_ready, (0, 1, 2))
                dve.wait_ge(tables, 2)
                dve.wait_ge(kpe_rot, 1)
                step(v.tensor_tensor(krope, PS[:, 6, 0:T], sin_t, ALU.mult))
                step(v.tensor_tensor(ropetmp[:, 0, :], ropetmp[:, 1, :], cos_t, ALU.mult))
                v.tensor_tensor(krope, krope, ropetmp[:, 0, :], ALU.add).then_inc(krope_ready, 1)

            def scale_keys():
                dve.wait_ge(krope_ready, 1)
                for i in range(PAIRS):
                    dve.wait_ge(bc_done, i + 1)
                    b = PS[:, 5 + i % 2, :].rearrange("p (a t) -> p a t", t=T)
                    ks = kn[:, 2 * i:2 * i + 2, :]
                    v.tensor_tensor(ks, ks, b, ALU.mult)
                    for a in range(2):
                        r = slice(ROPE * a, ROPE * a + ROPE)
                        ins = v.tensor_tensor(kr[r, i, :], krope[r, :], b[r, a, :], ALU.mult)
                    ins.then_inc(bc_used, 1)

            def queries():
                dve.wait_ge(q_root, 1)
                v.reciprocal(rstd[0:HEADS, 0:T], root[0:HEADS, 0:T]).then_inc(q_recip, 1)
                for i in range(2):
                    dve.wait_ge(q_rot, i + 1)
                    qs = qr[:, 2 * i:2 * i + 2, :]
                    step(v.tensor_tensor(ropetmp, PS[:, i, :].rearrange("p (a t) -> p a t", t=T),
                                         bc(sin_t.unsqueeze(1), [P, 2, T]), ALU.mult))
                    step(v.tensor_tensor(qs, qs, bc(cos_t.unsqueeze(1), [P, 2, T]), ALU.mult))
                    v.tensor_tensor(qs, qs, ropetmp, ALU.add).then_inc(q_ready, 1)
                    dve.wait_ge(q_ready, i + 1)
                dve.wait_ge(q_turned, 1)
                v.tensor_scalar(kq_rstd, PS[:, 6, 0:2 * HEADS], SCALE, None, ALU.mult).then_inc(rq_ready, 1)
                dve.wait_ge(rq_ready, 1)

            def softmax(h):
                s, sm = attn_s[:, h % 2, :], attn_sm[:, h % 2, :]
                dve.wait_ge(s_done, h + 1)
                for t, c in ((0, slice(0, P)), (1, slice(P, 3 * P))):
                    ins = v.scalar_tensor_tensor(out=s[:, c], in0=PS[:, h % 2, c],
                                                 scalar=kq_rstd[:, t * HEADS + h:t * HEADS + h + 1],
                                                 in1=con_("causal", 3 * P)[:, c], op0=ALU.mult, op1=ALU.add)
                ins.then_inc(s_masked, 1)
                dve.wait_ge(s_masked, h + 1)
                v.tensor_reduce(sm[:, 0:1], s[:, 0:P], AX, ALU.max)
                step(v.tensor_reduce(sm[:, 1:2], s[:, P:3 * P], AX, ALU.max))
                v.tensor_scalar(sm[:, 2:4], sm[:, 0:2], -1.0, None, ALU.mult).then_inc(s_max, 1)

            def normalise(h):
                sm = attn_sm[:, h % 2, :]
                dve.wait_ge(p_exp, 2 * h + 2)
                step(v.reciprocal(sm[:, 6:8], sm[:, 4:6]))
                p = attn_p[:, h % 2, :]
                v.tensor_scalar(p[:, 0:P], p[:, 0:P], sm[:, 6:7], None, ALU.mult)
                v.tensor_scalar(p[:, P:3 * P], p[:, P:3 * P], sm[:, 7:8], None, ALU.mult).then_inc(p_ready, 1)

            def o_low(h):
                dve.wait_ge(oh_ready, h + 1)
                v.tensor_tensor(xl[:, h, :], PS[:, 5 + h % 2, 0:T], xh[:, h, :].bitcast(F32),
                                ALU.subtract).then_inc(ol_ready, 1)

            def mixer0():
                ada_sum(0, 0)
                ada_sum(0, 1)
                norm(0)
                ada_sum(0, 2)
                ada_sum(0, 3)
                ada_store(0)
                mods_for(0)
                lo(0, 0)
                split_x(hT, xh_ready, 0, xl_ready)
                dve.wait_ge(con_in, 16)
                dve.wait_ge(rb_in, 16)
                lo(0, 1)
                rope_tables()
                for n in range(2, 5):
                    lo(0, n)
                ada_sum(0, 5)
                for n in range(5, 7):
                    lo(0, n)
                latents()
                ada_sum(0, 7)
                for n in range(7, 9):
                    lo(0, n)
                dve.wait_ge(k_root, 1)
                dve.wait_ge(lat_ready, 4)
                v.reciprocal(rstd[0:HEADS, 0:T], root[0:HEADS, 0:T]).then_inc(k_recip, 1)
                scale_keys()
                for n in range(9, 11):
                    lo(0, n)
                ada_sum(0, 9)
                for n in range(11, 13):
                    lo(0, n)
                ada_sum(0, 11)
                dve.wait_ge(bc_used, PAIRS)
                queries()
                for h in range(HEADS):
                    softmax(h)
                    if h:
                        o_low(h - 1)
                    normalise(h)
                    if h == 1:
                        lo(0, 13)
                        lo(0, 14)
                    if h == 4:
                        ada_store(1)
                        mods_for(1)
                o_low(HEADS - 1)
                ada_sum(0, 13)
                lo(0, 15)
                lo(0, 16)
                for k in range(KD):
                    dve.wait_ge(proj_done[0], k // 2 + 1)
                    residual(k // 2, k, mods[:, 0, 16 + k:17 + k]).then_inc(resid, 1)
                    if k == 5:
                        ada_sum(0, 15)

            def conv_pair(i):
                cs = (2 * i, 2 * i + 1)
                for c in cs:
                    a = c % 2
                    dve.wait_ge(glu_sig, c + 1)
                    v.scalar_tensor_tensor(out=upad[:, c, PADL:], in0=PS[:, (2 * i) % 4, a * T:(a + 1) * T],
                                           scalar=vcol("pw1_b", c), in1=sig[:, c % 4, :], op0=ALU.add,
                                           op1=ALU.mult).then_inc(glu_ready, 1)
                dve.wait_ge(glu_ready, cs[1] + 1)
                for c in cs:
                    j = PE_TAPS
                    tick(v.tensor_scalar(cacc[:, c, :], upad[:, c, j:j + T], vcol("dw_w", c * TAPS + j),
                                         vcol("dw_b", c), ALU.mult, ALU.add))
                for j in range(PE_TAPS + 1, TAPS):
                    for c in cs:
                        dve.wait_ge(dve_seq, seq[0] - 1)
                        tick(v.scalar_tensor_tensor(out=cacc[:, c, :], in0=upad[:, c, j:j + T],
                                                    scalar=vcol("dw_w", c * TAPS + j), in1=cacc[:, c, :],
                                                    op0=ALU.mult, op1=ALU.add))
                dve.wait_ge(dve_seq, seq[0])

            def conv_finish(i):
                dve.wait_ge(conv_pe, 2 * i + 2)
                ks = slice(2 * i, 2 * i + 2)
                v.tensor_tensor(cacc[:, ks, :], cacc[:, ks, :],
                                PS[:, CONV_BANKS[i], :].rearrange("p (a t) -> p a t", t=T),
                                ALU.add).then_inc(conv_ready, 1)

            def mixer1():
                lo(1, 0)
                lo(1, 1)
                ada_sum(1, 17)
                ada_store(2)
                mods_for(2)
                for k in range(KD):
                    dve.wait_ge(moe_done, k // 2 + 1)
                    residual(k // 2, k, mods[:, 0, 40 + k:41 + k]).then_inc(resid, 1)
                step(v.memset(upad[:, :, 0:PADL], 0.0))
                norm(2)
                split_x(hT, xh_ready, 4, xl_ready)
                lo(1, 2)
                lo(1, 3)
                for i in range(4):
                    if i in (1, 2):
                        lo(1, 2 * i + 2)
                        lo(1, 2 * i + 3)
                    if i == 3:
                        ada_sum(1, 21)
                    conv_pair(i)
                    if i:
                        conv_finish(i - 1)
                ada_sum(1, 23)
                conv_finish(3)
                for n in range(8, 11):
                    lo(1, n)
                dve.wait_ge(ln_mean, 1)
                for i in range(4):
                    ks = slice(2 * i, 2 * i + 2)
                    v.tensor_tensor(cacc[:, ks, :], cacc[:, ks, :], bc(rstd[:, T:2 * T].unsqueeze(1), [P, 2, T]),
                                    ALU.subtract).then_inc(ln_centred, 1)
                dve.wait_ge(ln_root, 1)
                step(v.reciprocal(rstd[:, 0:T], root[:, 0:T]))
                for i in range(4):
                    ks = slice(2 * i, 2 * i + 2)
                    v.tensor_tensor(cacc[:, ks, :], cacc[:, ks, :], bc(rstd[:, 0:T].unsqueeze(1), [P, 2, T]),
                                    ALU.mult).then_inc(ln_scaled, 1)
                split_x(cacc, xh_ready, 8, xl_ready)
                lo(1, 11)
                ada_store(3)
                mods_for(3)
                step(v.tensor_tensor(gate_bias, mods[:, 1, 16:24], vcol("pw2_b", 0, KD), ALU.mult))
                for k in range(KD):
                    tick(v.tensor_scalar(XT[:, k, :], XT[:, k, :], gate_bias[:, k:k + 1], None, ALU.add))
                dve.wait_ge(dve_seq, seq[0])
                for k in range(KD):
                    dve.wait_ge(proj_done[1], k // 2 + 1)
                    residual(k // 2, k, mods[:, 1, 16 + k:17 + k]).then_inc(resid, 1)

            def lo_m(l, j, i, end=False):
                ph = 2 * l + 1
                raw, h, l_ = moe_piece(j, i, end)
                dve.wait_ge(hi_ready[ph], upto(j, i))
                v.tensor_tensor(l_, raw, h.bitcast(F32), ALU.subtract).then_inc(lo_ready[ph], 1)

            def route(l):
                def buf(at, *shape):
                    n = 1
                    for s_ in shape:
                        n *= s_
                    b = small[:, at:at + n]
                    return b if len(shape) == 1 else b.rearrange("p (a b) -> p a b", b=shape[1])
                G8 = NT * GRP
                score, biased = buf(0, NT, E), buf(32, NT, E)
                b4 = buf(32, G8, PER)
                dve.wait_ge(scores_ready, l + 1)
                step(v.tensor_tensor(biased, score, bc(rb[:].unsqueeze(1), [P, NT, E]), ALU.add))
                hi2, lo2 = buf(64, G8, 2), buf(80, G8, 2)
                v.tensor_tensor(hi2, b4[:, :, 0::2], b4[:, :, 1::2], ALU.max)
                step(v.tensor_tensor(lo2, b4[:, :, 0::2], b4[:, :, 1::2], ALU.min))
                top1, t2a, t2b, gs = buf(96, G8), buf(104, G8), buf(112, G8), buf(120, G8)
                v.tensor_tensor(top1, hi2[:, :, 0], hi2[:, :, 1], ALU.max)
                v.tensor_tensor(t2a, hi2[:, :, 0], hi2[:, :, 1], ALU.min)
                step(v.tensor_tensor(t2b, lo2[:, :, 0], lo2[:, :, 1], ALU.max))
                step(v.tensor_tensor(t2a, t2a, t2b, ALU.max))
                step(v.tensor_tensor(gs, top1, t2a, ALU.add))
                gs2, gmax, eq, eqi = buf(120, NT, GRP), buf(128, NT), buf(136, NT, GRP), buf(144, NT, GRP)
                step(v.tensor_reduce(gmax, gs2, AX, ALU.max))
                step(v.tensor_tensor(eq, gs2, bc(gmax.unsqueeze(2), [P, NT, GRP]), ALU.is_equal))
                step(v.tensor_tensor(eqi, eq, con_("first4", 2 * GRP).rearrange("p (a b) -> p a b", b=GRP), ALU.mult))
                step(v.tensor_reduce(gmax, eqi, AX, ALU.max))
                step(v.tensor_tensor(eq, eqi, bc(gmax.unsqueeze(2), [P, NT, GRP]), ALU.is_equal))
                gt = small[:, 768:768 + G8 * 16].rearrange("p (g i j) -> p g i j", i=PER, j=PER)
                et = small[:, 896:896 + G8 * 16].rearrange("p (g i j) -> p g i j", i=PER, j=PER)
                vj = bc(b4.unsqueeze(2), [P, G8, PER, PER])
                vi = bc(b4.unsqueeze(3), [P, G8, PER, PER])
                v.tensor_tensor(gt, vj, vi, ALU.is_gt)
                step(v.tensor_tensor(et, vj, vi, ALU.is_equal))
                step(v.tensor_tensor(et.rearrange("p g i j -> p g (i j)"), et.rearrange("p g i j -> p g (i j)"),
                                     bc(con_("tri4", 16).unsqueeze(1), [P, G8, 16]), ALU.mult))
                step(v.tensor_tensor(gt, gt, et, ALU.add))
                rank = buf(160, G8, PER)
                step(v.tensor_reduce(rank, gt, AX, ALU.add))
                picks = buf(256, NT, E)
                p4 = buf(256, G8, PER)
                step(v.tensor_scalar(rank, rank, 1.5, None, ALU.is_lt))
                v.tensor_tensor(p4, rank, bc(buf(136, G8).unsqueeze(2), [P, G8, PER]),
                                ALU.mult).then_inc(picks_ready, 1)
                for i in range(4):
                    t, half = divmod(i, 2)
                    dve.wait_ge(htokh_ready, 4 * l + i + 1)
                    c = slice(half * 512, (half + 1) * 512)
                    v.tensor_tensor(htokl[:, t, c], PS[:, HTOK_BANKS[i], :], htokh[:, t, c].bitcast(F32),
                                    ALU.subtract).then_inc(htokl_ready, 1)
                dve.wait_ge(picks_ready, l + 1)
                w, ws = buf(288, NT, E), buf(320, NT)
                step(v.tensor_tensor(w, score, picks, ALU.mult))
                step(v.tensor_reduce(ws, w, AX, ALU.add))
                step(v.reciprocal(ws, ws))
                step(v.tensor_tensor(w, w, bc(ws.unsqueeze(2), [P, NT, E]), ALU.mult))
                dve.wait_ge(counts_done, l + 1)
                c16, n16 = small[0:E, 512:512 + P], small[0:E, 640:641]
                cum = buf(336, NT, E)
                v.tensor_copy(cum, PS[:, 1, 0:2 * E].rearrange("p (t e) -> p t e", e=E))
                step(v.tensor_copy(c16, PS[0:E, 1, 64:64 + P]))
                v.tensor_scalar(n16, c16[:, 0:1], P + 0.5, 1.0, ALU.is_gt, ALU.add).then_inc(count_rows, 1)
                dve.wait_ge(offs_done, l + 1)
                pm = buf(368, NT, E)
                step(v.tensor_tensor(pm, cum, bc(PS[:, 2, 0:E].unsqueeze(1), [P, NT, E]), ALU.add))
                step(v.scalar_tensor_tensor(out=pm, in0=pm, scalar=1.0, in1=picks, op0=ALU.add, op1=ALU.mult))
                sa, sb_, wa, wb = buf(400, NT), buf(404, NT), buf(408, NT), buf(412, NT)
                v.tensor_reduce(sa, pm, AX, ALU.max)
                step(v.tensor_reduce(sb_, pm, AX, ALU.add))
                step(v.tensor_tensor(sb_, sb_, sa, ALU.subtract))
                iota = con_("iota", SLOTS)
                pf = perm.bitcast(F32)
                for t in range(NT):
                    step(v.tensor_scalar(perm[:, t, :], iota, sa[:, t:t + 1], None, ALU.is_equal))
                    v.scalar_tensor_tensor(out=perm[:, t, :], in0=iota, scalar=sb_[:, t:t + 1], in1=pf[:, t, :],
                                           op0=ALU.is_equal, op1=ALU.add).then_inc(perm_ready, 1)
                off, beg = small[0:E, 660:661], small[0:E, 661:662]
                extra, more, last = small[0:E, 662:663], small[0:E, 663:664], small[0:E, 664:665]
                e = con_("expert", 1, 0, E)
                step(v.tensor_copy(small[0:E, 660:662], PS[0:E, 2, 64:66]))
                v.tensor_scalar(extra, beg, e, E + 1.0, ALU.subtract, ALU.add)
                v.tensor_scalar(last, c16[:, 0:1], off, float(P), ALU.add, ALU.subtract)
                step(v.tensor_scalar(more, n16, 1.0, None, ALU.subtract))
                js = con_("iota", MAXB + 1, 0, E)
                b0 = small[0:E, 672:672 + MAXB + 1]
                own, ext = small[0:E, 704:704 + MAXB + 1], small[0:E, 736:736 + MAXB + 1]
                tb = small[0:E, 1024:1024 + NTAB]
                te, ts = tb[:, 0:MAXB + 1], tb[:, MAXB + 1:2 * MAXB + 2]
                step(v.tensor_scalar(b0, js, -1.0, None, ALU.add))
                step(v.tensor_scalar(ext, b0, extra, more, ALU.is_equal, ALU.mult))
                step(v.tensor_scalar(b0, b0, -1.0, None, ALU.add))
                step(v.tensor_scalar(own, b0, e, None, ALU.is_equal))
                v.tensor_tensor(te, own, ext, ALU.add)
                step(v.tensor_scalar(ts, ext, last, None, ALU.mult))
                step(v.tensor_scalar(te, te, e, None, ALU.mult))
                step(v.scalar_tensor_tensor(out=ts, in0=own, scalar=off, in1=ts, op0=ALU.mult, op1=ALU.add))
                v.tensor_scalar(tb[:, 0:1], n16, 3.0 / E, None, ALU.subtract).then_inc(slots_ready, 1)
                dve.wait_ge(rows_done, l + 1)
                v.tensor_copy(tab[0:1, l, :], PS[0:1, 3, 0:NTAB]).then_inc(table_ready, 1)
                m = buf(416, NT, E)
                for s_, w_ in ((sa, wa), (sb_, wb)):
                    step(v.tensor_tensor(m, pm, bc(s_.unsqueeze(2), [P, NT, E]), ALU.is_equal))
                    step(v.tensor_tensor(m, m, w, ALU.mult))
                    step(v.tensor_reduce(w_, m, AX, ALU.add))

                def weighted(t):
                    wp = wperm[:, t, :]
                    step(v.tensor_scalar(wp, iota, sa[:, t:t + 1], wa[:, t:t + 1], ALU.is_equal, ALU.mult))
                    tmp = rstd if t == 0 else root
                    step(v.tensor_scalar(tmp[:], iota, sb_[:, t:t + 1], wb[:, t:t + 1], ALU.is_equal, ALU.mult))
                    v.tensor_tensor(wp, wp, tmp[:], ALU.add).then_inc(wperm_ready, 1)

                return weighted

            def moe(l):
                ph = 2 * l + 1
                norm(ph)
                for i in range(4):
                    lo_m(l, (None, 1), i)
                weighted = route(l)
                for half in range(2):
                    ks = slice(4 * half, 4 * half + 4)
                    dve.wait_ge(half_high, 2 * l + half + 1)
                    v.tensor_tensor(hcl[:, ks, :], hgT[:, ks, 0:P], hch[:, ks, :].bitcast(F32),
                                    ALU.subtract).then_inc(half_low, 1)
                    if half == 0:
                        weighted(0)
                inner = inner_blocks(dve, l)

                def slot_in(j):
                    dve.wait_ge(hch_ready[l], nth(j, 1, -1))
                    s0 = block_slot(dve, l, j)
                    v.tensor_tensor(hcl, hgT[:, :, bass.ds(s0, P)], hch.bitcast(F32),
                                    ALU.subtract).then_inc(hcl_ready[l], 1)

                def y_out(j):
                    dve.wait_ge(ytt_done[l], nth(j, 2))
                    s0 = block_slot(dve, l, j)
                    v.tensor_copy(yT[:, 4:8, bass.ds(s0, P)],
                                  PS[:, 6, :].rearrange("p (m c) -> p m c", c=P)).then_inc(ytd_stored[l], 1)

                def act_low(j):
                    dve.wait_ge(ath_ready[l], nth(j, 2))
                    for half in range(2):
                        hs = slice(2 * half, 2 * half + 2)
                        v.tensor_tensor(aTl[:, hs, :],
                                        PS[:, 2, 256 * half:256 * half + 256].rearrange("p (m c) -> p m c", c=P),
                                        aTh[:, hs, :].bitcast(F32), ALU.subtract).then_inc(atl_ready[l], 1)

                def multiply(j):
                    dve.wait_ge(silu_done[l], nth(j))
                    dve.wait_ge(piece_used[ph], upto(j, 7))
                    v.tensor_tensor(act, PS[:, 1, :], sg, ALU.mult).then_inc(act_ready[l], 1)

                def moe_step(j, second=False, last=False):
                    lo_m(l, j, 4)
                    lo_m(l, j, 5)
                    act_low(after(j, -1))
                    for i in (6, 7, 8, 9):
                        lo_m(l, j, i)
                    if not second:
                        y_out(after(j, -2))
                    lo_m(l, j, 10)
                    lo_m(l, j, 11)
                    dve.wait_ge(att_done[l], nth(j, 1, -1))
                    multiply(j)
                    if not last:
                        slot_in(after(j))
                    for i in range(4):
                        lo_m(l, after(j), i, last)

                one = (None, 1)
                lo_m(l, one, 4)
                lo_m(l, one, 5)
                weighted(1)
                v.memset(hgT[:, :, SLOTS:], 0.0)
                lo_m(l, one, 6)
                lo_m(l, one, 7)
                lo_m(l, after(one), 0)
                lo_m(l, after(one), 1)
                slot_in(after(one))
                multiply(one)
                lo_m(l, after(one), 2)
                lo_m(l, after(one), 3)
                for i in range(2):
                    dve.wait_ge(wpt_done, 2 * l + i + 1)
                    v.tensor_copy(wpT[:, 2 * i:2 * i + 2, :], PS[:, 5 + i, :].rearrange("p (s t) -> p s t", t=T)
                                  ).then_inc(wpt_stored, 1)
                moe_step((None, 2), second=True)
                with dve.Fori(0, inner) as r:
                    moe_step((r, 3))
                final = (inner, 3)
                moe_step(final, last=True)
                act_low(final)
                y_out(after(final, -1))
                y_out(final)
                for k in range(KD if l else 0):
                    dve.wait_ge(moe_done, 4 * l + k // 2 + 1)
                    residual(k // 2, k, mods[:, l, 40 + k:41 + k]).then_inc(resid, 1)

            mixer0()
            moe(0)
            mixer1()
            moe(1)


def kernel(**inputs):
    import numpy as np
    import concourse.bacc as bacc
    from concourse.bass_utils import run_bass_kernel_spmd

    f = {k: np.asarray(a) for k, a in inputs.items()}

    def cols(a):
        return a.reshape(-1, P).T

    def rope2(a):
        return np.concatenate([a, a]).reshape(P, 1)

    half = ROPE // 2
    inv_freq = (1.0 / (10000.0 ** (np.arange(half, dtype=np.float32) * np.float32(2.0 / ROPE)))).astype(np.float32)
    dw = f["conv_dw_w"][0]
    vec = np.concatenate([
        cols(f["norm1_g"]), cols(f["norm2_g"]), cols(f["ada_b"]), cols(f["mla_q_norm_g"]), cols(f["mla_kv_norm_g"]),
        f["mla_qk_q_g"][0, :NOPE].reshape(P, 1), f["mla_qk_k_g"][0, :NOPE].reshape(P, 1),
        rope2(f["mla_qk_q_g"][0, NOPE:]), rope2(f["mla_qk_k_g"][0, NOPE:]),
        np.tile(inv_freq, 4).reshape(P, 1),
        cols(f["conv_pw1_b"]), cols(f["conv_dw_b"]), cols(f["conv_ln_g"]), cols(f["conv_ln_b"]),
        cols(f["conv_pw2_b"]), cols(f["c"]),
        dw.T.reshape(KD, P, TAPS).transpose(1, 0, 2).reshape(P, KD * TAPS),
        f["router_w"].reshape(KD, P, E).transpose(1, 0, 2).reshape(P, KD * E),
    ], axis=1)
    i = np.arange(P)
    causal = np.where(i[None, :] <= i[:, None], 0.0, -1e30)
    rot1 = np.zeros((ROPE, ROPE))
    for a in range(half):
        rot1[a + half, a] = -1.0
        rot1[a, a + half] = 1.0
    rot = np.zeros((P, P))
    rot[:ROPE, :ROPE] = rot1
    rot[ROPE:, ROPE:] = rot1
    e = np.arange(P)[:, None]
    tri16 = np.concatenate([e < np.arange(E)[None, :], e <= np.arange(E)[None, :]], axis=1)
    tri4 = (np.arange(PER)[None, :] < np.arange(PER)[:, None]).astype(np.float32).reshape(1, -1)
    head = np.arange(HEADS)
    hsel = np.tile(np.eye(HEADS).reshape(1, -1), (P, 1))
    kpesel = np.tile((i < ROPE)[:, None], (1, HEADS))
    psel = np.concatenate([head[None, :] == 2 * g + (i[:, None] >= ROPE) for g in range(PAIRS)], axis=1)
    con = np.concatenate([
        np.eye(P), np.ones((P, P)), i[:, None] < i[None, :],
        np.concatenate([causal, np.zeros((P, P)), causal], axis=1), rot,
        np.tile(np.arange(1, SLOTS + 1)[None, :], (P, 1)), hsel, kpesel, psel, tri16,
        np.tile(np.array([4, 3, 2, 1, 4, 3, 2, 1])[None, :], (P, 1)), np.tile(tri4, (P, 1)),
        i[:, None],
    ], axis=1).astype(np.float32)
    uq = f["mla_w_uq"][0].reshape(QR, HEADS, QK)
    arrays = {
        "xT": f["x"][0].T.reshape(KD, P, T).transpose(1, 0, 2),
        "vec": vec,
        "con": con,
        "rbias": np.tile(f["router_bias"][None, :], (P, 1)),
        "pos": np.tile(f["positions"], (P, 1)),
        "ada_w": f["ada_w"],
        "w_dqkv": f["mla_w_dqkv"][0],
        "w_uq": np.concatenate([uq[:, :, :NOPE].reshape(QR, -1), uq[:, :, NOPE:].reshape(QR, -1)], axis=1),
        "w_ukv": f["mla_w_ukv"][0],
        "w_o": f["mla_w_o"][0],
        "pw1": f["conv_pw1_w"][0],
        "pw2": f["conv_pw2_w"][0],
        "w_gate": f["moe_w_gate"],
        "w_up": f["moe_w_up"],
        "w_down": f["moe_w_down"],
    }
    nc = bacc.Bacc("TRN2", target_bir_lowering=False, num_devices=1)
    args = []
    for name in arrays:
        arrays[name] = np.ascontiguousarray(arrays[name])
        args.append(nc.dram_tensor(name, arrays[name].shape, mybir.dt.from_np(arrays[name].dtype),
                                   kind="ExternalInput").ap())
    out = nc.dram_tensor("out", (P, KD, T), F32, kind="ExternalOutput").ap()
    build(nc, *args, out)
    r = run_bass_kernel_spmd(nc, [arrays], core_ids=[0])
    o = r.results[0]["out"]
    return np.ascontiguousarray(o.transpose(1, 0, 2).reshape(D, T).T).reshape(1, T, D)
```
